# Optimizing a Trainium2 kernel written in Bass

```python
import math
import jax
import jax.numpy as jnp
from jax import lax
import numpy as np
import jax, jax.numpy as jnp

D_MODEL = 2048
BATCH = 1
SEQ = 256
DEPTH = 1

GDN_HEADS = 8
GDN_HEAD_DIM = 128
GDN_WIDTH = GDN_HEADS * GDN_HEAD_DIM
GDN_CONV = 4
GDN_CHUNK = 64

MOBA_HEADS = 8
MOBA_HEAD_DIM = 128
MOBA_WIDTH = MOBA_HEADS * MOBA_HEAD_DIM
MOBA_BLOCK = 256
MOBA_TOPK = 3
MOBA_QBLOCK = 64
ROPE_THETA = 500000.0
ROPE_DIM = MOBA_HEAD_DIM // 4

D_FF = 5632
FFN_CONV = 3

NORM_EPS = 1e-6
NEG_INF = -1e30

IN_SPLITS = (3 * GDN_WIDTH, GDN_HEADS, GDN_HEADS, GDN_WIDTH, 3 * MOBA_WIDTH, D_MODEL, D_MODEL)
IN_DIM = sum(IN_SPLITS)


def rms_norm(x, w):
    xf = x.astype(jnp.float32)
    y = xf * lax.rsqrt(jnp.mean(xf * xf, axis=-1, keepdims=True) + NORM_EPS)
    return (y * w.astype(jnp.float32)).astype(x.dtype)

def l2norm(x):
    return x * lax.rsqrt(jnp.sum(x * x, axis=-1, keepdims=True) + 1e-6)

def causal_dwconv(x, w, bias=None):
    width, ch = w.shape
    y = lax.conv_general_dilated(
        x, w[:, None, :].astype(x.dtype), window_strides=(1,), padding=[(width - 1, 0)],
        dimension_numbers=('NWC', 'WIO', 'NWC'), feature_group_count=ch)
    if bias is not None:
        y = y + bias.astype(x.dtype)
    return y

def partial_rope(x, positions):
    half = ROPE_DIM // 2
    inv_freq = ROPE_THETA ** (-jnp.arange(half, dtype=jnp.float32) / half)
    ang = positions.astype(jnp.float32)[..., None] * inv_freq
    cos = jnp.cos(ang)[:, :, None, :]
    sin = jnp.sin(ang)[:, :, None, :]
    xr = x[..., :ROPE_DIM].astype(jnp.float32)
    x1, x2 = xr[..., :half], xr[..., half:]
    rot = jnp.concatenate([x1 * cos - x2 * sin, x2 * cos + x1 * sin], axis=-1).astype(x.dtype)
    return jnp.concatenate([rot, x[..., ROPE_DIM:]], axis=-1)

def chunk_gated_delta_rule(q, k, v, g, beta):
    B, S, H, Dk = q.shape
    Dv = v.shape[-1]
    C = GDN_CHUNK
    N = S // C

    def chunks(t):
        return jnp.moveaxis(t.reshape((B, N, C, H) + t.shape[3:]), 3, 1)

    q = chunks(q) * (Dk ** -0.5)
    k = chunks(k)
    v = chunks(v)
    g = chunks(g)
    beta = chunks(beta)
    gc = jnp.cumsum(g, axis=-1)
    r = jnp.arange(C)
    causal = r[:, None] >= r[None, :]
    strict = r[:, None] > r[None, :]
    gamma = jnp.exp(jnp.where(causal, gc[..., :, None] - gc[..., None, :], -jnp.inf))
    kb = k * beta[..., None]
    a_mat = jnp.where(strict, jnp.einsum('bhncd,bhnsd->bhncs', kb, k) * gamma, 0.0)
    eye = jnp.eye(C, dtype=q.dtype)
    t_mat = lax.linalg.triangular_solve(eye + a_mat, jnp.broadcast_to(eye, a_mat.shape),
                                        left_side=True, lower=True, unit_diagonal=True)
    u = jnp.einsum('bhncs,bhnsv->bhncv', t_mat, v * beta[..., None])
    w = jnp.einsum('bhncs,bhnsk->bhnck', t_mat, kb * jnp.exp(gc)[..., None])
    qk = jnp.einsum('bhncd,bhnsd->bhncs', q, k) * gamma
    qg = q * jnp.exp(gc)[..., None]
    kd = k * jnp.exp(gc[..., -1:] - gc)[..., None]
    glast = jnp.exp(gc[..., -1])

    def step(state, xs):
        u_n, w_n, qg_n, qk_n, kd_n, gl_n = xs
        v_new = u_n - jnp.einsum('bhck,bhkv->bhcv', w_n, state)
        o = jnp.einsum('bhck,bhkv->bhcv', qg_n, state) + jnp.einsum('bhcs,bhsv->bhcv', qk_n, v_new)
        state = state * gl_n[..., None, None] + jnp.einsum('bhck,bhcv->bhkv', kd_n, v_new)
        return state, o

    xs = tuple(jnp.moveaxis(t, 2, 0) for t in (u, w, qg, qk, kd, glast))
    s0 = jnp.zeros((B, H, Dk, Dv), q.dtype)
    _, o = lax.scan(step, s0, xs)
    return o.transpose(1, 0, 3, 2, 4).reshape(B, S, H, Dv)

def gated_deltanet(qkv, beta_logit, a_logit, z, conv_w, a_log, dt_bias, norm_w):
    B, S, _ = qkv.shape
    dtype = qkv.dtype
    f32 = jnp.float32
    qkv = jax.nn.silu(causal_dwconv(qkv, conv_w))
    q, k, v = jnp.split(qkv.astype(f32), 3, axis=-1)
    shp = (B, S, GDN_HEADS, GDN_HEAD_DIM)
    q = l2norm(q.reshape(shp))
    k = l2norm(k.reshape(shp))
    v = v.reshape(shp)
    beta = jax.nn.sigmoid(beta_logit.astype(f32))
    g = -jnp.exp(a_log.astype(f32)) * jax.nn.softplus(a_logit.astype(f32) + dt_bias.astype(f32))
    o = chunk_gated_delta_rule(q, k, v, g, beta)
    o = rms_norm(o, norm_w) * jax.nn.silu(z.astype(f32).reshape(shp))
    return o.reshape(B, S, GDN_WIDTH).astype(dtype)

def moba_attention(q, k, v):
    B, S, H, D = q.shape
    BLK = MOBA_BLOCK
    NB = -(-S // BLK)
    Sp = NB * BLK
    K = min(MOBA_TOPK, NB)
    QB = MOBA_QBLOCK
    NQ = Sp // QB
    pad = ((0, 0), (0, Sp - S), (0, 0), (0, 0))
    qh = jnp.pad(q, pad).transpose(0, 2, 1, 3) * (D ** -0.5)
    kb = jnp.pad(k, pad).transpose(0, 2, 1, 3).reshape(B, H, NB, BLK, D)
    vb = jnp.pad(v, pad).transpose(0, 2, 1, 3).reshape(B, H, NB, BLK, D)
    k_mean = jnp.mean(kb.astype(jnp.float32), axis=3)
    gate = jnp.einsum('bhsd,bhnd->bhsn', qh.astype(jnp.float32), k_mean)
    q_blk = jnp.arange(Sp) // BLK
    fully_past = jnp.arange(NB)[None, :] < q_blk[:, None]
    gate = jnp.where(fully_past, gate, -jnp.inf)
    _, sel = lax.top_k(gate, K)
    qs = qh.reshape(B, H, NQ, QB, D).transpose(0, 2, 1, 3, 4).reshape(B * NQ, H, QB, D)
    ss = sel.reshape(B, H, NQ, QB, K).transpose(0, 2, 1, 3, 4).reshape(B * NQ, H, QB, K)
    b_idx = jnp.repeat(jnp.arange(B, dtype=jnp.int32), NQ)
    n_idx = jnp.tile(jnp.arange(NQ, dtype=jnp.int32), B)
    head = jnp.arange(H)[:, None, None]

    def query_block(args):
        qn, sn, b, n = args
        kb_b = kb[b]
        vb_b = vb[b]
        k_sel = kb_b[head, sn]
        v_sel = vb_b[head, sn]
        t = n * QB + jnp.arange(QB)
        own = (n * QB) // BLK
        k_own = lax.dynamic_index_in_dim(kb_b, own, axis=1, keepdims=False)
        v_own = lax.dynamic_index_in_dim(vb_b, own, axis=1, keepdims=False)
        s_past = jnp.einsum('hqd,hqkld->hqkl', qn, k_sel, preferred_element_type=jnp.float32)
        slot_ok = jnp.arange(K)[None, :] < (t // BLK)[:, None]
        s_past = jnp.where(slot_ok[None, :, :, None], s_past, NEG_INF).reshape(H, QB, K * BLK)
        s_own = jnp.einsum('hqd,hld->hql', qn, k_own, preferred_element_type=jnp.float32)
        own_ok = (own * BLK + jnp.arange(BLK))[None, :] <= t[:, None]
        s_own = jnp.where(own_ok[None], s_own, NEG_INF)
        p = jax.nn.softmax(jnp.concatenate([s_past, s_own], axis=-1), axis=-1).astype(v.dtype)
        p_past = p[..., :K * BLK].reshape(H, QB, K, BLK)
        p_own = p[..., K * BLK:]
        return (jnp.einsum('hqkl,hqkld->hqd', p_past, v_sel)
                + jnp.einsum('hql,hld->hqd', p_own, v_own))

    out = lax.map(query_block, (qs, ss, b_idx, n_idx))
    out = out.reshape(B, NQ, H, QB, D).transpose(0, 1, 3, 2, 4).reshape(B, Sp, H, D)
    return out[:, :S]

def split_columns(proj):
    offs = [int(o) for o in np.cumsum(IN_SPLITS)[:-1]]
    return jnp.split(proj, offs, axis=-1)

def first_inputs(seed: int = 0) -> dict:
    key = jax.random.key(seed)
    ks = jax.random.split(key, 20)
    f32 = jnp.float32
    L = DEPTH

    def nrm(k, shape, scale):
        return jax.random.normal(k, shape, f32) * scale

    x = nrm(ks[0], (BATCH, SEQ, D_MODEL), 1.0)
    positions = jnp.broadcast_to(jnp.arange(SEQ, dtype=jnp.int32), (BATCH, SEQ))
    ln1 = 1.0 + nrm(ks[1], (L, D_MODEL), 0.02)
    w_in = nrm(ks[2], (L, D_MODEL, IN_DIM), D_MODEL ** -0.5)
    gdn_conv = nrm(ks[3], (L, GDN_CONV, 3 * GDN_WIDTH), GDN_CONV ** -0.5)
    gdn_a_log = jnp.log(jax.random.uniform(ks[4], (L, GDN_HEADS), f32, 1.0, 16.0))
    dt = jnp.exp(jax.random.uniform(ks[5], (L, GDN_HEADS), f32, math.log(1e-3), math.log(1e-1)))
    gdn_dt_bias = dt + jnp.log(-jnp.expm1(-dt))
    gdn_norm = 1.0 + nrm(ks[6], (L, GDN_HEAD_DIM), 0.02)
    w_branch_a = nrm(ks[7], (L, GDN_WIDTH, D_MODEL), GDN_WIDTH ** -0.5)
    w_branch_b = nrm(ks[8], (L, MOBA_WIDTH, D_MODEL), MOBA_WIDTH ** -0.5)
    w_out = nrm(ks[9], (L, D_MODEL, D_MODEL), D_MODEL ** -0.5)
    ln2 = 1.0 + nrm(ks[10], (L, D_MODEL), 0.02)
    w_up = nrm(ks[11], (L, D_MODEL, 2 * D_FF), D_MODEL ** -0.5)
    ffn_conv = nrm(ks[12], (L, FFN_CONV, 2 * D_FF), FFN_CONV ** -0.5)
    ffn_conv_bias = nrm(ks[13], (L, 2 * D_FF), 0.01)
    w_down = nrm(ks[14], (L, D_FF, D_MODEL), D_FF ** -0.5)
    final_norm = 1.0 + nrm(ks[15], (D_MODEL,), 0.02)
    return {"x": x, "positions": positions, "ln1": ln1, "w_in": w_in, "gdn_conv": gdn_conv,
            "gdn_a_log": gdn_a_log, "gdn_dt_bias": gdn_dt_bias, "gdn_norm": gdn_norm,
            "w_branch_a": w_branch_a, "w_branch_b": w_branch_b, "w_out": w_out, "ln2": ln2,
            "w_up": w_up, "ffn_conv": ffn_conv, "ffn_conv_bias": ffn_conv_bias,
            "w_down": w_down, "final_norm": final_norm}

def first_block(x, positions, ln1, w_in, gdn_conv, gdn_a_log, gdn_dt_bias, gdn_norm,
              w_branch_a, w_branch_b, w_out, ln2, w_up, ffn_conv, ffn_conv_bias, w_down,
              final_norm):
    B, S, _ = x.shape
    for l in range(DEPTH):
        h = rms_norm(x, ln1[l])
        proj = h @ w_in[l]
        qkv_a, beta_a, decay_a, z_a, qkv_b, gate_a, gate_b = split_columns(proj)
        y_a = gated_deltanet(qkv_a, beta_a, decay_a, z_a, gdn_conv[l], gdn_a_log[l],
                             gdn_dt_bias[l], gdn_norm[l]) @ w_branch_a[l]
        q_b, k_b, v_b = jnp.split(qkv_b, 3, axis=-1)
        shp = (B, S, MOBA_HEADS, MOBA_HEAD_DIM)
        q_b = partial_rope(q_b.reshape(shp), positions)
        k_b = partial_rope(k_b.reshape(shp), positions)
        y_b = moba_attention(q_b, k_b, v_b.reshape(shp)).reshape(B, S, MOBA_WIDTH) @ w_branch_b[l]
        merged = jax.nn.sigmoid(gate_a) * y_a + jax.nn.sigmoid(gate_b) * y_b
        x = x + merged @ w_out[l]
        h = rms_norm(x, ln2[l])
        u = causal_dwconv(h @ w_up[l], ffn_conv[l], ffn_conv_bias[l])
        u_gate, u_val = jnp.split(u, 2, axis=-1)
        x = x + (jax.nn.silu(u_gate) * u_val) @ w_down[l]
    return rms_norm(x, final_norm)


DEPTH_2 = 2

D_MIX = D_MODEL
HEAD_DIM = 128
N_HEADS_A = 8
N_HEADS_B = 8
D_A = N_HEADS_A * HEAD_DIM
D_B = N_HEADS_B * HEAD_DIM
IDX_HEADS = 16
IDX_DIM = 64
TOPK_MAX = 256
Q_BLOCK = 128
RET_CHUNK = 128
N_BUCKETS = 32
MAX_EXACT = 16
MAX_DISTANCE = 128
ROPE_BASE = 10000.0
EPS = 1e-6
IN_SIZES = (D_A, HEAD_DIM, HEAD_DIM, D_A, IDX_HEADS * IDX_DIM, IDX_DIM, IDX_HEADS, D_B, D_B, D_B, D_B)
N_IN = 2 * D_A + 2 * HEAD_DIM + IDX_HEADS * IDX_DIM + IDX_DIM + IDX_HEADS + 4 * D_B


def rmsnorm(x, g):
    xf = x.astype(jnp.float32)
    y = xf * lax.rsqrt(jnp.mean(xf * xf, axis=-1, keepdims=True) + EPS)
    return (y * g.astype(jnp.float32)).astype(x.dtype)

def head_groupnorm(x, g):
    xf = x.astype(jnp.float32)
    mu = jnp.mean(xf, axis=-1, keepdims=True)
    var = jnp.mean(jnp.square(xf - mu), axis=-1, keepdims=True)
    y = (xf - mu) * lax.rsqrt(var + EPS)
    B, S, H, D = x.shape
    return (y.reshape(B, S, H * D) * g.astype(jnp.float32)).astype(x.dtype)

def rotary(x, pos):
    half = x.shape[-1] // 2
    inv = ROPE_BASE ** (-jnp.arange(half, dtype=jnp.float32) / half)
    ang = pos.astype(jnp.float32)[..., None] * inv
    cos = jnp.cos(ang)[:, :, None, :]
    sin = jnp.sin(ang)[:, :, None, :]
    xf = x.astype(jnp.float32)
    x1, x2 = xf[..., :half], xf[..., half:]
    return jnp.concatenate([x1 * cos - x2 * sin, x1 * sin + x2 * cos], axis=-1).astype(x.dtype)

def t5_bucket(rel):
    rel = jnp.maximum(rel, 0)
    relf = jnp.maximum(rel, 1).astype(jnp.float32)
    large = MAX_EXACT + (jnp.log(relf / MAX_EXACT) / math.log(MAX_DISTANCE / MAX_EXACT)
                         * (N_BUCKETS - MAX_EXACT)).astype(jnp.int32)
    large = jnp.minimum(large, N_BUCKETS - 1)
    return jnp.where(rel < MAX_EXACT, rel, large)

def sparse_attention(q, k, v, q_idx, k_idx, w_idx, pos, rel_bias):
    B, S, H, Dh = q.shape
    n_blk = S // Q_BLOCK
    top_k = min(TOPK_MAX, S // 4)
    scale = HEAD_DIM ** -0.5
    key_pos = jnp.arange(S)

    def block(xs):
        qb, qib, wb, pb, start = xs
        t = start + jnp.arange(Q_BLOCK)
        dots = jnp.einsum('bqhd,bsd->bqhs', qib, k_idx).astype(jnp.float32)
        I = jnp.einsum('bqh,bqhs->bqs', wb.astype(jnp.float32), jax.nn.relu(dots))
        causal = key_pos[None, :] <= t[:, None]
        I = jnp.where(causal[None], I, -jnp.inf)
        _, sel = lax.top_k(I, top_k)
        valid = sel <= t[None, :, None]
        ks = jax.vmap(lambda kb, ib: kb[ib])(k, sel)
        vs = jax.vmap(lambda vb, ib: vb[ib])(v, sel)
        ps = jax.vmap(lambda pb_, ib: pb_[ib])(pos, sel)
        bias = rel_bias[t5_bucket(pb[:, :, None] - ps)]
        bias = jnp.moveaxis(bias, -1, 2).astype(jnp.float32)
        logits = jnp.einsum('bqhd,bqkd->bqhk', qb, ks).astype(jnp.float32) * scale + bias
        logits = jnp.where(valid[:, :, None, :], logits, -jnp.inf)
        p = jax.nn.softmax(logits, axis=-1).astype(v.dtype)
        return jnp.einsum('bqhk,bqkd->bqhd', p, vs)

    def to_blocks(a):
        return a.reshape((B, n_blk, Q_BLOCK) + a.shape[2:]).swapaxes(0, 1)

    xs = (to_blocks(q), to_blocks(q_idx), to_blocks(w_idx), to_blocks(pos),
          jnp.arange(n_blk) * Q_BLOCK)
    out = lax.map(block, xs)
    return out.swapaxes(0, 1).reshape(B, S, H, Dh)

def retention(q, k, v):
    B, S, H, D = q.shape
    C = RET_CHUNK
    nC = S // C
    log_g = jnp.log1p(-jnp.exp2(-5.0 - jnp.arange(H, dtype=jnp.float32)))
    i = jnp.arange(C, dtype=jnp.float32)
    diff = i[:, None] - i[None, :]
    dmask = jnp.where(diff >= 0, jnp.exp(log_g[:, None, None] * jnp.maximum(diff, 0.0)), 0.0)
    qc = q.astype(jnp.float32).reshape(B, nC, C, H, D)
    kc = k.astype(jnp.float32).reshape(B, nC, C, H, D)
    vc = v.astype(jnp.float32).reshape(B, nC, C, H, D)
    s_in = jnp.einsum('bnihd,bnjhd->bnhij', qc, kc) * dmask
    intra = jnp.einsum('bnhij,bnjhd->bnihd', s_in, vc)
    zeta = jnp.exp(log_g[None, :] * (C - 1.0 - i)[:, None])
    u = jnp.einsum('bnjhd,bnjhe->bnhde', kc * zeta[None, None, :, :, None], vc)
    g_chunk = jnp.exp(log_g * C)[None, :, None, None]

    def step(R, u_n):
        return g_chunk * R + u_n, R

    _, R_prev = lax.scan(step, jnp.zeros((B, H, D, D), jnp.float32), u.swapaxes(0, 1))
    R_prev = R_prev.swapaxes(0, 1)
    xi = jnp.exp(log_g[None, :] * (i + 1.0)[:, None])
    cross = jnp.einsum('bnihd,bnhde->bnihe', qc, R_prev) * xi[None, None, :, :, None]
    return (intra + cross).reshape(B, S, H, D)

def second_inputs(seed: int = 0) -> dict:
    key = jax.random.key(seed)
    ks = jax.random.split(key, 12)
    f32 = jnp.float32
    x = jax.random.normal(ks[0], (BATCH, SEQ, D_MODEL), f32)
    c = jax.random.normal(ks[1], (BATCH, D_MODEL), f32)
    positions = jnp.broadcast_to(jnp.arange(SEQ, dtype=jnp.int32)[None, :], (BATCH, SEQ))
    rel_bias = 0.5 * jax.random.normal(ks[2], (N_BUCKETS, N_HEADS_A), f32)
    norm_gain = 1.0 + 0.05 * jax.random.normal(ks[3], (DEPTH_2, D_MODEL), f32)
    w_mod = 0.5 * D_MODEL ** -0.5 * jax.random.normal(ks[4], (DEPTH_2, D_MODEL, 3 * D_MODEL), f32)
    b_mod = 0.02 * jax.random.normal(ks[5], (DEPTH_2, 3 * D_MODEL), f32)
    w_in = D_MODEL ** -0.5 * jax.random.normal(ks[6], (DEPTH_2, D_MODEL, N_IN), f32)
    q_norm_gain = 1.0 + 0.05 * jax.random.normal(ks[7], (DEPTH_2, HEAD_DIM), f32)
    k_norm_gain = 1.0 + 0.05 * jax.random.normal(ks[8], (DEPTH_2, HEAD_DIM), f32)
    ret_norm_gain = 1.0 + 0.05 * jax.random.normal(ks[9], (DEPTH_2, D_B), f32)
    w_out = D_MIX ** -0.5 * jax.random.normal(ks[10], (DEPTH_2, D_MIX, D_MODEL), f32)
    return {"x": x, "c": c, "positions": positions, "rel_bias": rel_bias,
            "norm_gain": norm_gain, "w_mod": w_mod, "b_mod": b_mod, "w_in": w_in,
            "q_norm_gain": q_norm_gain, "k_norm_gain": k_norm_gain,
            "ret_norm_gain": ret_norm_gain, "w_out": w_out}

def second_block(x, c, positions, rel_bias, norm_gain, w_mod, b_mod, w_in,
              q_norm_gain, k_norm_gain, ret_norm_gain, w_out):
    B, S, _ = x.shape
    split_points = [int(p) for p in np.cumsum(IN_SIZES)[:-1]]
    c_act = jax.nn.silu(c)
    for l in range(DEPTH_2):
        mod = c_act @ w_mod[l] + b_mod[l]
        shift, scale, gate = jnp.split(mod, 3, axis=-1)
        h = rmsnorm(x, norm_gain[l]) * (1.0 + scale[:, None, :]) + shift[:, None, :]
        proj = h @ w_in[l]
        q_a, k_a, v_a, g_a, q_i, k_i, w_i, q_b, k_b, v_b, g_b = jnp.split(proj, split_points, axis=-1)
        q_a = rmsnorm(q_a.reshape(B, S, N_HEADS_A, HEAD_DIM), q_norm_gain[l])
        k_a = rmsnorm(k_a, k_norm_gain[l])
        att = sparse_attention(q_a, k_a, v_a, q_i.reshape(B, S, IDX_HEADS, IDX_DIM), k_i, w_i,
                               positions, rel_bias)
        y_a = att.reshape(B, S, D_A) * jax.nn.silu(g_a)
        q_b = rotary(q_b.reshape(B, S, N_HEADS_B, HEAD_DIM), positions)
        k_b = rotary(k_b.reshape(B, S, N_HEADS_B, HEAD_DIM), positions) * (HEAD_DIM ** -0.5)
        ret = retention(q_b, k_b, v_b.reshape(B, S, N_HEADS_B, HEAD_DIM))
        y_b = head_groupnorm(ret, ret_norm_gain[l]).astype(x.dtype) * jax.nn.silu(g_b)
        y = jnp.concatenate([y_a, y_b], axis=-1) @ w_out[l]
        x = x + gate[:, None, :] * y
    return x


def setup_inputs(seed=0):
    out = dict(first_inputs(seed))
    for name, value in second_inputs(seed + 1).items():
        if name != "x":
            out[name + "_2"] = value
    return out


def reference(
    x, positions, ln1, w_in, gdn_conv, gdn_a_log, gdn_dt_bias, gdn_norm, w_branch_a, w_branch_b,
    w_out, ln2, w_up, ffn_conv, ffn_conv_bias, w_down, final_norm, c_2, positions_2, rel_bias_2,
    norm_gain_2, w_mod_2, b_mod_2, w_in_2, q_norm_gain_2, k_norm_gain_2, ret_norm_gain_2,
    w_out_2,
):
    x = first_block(
        x, positions, ln1, w_in, gdn_conv, gdn_a_log, gdn_dt_bias, gdn_norm, w_branch_a,
        w_branch_b, w_out, ln2, w_up, ffn_conv, ffn_conv_bias, w_down, final_norm,
    )
    return second_block(
        x, c_2, positions_2, rel_bias_2, norm_gain_2, w_mod_2, b_mod_2, w_in_2, q_norm_gain_2,
        k_norm_gain_2, ret_norm_gain_2, w_out_2,
    )


_drawn_inputs = setup_inputs


def setup_inputs(seed=0):
    import zlib

    import numpy as np

    out = dict(_drawn_inputs(seed))
    spreads = {}
    factors = {'ln1': 4.019,
     'gdn_norm': 7.1,
     'ln2': 3.595,
     'ffn_conv_bias': 6.709,
     'b_mod_2': 2.699,
     'q_norm_gain_2': 8.0,
     'k_norm_gain_2': 8.0,
     'ret_norm_gain_2': 5.429,
     'rel_bias_2': 4.74}
    for name, (base, spread) in spreads.items():
        noise = np.random.default_rng([zlib.crc32(name.encode()), seed]).standard_normal(out[name].shape)
        drawn = base * np.exp(spread * noise) if base else spread * noise
        out[name] = jnp.asarray(drawn.astype(out[name].dtype))
    for name, factor in factors.items():
        out[name] = (out[name] * factor).astype(out[name].dtype)
    return out
```

```python
import math
from contextlib import ExitStack

import concourse.bass as bass
from concourse import mybir
import numpy as np

F32 = mybir.dt.float32
BF16 = mybir.dt.bfloat16
I32 = mybir.dt.int32
ALU = mybir.AluOpType
ACT = mybir.ActivationFunctionType
AX = mybir.AxisListType.X
ADD, SUB, MUL, MAX, MIN = ALU.add, ALU.subtract, ALU.mult, ALU.max, ALU.min

D = 2048
S = 256
KT = D // 128
GW = 1024
DFF = 5632
FT = DFF // 128
EPS = 1e-6
NEG = -1e30
R1 = 3
R2 = 4
LOOK = 3
NSTG = 6
CH = 2048

ROPE1 = 16
THETA1 = 500000.0
THETA2 = 10000.0
TWO_PI = [6.25, 0.03125, 0.0019350051879882812, 3.0199159819567e-07]

C_ID, C_TRI, C_ONE, C_ON128, C_CAUS, C_GMASK, C_LEV, C_PERM = 0, 128, 256, 384, 512, 768, 896, 1792
C_INV1, C_INV2, C_SG1, C_SG2, C_HPI, C_THR = 1824, 1825, 1826, 1827, 1828, 1829
NCONST = 1832


def constants():
    c = np.zeros((128, NCONST), np.float32)
    i = np.arange(128)
    c[:, C_ID:C_ID + 128] = np.eye(128)
    c[:, C_TRI:C_TRI + 128] = i[:, None] <= i[None, :]
    c[:, C_ONE:C_ONE + 128] = 1.0
    c[:, C_ON128:C_ON128 + 128] = 1.0 / 128
    c[:, C_CAUS + 128:C_CAUS + 256] = np.where(i[None, :] <= i[:, None], 0.0, NEG)
    c[:, C_GMASK:C_GMASK + 128] = np.where(i[None, :] >= i[:, None], 0.0, NEG)
    for l in range(7):
        b = 1 << l
        same = (i[:, None] // (2 * b)) == (i[None, :] // (2 * b))
        low = (i[:, None] % (2 * b)) < b
        up = (i[None, :] % (2 * b)) >= b
        c[:, C_LEV + 128 * l:C_LEV + 128 * l + 128] = same & low & up
    for m in range(32):
        c[(m + 16) % 32, C_PERM + m] = 1.0
    h1 = np.arange(16, dtype=np.float32)
    inv1 = (np.float32(THETA1) ** (-h1 / np.float32(16))).astype(np.float32)
    c[0:16, C_INV1] = inv1
    c[16:32, C_INV1] = inv1
    c[0:16, C_SG1] = -1.0
    c[16:32, C_SG1] = 1.0
    h2 = np.arange(64, dtype=np.float32)
    inv2 = (np.float32(THETA2) ** (-h2 / np.float32(64))).astype(np.float32)
    c[0:64, C_INV2] = inv2
    c[64:128, C_INV2] = inv2
    c[0:64, C_SG2] = 1.0
    c[64:128, C_SG2] = -1.0
    c[:, C_HPI] = math.pi / 2
    return c


def decay():
    h = np.arange(8, dtype=np.float32)
    lg = np.log1p(-np.exp2(-5.0 - h)).astype(np.float32)
    j = np.arange(128)
    out = np.zeros((128, 8, 384), np.float32)
    for hh in range(8):
        d0 = np.arange(256)[None, :] - j[:, None]
        out[:, hh, 0:256] = np.where(d0 >= 0, np.exp(lg[hh] * np.maximum(d0, 0)), 0.0)
        d1 = j[None, :] - j[:, None]
        out[:, hh, 256:384] = np.where(d1 >= 0, np.exp(lg[hh] * np.maximum(d1, 0)), 0.0)
    return (out * np.float32(128.0 ** -0.5)).astype(np.float32).reshape(128, 3072)


def thresholds():
    out = list(range(1, 17))
    for b in range(17, 32):
        out.append(int(math.ceil(16.0 * 8.0 ** ((b - 16) / 16.0) - 1e-9)))
    return out


class Queue:

    def __init__(self, sem):
        self.sem, self.n, self.todo, self.seen = sem, 0, [], {}

    def wait(self, toks):
        for t in toks:
            if t is None:
                continue
            sem, v = t
            if self.seen.get(id(sem), 0) < v:
                self.seen[id(sem)] = v
                self.todo.append((0, sem, v))

    def op(self, fn, after=(), sig=True):
        self.wait(after)
        if sig:
            self.n += 1
            self.todo.append((1, fn, self.sem))
            return (self.sem, self.n)
        self.todo.append((2, fn, None))
        return None

    def dma(self, out, in_, slot, after=()):
        self.wait(after)
        slot.n += 16
        sem = slot.sem
        self.todo.append((2, lambda e: e.dma_start(out, in_).then_inc(sem, 16), None))
        return (sem, slot.n)

    def emit(self, e):
        for kind, a, b in self.todo:
            if kind == 0:
                e.wait_ge(a, b)
            elif kind == 1:
                a(e).then_inc(b, 1)
            else:
                a(e)


class Slot:
    def __init__(self, sem):
        self.sem, self.n = sem, 0


def mm(o, l, r, start=True, stop=True):
    return lambda e: e.matmul(o, l, r, start=start, stop=stop, skip_group_check=True)


def mms(*fns):
    def run(e):
        for f in fns:
            last = f(e)
        return last
    return run


def tp(o, i, ident):
    return lambda e: e.transpose(o, i, ident)


def act(o, i, f, bias=None, scale=1.0, acc=None):
    if bias is None:
        if acc is None:
            return lambda e: e.activation(o, i, f, scale=scale)
        return lambda e: e.activation(o, i, f, scale=scale, accum_out=acc)
    if acc is None:
        return lambda e: e.activation(o, i, f, bias=bias, scale=scale)
    return lambda e: e.activation(o, i, f, bias=bias, scale=scale, accum_out=acc)


def cp(o, i):
    return lambda e: e.tensor_copy(o, i)


def tt(o, a, b, op):
    return lambda e: e.tensor_tensor(o, a, b, op)


def ts(o, a, s1, op0, s2=None, op1=None):
    if op1 is None:
        return lambda e: e.tensor_scalar(o, a, s1, None, op0)
    return lambda e: e.tensor_scalar(o, a, s1, s2, op0, op1)


def stt(o, a, s, b, op0, op1):
    return lambda e: e.scalar_tensor_tensor(o, a, s, b, op0, op1)


def red(o, a, op):
    return lambda e: e.tensor_reduce(o, a, AX, op)


def recip(o, a):
    return lambda e: e.reciprocal(o, a)


def mid(a, n):
    return a.unsqueeze(1).to_broadcast([a.shape[0], n, a.shape[1]])


def rep(a, n):
    return a.unsqueeze(2).to_broadcast([a.shape[0], a.shape[1], n])


def build(nc, t, out):
    ctx = ExitStack()
    with ctx:
        program(nc, t, out, ctx)


def program(nc, t, out, ctx):
    def sb(name, shape, dt=F32):
        return ctx.enter_context(nc.sbuf_tensor(name, shape, dt))

    def sem(name):
        return ctx.enter_context(nc.semaphore(name))

    bank = [ctx.enter_context(nc.psum_tensor(f"ps{i}", [128, 512], F32)) for i in range(8)]
    PE, AC, DV, GP, SP = (Queue(sem(f"done_{n}")) for n in ("pe", "act", "dve", "pool", "sp"))

    ring = sb("ring", [128, R1, CH])
    whi = sb("whi", [128, R2, CH], BF16)
    wlo = sb("wlo", [128, R2, CH], BF16)
    X = sb("X", [128, 2, D])
    hhi = sb("hhi", [128, KT, S], BF16)
    hlo = sb("hlo", [128, KT, S], BF16)
    cst = sb("cst", [128, NCONST])
    VT = sb("VT", [128, 6 * 128])
    cs = sb("cs", [128, 4, S])
    stg = sb("stg", [128, NSTG, 512])
    sm = sb("sm", [128, 512])
    modcm = sb("modcm", [128, 2, 32])
    AR = sb("AR", [128, 22528])
    arp = [0]

    def carve(at, *shape, dt=F32):
        n = 1
        for s_ in shape:
            n *= s_
        w = (n + 1) // 2 if dt == BF16 else n
        v = AR[:, at:at + w]
        if dt != F32:
            v = v.bitcast(dt)
        if len(shape) == 1:
            return v
        names = "abcd"[:len(shape)]
        kw = {names[i]: shape[i] for i in range(1, len(shape))}
        return v.rearrange(f"p ({' '.join(names)}) -> p {' '.join(names)}", **kw)

    ident = cst[:, C_ID:C_ID + 128]
    tri = cst[:, C_TRI:C_TRI + 128]
    ones = cst[:, C_ONE:C_ONE + 128]
    on128 = cst[:, C_ON128:C_ON128 + 128]
    causal = cst[:, C_CAUS:C_CAUS + 256]
    gmask = cst[:, C_GMASK:C_GMASK + 128]

    ssq = sm[:, 0:8]
    rst = sm[:, 8:12]
    eps_c = sm[:, 12:13]
    eps4_c = sm[:, 13:14]
    eps512_c = sm[:, 14:15]
    hpi_c = cst[:, C_HPI:C_HPI + 1]
    bd = sm[:, 16:48].rearrange("p (n c) -> p n c", n=2)
    gd = sm[:, 48:64].rearrange("p (n c) -> p n c", n=2)
    bet = sm[:, 64:80].rearrange("p (n c) -> p n c", n=2)
    gcn = sm[:, 80:96].rearrange("p (n c) -> p n c", n=2)
    eg = sm[:, 96:112].rearrange("p (n c) -> p n c", n=2)
    alog = sm[:, 112:120]
    dtb = sm[:, 120:128]
    tA = sm[:, 128:144].rearrange("p (n c) -> p n c", n=2)
    tB = sm[:, 144:160].rearrange("p (n c) -> p n c", n=2)
    c2 = sm[:, 160:176]
    wi = sm[:, 176:208].rearrange("p (n c) -> p n c", n=2)
    gsc = sm[:, 208:224]
    posc = sm[:, 224:226]
    beg = sm[:, 232:240]
    lane_sm = [sm[:, 240 + 48 * i:288 + 48 * i] for i in range(2)]
    mx8 = sm[:, 336:344]

    s_x, s_c, s_v = Slot(sem("in_x")), Slot(sem("in_const")), Slot(sem("in_vec"))
    s_row, s_out, s_dm, s_gb = Slot(sem("in_rows")), Slot(sem("out")), Slot(sem("in_decay")), [Slot(sem(f"in_gate{i}")) for i in range(2)]
    s_fn = Slot(sem("in_final_norm"))
    vst = carve(0, 6, 128)
    t_x = [SP.dma(X[:, i, :], t["x"][0, 128 * i:128 * i + 128, :], s_x) for i in range(2)][-1]
    t_cst = SP.dma(cst[:, :], t["cst"], s_c)
    vec = {}
    vrow = [0]

    def vload(name, src):
        n = src.shape[0]
        vec[name] = vrow[0]
        done = 0
        tok = None
        while done < n:
            r = vrow[0]
            k = min(n - done, 128 - r % 128)
            tok = SP.dma(vst[r % 128:r % 128 + k, r // 128, :], src[done:done + k, :], s_v)
            done += k
            vrow[0] += k
        return tok

    vload("ln1", t["ln1"].rearrange("a (t p) -> (a t) p", p=128))
    vload("ln2", t["ln2"].rearrange("a (t p) -> (a t) p", p=128))
    vload("conv", t["gdn_conv"].rearrange("a i (t p) -> (a i t) p", p=128))
    vload("fconv", t["ffn_conv"].rearrange("a i (t p) -> (a i t) p", p=128))
    vload("fbias", t["ffn_conv_bias"].rearrange("a (t p) -> (a t) p", p=128))
    vload("c", t["c_2"].rearrange("a (t p) -> (a t) p", p=128))
    vload("ng", t["norm_gain_2"].rearrange("a (t p) -> (a t) p", p=128))
    vload("bmod", t["b_mod_2"].rearrange("a (t p) -> (a t) p", p=128))
    vload("gn", t["gdn_norm"])
    vload("qn", t["q_norm_gain_2"])
    vload("kn", t["k_norm_gain_2"])
    t_v = vload("rn", t["ret_norm_gain_2"].rearrange("a (t p) -> (a t) p", p=128))

    def col(name, i):
        c = vec[name] + i
        return VT[:, c:c + 1]

    def cols(name, i, n):
        c = vec[name] + i
        return VT[:, c:c + n]

    pos_i = carve(1024, S, dt=I32)
    posr = carve(1280, S)
    posc_i = carve(1536, 2, dt=I32)
    SP.dma(alog, t["gdn_a_log"].rearrange("a h -> (a h)").partition_broadcast(128), s_row)
    SP.dma(dtb, t["gdn_dt_bias"].rearrange("a h -> (a h)").partition_broadcast(128), s_row)
    t_row = SP.dma(pos_i, t["positions"].rearrange("a s -> (a s)").partition_broadcast(128), s_row)
    pos2_i = carve(2048, S, dt=I32)
    t_row = SP.dma(pos2_i, t["positions_2"].rearrange("a s -> (a s)").partition_broadcast(128), s_row)

    main = [[bank[0], bank[1]], [bank[2], bank[3]]]
    main_free = [[], []]
    bg_free = [(bank[i], []) for i in range(4, 8)]

    def take():
        assert bg_free, "no background bank"
        return bg_free.pop(0)

    def give(b, *toks):
        bg_free.append((b, list(toks)))

    stg_free = [(i, []) for i in range(NSTG)]

    def stage():
        assert stg_free, "no staging buffer"
        i, w = stg_free.pop(0)
        return i, stg[:, i, :], w

    def unstage(i, *toks):
        stg_free.append((i, list(toks)))

    t0 = DV.op(lambda e: e.memset(eps_c, EPS))
    t0 = DV.op(lambda e: e.memset(eps4_c, 4 * EPS))
    t_eps = DV.op(lambda e: e.memset(eps512_c, 512 * EPS))
    nrow = vrow[0]
    t_vt = []
    for k in range((nrow + 127) // 128):
        r = min(128, nrow - 128 * k)
        b, w = take()
        t_ = PE.op(tp(b[:, 0:r], vst[0:r, k, :], ident[0:r, 0:r]), [t_cst, t_v, *w])
        e_ = AC.op(act(VT[:, 128 * k:128 * k + r], b[:, 0:r], ACT.Copy), [t_])
        give(b, e_)
        t_vt.append(e_)
    t_vt = t_vt[-1]

    state = {"h": None, "x": [[t_x] * 4, [t_x] * 4], "h_free": []}

    def sumsq(i, j, after):
        k, s_, w = stage()
        tk = AC.op(act(s_, X[:, i, 512 * j:512 * j + 512], ACT.Square, acc=ssq[:, 4 * i + j:4 * i + j + 1]),
                   [*after, *w])
        unstage(k, tk)
        return tk

    def rstd_of(toks):
        r = DV.op(red(rst[:, 0:2], ssq.rearrange("p (i j) -> p i j", i=2), ADD), toks)
        r = AC.op(act(rst[:, 0:2], rst[:, 0:2], ACT.Sqrt, bias=eps_c, scale=1.0 / D), [r, t_eps])
        return DV.op(recip(rst[:, 2:4], rst[:, 2:4] if False else rst[:, 0:2]), [r])

    def norm_to_h(scale, shift, sq, after):
        r = rstd_of(sq)
        dg = []
        dgt = []
        kd_, dbuf, w = stage()
        for i in range(2):
            dg.append(dbuf[:, 128 * i:128 * i + 128])
            dgt.append(DV.op(ts(dg[i], ident, rst[:, 2 + i:3 + i], MUL), [r, *w]))
        toks = []
        last_pe = None
        for k2 in range(KT // 2):
            b, w = take()
            fs = []
            for kk in range(2):
                for i in range(2):
                    k = 2 * k2 + kk
                    fs.append(mm(b[:, 256 * kk + 128 * i:256 * kk + 128 * i + 128],
                                 X[:, i, 128 * k:128 * k + 128], dg[i]))
            p = PE.op(mms(*fs), [*dgt, *w, *[x for xs in state["x"] for x in xs]])
            last_pe = p
            si, s_, w2 = stage()
            for kk in range(2):
                k = 2 * k2 + kk
                if shift is None:
                    e = DV.op(ts(s_[:, 256 * kk:256 * kk + 256], b[:, 256 * kk:256 * kk + 256], scale(k), MUL),
                              [p, *w2, *after])
                else:
                    e = DV.op(ts(s_[:, 256 * kk:256 * kk + 256], b[:, 256 * kk:256 * kk + 256], scale(k), MUL,
                                 shift(k), ADD), [p, *w2, *after])
            give(b, e)
            hv = hhi[:, 2 * k2:2 * k2 + 2, :].rearrange("p a s -> p (a s)")
            lv = hlo[:, 2 * k2:2 * k2 + 2, :].rearrange("p a s -> p (a s)")
            a = AC.op(act(hv, s_, ACT.Copy), [e, *state["h_free"]])
            l = DV.op(tt(lv, s_, hv, SUB), [a])
            unstage(si, l)
            toks.append(l)
        unstage(kd_, last_pe)
        state["h"] = toks
        state["h_free"] = []

    chunks = []
    blocks = []

    def add(w, c0, n, kt, orient, lhs, evac, need=None, dup=False):
        b = dict(w=w, c0=c0, n=n, kt=kt, orient=orient, lhs=lhs, evac=evac, need=need, dup=dup)
        blocks.append(b)
        per = min(kt, CH // n)
        k = 0
        while k < kt:
            m = min(per, kt - k)
            chunks.append(("w", b, k, m))
            k += m
        return b

    slots = [Slot(sem(f"ring{i}")) for i in range(R1)]
    ring_free = [[] for _ in range(R1)]
    ring_tok = {}
    w_free = [[] for _ in range(R2)]
    w_tok = {}
    sent = [0]
    split = [0]
    wn = [0]
    wslot = {}

    def send(j):
        if j >= len(chunks):
            return
        kind, b, k, m = chunks[j]
        i = j % R1
        n = b["n"]
        dst = ring[:, i, 0:m * n].rearrange("p (k n) -> p k n", n=n)
        src = b["w"][128 * k:128 * (k + m), :].rearrange("(k p) n -> p k n", p=128)
        if b["dup"]:
            h = n // 2
            SP.dma(dst[:, :, 0:h], src[:, :, b["c0"]:b["c0"] + h], slots[i], ring_free[i])
            ring_tok[j] = SP.dma(dst[:, :, h:n], src[:, :, b["c0"]:b["c0"] + h], slots[i])
        else:
            ring_tok[j] = SP.dma(dst, src[:, :, b["c0"]:b["c0"] + n], slots[i], ring_free[i])

    def split_chunk(j):
        kind, b, k, m = chunks[j]
        i = j % R1
        n = m * b["n"]
        if kind == "mod":
            ring_free[i] = [mod_step(b, k, m, ring[:, i, 0:n].rearrange("p (k n) -> p k n", n=b["n"]), ring_tok[j])]
        else:
            q = wn[0] % R2
            wn[0] += 1
            wslot[j] = q
            a = AC.op(act(whi[:, q, 0:n], ring[:, i, 0:n], ACT.Copy), [ring_tok[j], *w_free[q]])
            l = DV.op(tt(wlo[:, q, 0:n], ring[:, i, 0:n], whi[:, q, 0:n], SUB), [a])
            ring_free[i] = [l]
            w_free[q] = None
            w_tok[j] = l
        send(j + R1)

    def ensure(j):
        while split[0] <= min(j, len(chunks) - 1):
            split_chunk(split[0])
            split[0] += 1

    jobs = []

    def step_jobs(n=1):
        for _ in range(n):
            for g in list(jobs[:2]):
                try:
                    next(g)
                except StopIteration:
                    jobs.remove(g)

    def finish(g):
        while g in jobs:
            step_jobs()

    def finish_all():
        while jobs:
            step_jobs()

    pair = [0]

    def run_block(b, j0):
        kind = "w"
        if b["need"] is not None:
            b["need"]()
        cur = pair[0] % 2
        pair[0] += 1
        ps = main[cur]
        free = main_free[cur]
        assert free is not None
        main_free[cur] = None
        n, kt = b["n"], b["kt"]
        lhi, llo, ltok = b["lhs"]()
        j = j0
        tok = None
        started = [False, False]
        while j < len(chunks) and (chunks[j][0] == "mod" or chunks[j][1] is b):
            look = 0
            if chunks[j][0] == "mod":
                ensure(j)
                j += 1
                continue
            ahead, q = 0, j
            while q + 1 < len(chunks) and ahead < LOOK:
                q += 1
                if chunks[q][0] == "w":
                    ahead += 1
            ensure(q)
            _, _, k0, m = chunks[j]
            q = wslot[j]
            wh = whi[:, q, 0:m * n].rearrange("p (k n) -> p k n", n=n)
            wl = wlo[:, q, 0:m * n].rearrange("p (k n) -> p k n", n=n)
            fs = []
            for kk in range(m):
                k = k0 + kk
                last = k == kt - 1
                if b["orient"] == "TM":
                    for i in range(2):
                        o = ps[i][:, 0:n]
                        a, c = slice(128 * i, 128 * i + 128), kk
                        fs.append(mm(o, lhi(k)[:, a], wh[:, kk, :], start=(k == 0), stop=False))
                        fs.append(mm(o, lhi(k)[:, a], wl[:, kk, :], start=False, stop=False))
                        fs.append(mm(o, llo(k)[:, a], wh[:, kk, :], start=False, stop=last))
                else:
                    for ct in range(n // 128):
                        o = ps[ct // 2][:, 256 * (ct % 2):256 * (ct % 2) + 256]
                        a = slice(128 * ct, 128 * ct + 128)
                        fs.append(mm(o, wh[:, kk, a], lhi(k), start=(k == 0 and ct % 2 == 0), stop=False))
                        fs.append(mm(o, wh[:, kk, a], llo(k), start=False, stop=False))
                        fs.append(mm(o, wl[:, kk, a], lhi(k), start=False, stop=last))
            aft = [w_tok[j]]
            if k0 == 0:
                aft += list(free)
                aft += ltok
            tok = PE.op(mms(*fs), aft)
            w_free[q] = [tok]
            j += 1
            if j < len(chunks) and chunks[j][1] is b or not (j < len(chunks)):
                step_jobs()
            elif j < len(chunks):
                more = any(c[1] is b for c in chunks[j:j + 8])
                if more:
                    step_jobs()
        main_free[cur] = b["evac"](ps, tok)
        step_jobs()
        return j

    macc = sb("macc", [128, 512])
    mst = {"free": [], "tok": None, "c": None}
    mod_done = {}
    GB = carve(12288 + 3072, D)

    def add_mod(layer, blk):
        b = dict(w=t["w_mod_2"][layer], c0=512 * blk, n=512, kt=KT, dup=False, layer=layer, blk=blk)
        return [("mod", b, 4 * q, 4) for q in range(4)]

    def mod_step(b, k0, m, w, tok):
        last = None
        for kk in range(m):
            k = k0 + kk
            if k == 0:
                last = DV.op(ts(macc[:, :], w[:, 0, :], c2[:, 0:1], MUL), [tok, *mst["free"], mst["c"]])
            else:
                last = DV.op(stt(macc[:, :], w[:, kk, :], c2[:, k:k + 1], macc[:, :], MUL, ADD), [tok, mst["tok"]])
            mst["tok"] = last
        if k0 + m == KT:
            mod_end(b, last)
        return last

    def mod_end(b, tok):
        L, blk = b["layer"], b["blk"]
        p, w = take()
        if blk < 8:
            t_ = PE.op(mms(*[mm(p[:, i:i + 1], macc[:, 128 * i:128 * i + 128], ones[:, 0:1]) for i in range(4)]),
                       [tok, *w])
            e = DV.op(tt(modcm[:, L, 4 * blk:4 * blk + 4], p[:, 0:4], cols("bmod", 48 * L + 4 * blk, 4), ADD), [t_])
        else:
            g = GB[:, 512 * (blk - 8):512 * (blk - 8) + 512]
            t_ = PE.op(mm(p[:, :], ones, macc[:, :]), [tok, *w])
            e = DV.op(tt(g, p[:, :], g, ADD), [t_, gate_loaded[L]])
        mst["free"] = [t_]
        give(p, e)
        mod_done[(L, blk)] = e

    gate_loaded = {}

    def copy_out(dst, src, after, scale=1.0):
        return AC.op(act(dst, src, ACT.Copy, scale=scale), after)

    def h_ops():
        return (lambda k: hhi[:, k, :]), (lambda k: hlo[:, k, :]), state["h"]

    GQ, GK, GV = carve(0, 8, S), carve(2048, 8, S), carve(4096, 8, S)
    MQ, MK, MV = carve(6144, 8, S), carve(8192, 8, S), carve(10240, 2, GW)
    ZS = carve(12288, 2, GW)
    GBT = carve(8192, KT, S)
    YA = carve(4096, 8, 2, S, dt=BF16)
    YB = carve(6144, 8, 2, S, dt=BF16)
    MHI, MLO = carve(0, KT, S, dt=BF16), carve(2048, KT, S, dt=BF16)
    LANE = [14336, 14336 + 4096]

    tk = {}

    def rope_table(posint, posf, inv, sgn, dst, after, work):
        a, n_, r_ = work
        q = DV.op(cp(posf, posint), after)
        q = DV.op(ts(a, posf, inv, MUL), [q, t_cst])
        q = DV.op(ts(n_, a, 1.0 / (2 * math.pi), MUL, 12582912.0, ADD), [q])
        q = DV.op(ts(n_, n_, 12582912.0, SUB), [q])
        src = a
        for c in TWO_PI:
            q = DV.op(stt(r_, n_, -c, src, MUL, ADD), [q])
            src = r_
        q = DV.op(ts(r_, r_, math.pi, MIN, -math.pi, MAX), [q])
        q1 = AC.op(act(cs[:, dst + 1, :], r_, ACT.Sin), [q])
        q2 = DV.op(ts(cs[:, dst + 1, :], cs[:, dst + 1, :], sgn, MUL), [q1])
        q = DV.op(ts(a, r_, math.pi / 2, ADD), [q])
        q = DV.op(ts(n_, a, math.pi, ALU.is_gt, -2 * math.pi, MUL), [q])
        q = DV.op(tt(a, a, n_, ADD), [q])
        q = DV.op(ts(a, a, math.pi, MIN, -math.pi, MAX), [q])
        q = AC.op(act(cs[:, dst, :], a, ACT.Sin), [q])
        return [q, q2]

    work = [carve(1792 + 512 * i, S) for i in range(3)]
    work = [carve(2560, S), carve(2816, S), carve(3072, S)]
    t_rope1 = rope_table(pos_i, posr, cst[:, C_INV1:C_INV1 + 1], cst[:, C_SG1:C_SG1 + 1], 0, [t_row, t_cst], work)
    t_rope2 = rope_table(pos2_i, posr, cst[:, C_INV2:C_INV2 + 1], cst[:, C_SG2:C_SG2 + 1], 2,
                         [t_row, t_cst, *t_rope1], work)

    q = AC.op(act(gsc, cols("c", 0, 16), ACT.Tanh, scale=0.5), [t_vt])
    q = DV.op(stt(c2, gsc, 1.0, cols("c", 0, 16), ADD, MUL), [q])
    mst["c"] = DV.op(ts(c2, c2, 0.5, MUL), [q])

    sq0 = [sumsq(i, j, [t_x]) for i in range(2) for j in range(4)]
    norm_to_h(lambda k: col("ln1", k), None, sq0, [t_vt])
    early = [*t_rope1, *t_rope2, t_vt, mst["c"]]

    def swap_rope(dst, blk):
        def evac(ps, tok):
            free = []
            for hf in range(2):
                si, s_, w = stage()
                e = copy_out(s_, ps[hf][:, :], [tok, *w])
                free.append(e)
                jobs.insert(0, job(si, s_, e, 4 * blk + 2 * hf))
            return free

        def job(si, s_, e, h):
            sv = s_.rearrange("p (h s) -> p h s", h=2)
            d = dst[:, h:h + 2, :]
            m = DV.op(tt(d, sv, mid(cs[:, 0, :], 2), MUL), [e, *early])
            b, w = take()
            p = PE.op(mm(b[0:32, :], cst[0:32, C_PERM:C_PERM + 32], s_[0:32, :]), [e, *w])
            s2, s2_, w2 = stage()
            u = DV.op(tt(s2_[0:32, :].rearrange("p (h s) -> p h s", h=2),
                         b[0:32, :].rearrange("p (h s) -> p h s", h=2), mid(cs[0:32, 1, :], 2), MUL), [p, *w2])
            give(b, u)
            v = DV.op(tt(d[0:32, :, :], d[0:32, :, :], s2_[0:32, :].rearrange("p (h s) -> p h s", h=2), ADD), [u, m])
            unstage(si, m, p)
            unstage(s2, v)
            tk[("rope", id(dst), h // 2)] = v
            yield
        return evac

    def tm_copy(dst, c0, name, idx):
        def evac(ps, tok):
            f = [copy_out(dst[:, i, c0:c0 + 512], ps[i][:, :], [tok, *early]) for i in range(2)]
            tk[(name, idx)] = f
            return f
        return evac

    for blk in range(2):
        add(t["w_in"][0], 4112 + 512 * blk, 512, KT, "CM", h_ops, swap_rope(MQ, blk))
        add(t["w_in"][0], 5136 + 512 * blk, 512, KT, "CM", h_ops, swap_rope(MK, blk))
        add(t["w_in"][0], 6160 + 512 * blk, 512, KT, "TM", h_ops, tm_copy(MV, 512 * blk, "mv", blk))

    def softmax_rows(L0, L1, e0, e1, n, mcol, rcol, scale, lw):
        a0 = DV.op(red(mcol[:, 0:n], L0, MAX), [e0, *lw])
        a1 = DV.op(red(mcol[:, n:2 * n], L1, MAX), [e1, *lw])
        a = DV.op(ts(mcol, mcol, -scale, MUL), [a0, a1])
        for h in range(n):
            x0 = AC.op(act(L0[:, h, :], L0[:, h, :], ACT.Exp, bias=mcol[:, h:h + 1], scale=scale,
                           acc=rcol[:, h:h + 1]), [a])
            x1 = AC.op(act(L1[:, h, :], L1[:, h, :], ACT.Exp, bias=mcol[:, n + h:n + h + 1], scale=scale,
                           acc=rcol[:, n + h:n + h + 1]), [a])
        r = DV.op(recip(rcol, rcol), [x1])
        n0 = DV.op(tt(L0, L0, rep(rcol[:, 0:n], 128), MUL), [r])
        n1 = DV.op(tt(L1, L1, rep(rcol[:, n:2 * n], 256), MUL), [r])
        return n0, n1

    lane_free = [[], []]

    def split_out(dst, h, src, after):
        sv = src.rearrange("p (h s) -> p h s", h=2)
        a = AC.op(act(dst[:, h:h + 2, 0, :], sv, ACT.Copy), after)
        return DV.op(tt(dst[:, h:h + 2, 1, :], sv, dst[:, h:h + 2, 0, :], SUB), [a])

    def attend_pv(L0, L1, n0, n1, v0, v1, lane, base):
        b0, w0 = take()
        b1, w1 = take()
        PT0, PT1 = carve(base + 1024, 2, 256), carve(base + 1536, 2, 128)
        fs = []
        for h in range(2):
            fs.append(tp(b0[:, 256 * h:256 * h + 128], L0[:, h, :], ident))
            fs.append(tp(b0[:, 256 * h + 128:256 * h + 256], L1[:, h, 0:128], ident))
            fs.append(tp(b1[:, 128 * h:128 * h + 128], L1[:, h, 128:256], ident))
        p = PE.op(mms(*fs), [n0, n1, *w0, *w1])
        c0 = copy_out(PT0, b0[:, :].rearrange("p (h s) -> p h s", h=2), [p, *lane_free[lane]])
        c1 = copy_out(PT1, b1[:, 0:256].rearrange("p (h s) -> p h s", h=2), [p])
        give(b0, c0)
        give(b1, c1)
        return PT0, PT1, p, [c0, c1]

    def moba(hp):
        lane = hp % 2
        base = LANE[lane]
        h0 = 2 * hp
        L0, L1 = carve(base, 2, 128), carve(base + 256, 2, 256)
        sml = lane_sm[lane]
        mcol, rcol = sml[:, 0:4], sml[:, 4:8]
        b0, w0 = take()
        b1, w1 = take()
        fs = []
        for h in range(2):
            fs.append(mm(b0[:, 128 * h:128 * h + 128], MQ[:, h0 + h, 0:128], MK[:, h0 + h, 0:128]))
            fs.append(mm(b1[:, 256 * h:256 * h + 256], MQ[:, h0 + h, 128:256], MK[:, h0 + h, :]))
        p = PE.op(mms(*fs), [tk[("rope", id(MQ), hp)], tk[("rope", id(MK), hp)], *w0, *w1])
        e0 = DV.op(tt(L0, b0[:, 0:256].rearrange("p (h s) -> p h s", h=2), mid(causal[:, 128:256], 2), ADD),
                   [p, *lane_free[lane]])
        e1 = DV.op(tt(L1, b1[:, :].rearrange("p (h s) -> p h s", h=2), mid(causal, 2), ADD), [p, *lane_free[lane]])
        give(b0, e0)
        give(b1, e1)
        yield
        n0, n1 = softmax_rows(L0, L1, e0, e1, 2, mcol, rcol, 128.0 ** -0.5, [])
        yield
        PT0, PT1, pt, cc = attend_pv(L0, L1, n0, n1, None, None, lane, base)
        yield
        b, w = take()
        fs = []
        for h in range(2):
            sl = slice(128 * (h0 + h), 128 * (h0 + h) + 128)
            fs.append(mm(b[:, 256 * h:256 * h + 256], MV[:, 0, sl], PT0[:, h, :], start=(h == 0), stop=False))
            fs.append(mm(b[:, 256 * h + 128:256 * h + 256], MV[:, 1, sl], PT1[:, h, :], start=False, stop=True))
        p = PE.op(mms(*fs), [*cc, *w, *tk[("mv", h0 // 4)]])
        si, s_, w = stage()
        e = copy_out(s_, b[:, :], [p, *w])
        give(b, e)
        o = split_out(YB, h0, s_, [e])
        unstage(si, o)
        lane_free[lane] = [p]
        tk[("yb", hp)] = o
        tk[("moba_read", hp)] = [p]
        yield

    def conv_block(kind, blk):
        dst = {"q": GQ, "k": GK, "v": GV}[kind]
        ch0 = {"q": 0, "k": 8, "v": 16}[kind]

        def evac(ps, tok):
            free = []
            for hf in range(2):
                si, s_, w = stage()
                e = copy_out(s_, ps[hf][:, :], [tok, *w])
                free.append(e)
                jobs.insert(0, job(si, s_, e, 4 * blk + 2 * hf))
            return free

        def job(si, s_, e, h):
            d = dst[:, h:h + 2, :]
            for q_ in range(2):
                x_ = s_[:, 256 * q_:256 * q_ + 256]
                y_ = d[:, q_, :]
                wt = lambda i: col("conv", 24 * i + ch0 + h + q_)
                c_ = DV.op(ts(y_, x_, wt(3), MUL), [e, *early])
                for i in range(3):
                    sh = 3 - i
                    c_ = DV.op(stt(y_[:, sh:S], x_[:, 0:S - sh], wt(i), y_[:, sh:S], MUL, ADD), [c_])
            unstage(si, c_)
            dv = d.rearrange("p h s -> p (h s)")
            s2, s2_, w2 = stage()
            a = AC.op(act(s2_, dv, ACT.Tanh, scale=0.5), [c_, *w2])
            f = DV.op(stt(dv, s2_, 1.0, dv, ADD, MUL), [a])
            if kind == "v":
                unstage(s2, f)
                tk[("gv", h // 2)] = f
                yield
                return
            g = GP.op(tt(s2_, dv, dv, MUL), [f])
            yield
            b, w = take()
            p = PE.op(mm(b[:, :], ones, s2_), [g, *w])
            if kind == "q":
                a = AC.op(act(s2_, b[:, :], ACT.Sqrt, bias=eps512_c, scale=128.0), [p, t_eps])
            else:
                a = AC.op(act(s2_, b[:, :], ACT.Sqrt, bias=eps4_c, scale=1.0), [p, t_eps])
            give(b, a)
            r = DV.op(recip(s2_, s2_), [a])
            m = GP.op(tt(dv, dv, s2_, MUL), [r])
            unstage(s2, m)
            tk[("g" + kind, h // 2)] = m
            yield
        return evac

    def evac_bd(ps, tok):
        es = [copy_out(bd[:, i, :], ps[i][:, 0:16], [tok]) for i in range(2)]
        jobs.insert(0, job_bd(es))
        return es

    def job_bd(es):
        a = AC.op(act(bet, bd[:, :, 0:8], ACT.Tanh, scale=0.5), es)
        tk["bet"] = DV.op(ts(bet, bet, 1.0, ADD, 0.5, MUL), [a])
        z = DV.op(tt(tA, bd[:, :, 8:16], mid(dtb, 2), ADD), [*es, t_row])
        n_ = DV.op(ts(tB, tA, -1.0, MUL), [z])
        n_ = DV.op(tt(tB, tB, tA, MAX), [n_])
        n_ = AC.op(act(tB, tB, ACT.Exp, scale=-1.0), [n_])
        n_ = AC.op(act(tB, tB, ACT.Ln, bias=ones[:, 0:1]), [n_, t_cst])
        z = DV.op(ts(tA, tA, 0.0, MAX), [z, n_])
        z = DV.op(tt(tA, tA, tB, ADD), [z])
        ea = AC.op(act(alog, alog, ACT.Exp), [t_row])
        g = DV.op(stt(gd, tA, -1.0, mid(alog, 2), MUL, MUL), [z, ea])
        tk["g"] = g
        yield
        b, w = take()
        p = PE.op(mm(b[:, 0:16], tri, gd.rearrange("p n c -> p (n c)")), [g, *w])
        v = DV.op(ts(gcn, b[:, 0:16].rearrange("p (n c) -> p n c", n=2), -1.0, MUL), [p])
        give(b, v)
        x_ = AC.op(act(eg, gcn, ACT.Exp, scale=-1.0), [v])
        tk["gcn"] = v
        tk["eg"] = x_
        tk["beg"] = DV.op(tt(beg, bet[:, 1, :], eg[:, 1, :], MUL), [x_, tk["bet"]])
        yield

    def gdn(bt):
        lane = bt % 2
        base = LANE[lane]
        h0 = 2 * bt
        GM, AT, XT, XX, PP, AL, QK, VB = (carve(base + 512 * i, 4, 128) for i in range(8))
        KX = GM
        sml = lane_sm[lane]
        gl, ekd, oss, orr = sml[:, 0:2], sml[:, 2:4], sml[:, 4:8], sml[:, 8:12]
        U = [(u, h0 + u // 2, u % 2, slice(128 * (u % 2), 128 * (u % 2) + 128)) for u in range(4)]
        fl = lambda a: a.rearrange("p a b -> p (a b)")
        b1, w1 = take()
        b2, w2 = take()
        p1 = PE.op(mms(*[mm(b1[:, 128 * u:128 * u + 128], gd[:, n, h:h + 1].to_broadcast([128, 128]), tri)
                         for u, h, n, c in U]), [tk["g"], *w1])
        p2 = PE.op(mms(*[mm(b2[:, 128 * u:128 * u + 128], bet[:, n, h:h + 1].to_broadcast([128, 128]), ident)
                         for u, h, n, c in U]), [tk["bet"], *w2])
        lw = lane_free[lane]
        for u, h, n, c in U:
            m = DV.op(stt(GM[:, u, :], b1[:, 128 * u:128 * u + 128], gcn[:, n, h:h + 1], gmask, ADD, ADD),
                      [p1, tk["gcn"], *lw])
        gl_t = DV.op(cp(gl, b1[:, :].rearrange("p (a b) -> p a b", a=4)[:, 0:4:2, 127]), [p1])
        br = copy_out(fl(PP), b2[:, :], [p2, *lw])
        ex = AC.op(act(fl(GM), fl(GM), ACT.Exp), [m])
        for q_ in range(2):
            ek = AC.op(act(ekd[:, q_:q_ + 1], gcn[:, 0, h0 + q_:h0 + q_ + 1], ACT.Exp, bias=gl[:, q_:q_ + 1]), [gl_t])
        yield
        p1 = PE.op(mms(*[mm(b1[:, 128 * u:128 * u + 128], GK[:, h, c], GK[:, h, c]) for u, h, n, c in U]),
                   [tk[("gk", bt)], m, gl_t])
        p2 = PE.op(mms(*[mm(b2[:, 128 * u:128 * u + 128], GK[:, h, c], GQ[:, h, c]) for u, h, n, c in U]),
                   [tk[("gq", bt)], br])
        a = DV.op(tt(fl(AT), b1[:, :], fl(GM), MUL), [p1, ex, *lw])
        qk = DV.op(tt(fl(QK), b2[:, :], fl(GM), MUL), [p2, ex, *lw])
        at = GP.op(tt(fl(AT), fl(AT), fl(PP), MUL), [a, br])
        yield
        p1 = PE.op(mms(*[tp(b1[:, 128 * u:128 * u + 128], GV[:, h, c], ident) for u, h, n, c in U]),
                   [tk[("gv", bt)], a])
        p2 = PE.op(mms(*[tp(b2[:, 128 * u:128 * u + 128], GK[:, h, c], ident) for u, h, n, c in U]), [qk])
        for u, h, n, c in U:
            vb = DV.op(ts(VB[:, u, :], b1[:, 128 * u:128 * u + 128], bet[:, n, h:h + 1], MUL, 0.5, MUL),
                       [p1, tk["bet"], *lw])
            sc = ekd[:, u // 2:u // 2 + 1] if n == 0 else beg[:, h:h + 1]
            kx = DV.op(ts(KX[:, u, :], b2[:, 128 * u:128 * u + 128], sc, MUL), [p2, ek, qk, a, tk["beg"]])
        lev = lambda l: mid(cst[:, C_LEV + 128 * l:C_LEV + 128 * l + 128], 4)
        al = GP.op(tt(AL, AT, lev(0), MUL), [at, *lw])
        xt = DV.op(tt(XT, mid(ident, 4), AL, SUB), [al, *lw])
        al_free = xt
        yield
        p1 = PE.op(mms(*[tp(b1[:, 128 * u:128 * u + 128], XT[:, u, :], ident) for u in range(4)]), [xt, vb])
        xx = copy_out(fl(XX), b1[:, :], [p1, *lw])
        pz = None
        for l in range(1, 7):
            al = GP.op(tt(AL, AT, lev(l), MUL), [al_free])
            yield
            p1 = PE.op(mms(*[mm(b1[:, 128 * u:128 * u + 128], AL[:, u, :], XX[:, u, :]) for u in range(4)]),
                       [al, xx, xt])
            al_free = p1
            pp = copy_out(fl(PP), b1[:, :], [p1, at, pz])
            yield
            p1 = PE.op(mms(*[mm(b1[:, 128 * u:128 * u + 128], PP[:, u, :], XT[:, u, :]) for u in range(4)]),
                       [pp, xt])
            if l < 6:
                pz = PE.op(mms(*[mm(b2[:, 128 * u:128 * u + 128], XT[:, u, :], PP[:, u, :]) for u in range(4)]),
                           [kx, xx])
                xt = DV.op(tt(fl(XT), fl(XT), b1[:, :], SUB), [p1, pz])
                xx = DV.op(tt(fl(XX), fl(XX), b2[:, :], SUB), [pz])
            else:
                xt = DV.op(tt(fl(XT), fl(XT), b1[:, :], SUB), [p1])
        yield
        VN, WT, SS, QS = AT, XX, AL, PP
        p1 = PE.op(mms(*[mm(b1[:, 128 * u:128 * u + 128], XT[:, u, :], VB[:, u, :]) for u in range(4)]), [xt])
        p2 = PE.op(mms(*[mm(b2[:, 128 * q_:128 * q_ + 128], KX[:, 2 * q_ + 1, :], XT[:, 2 * q_ + 1, :])
                         for q_ in range(2)]), [xt, xx, kx])
        vn = copy_out(fl(VN), b1[:, :], [p1, al])
        wt = copy_out(fl(WT)[:, 0:256], b2[:, 0:256], [p2, xx, p1])
        yield
        p1 = PE.op(mms(*[mm(b1[:, 128 * q_:128 * q_ + 128], KX[:, 2 * q_, :], VN[:, 2 * q_, :]) for q_ in range(2)]),
                   [vn])
        ss = copy_out(fl(SS)[:, 0:256], b1[:, 0:256], [p1])
        yield
        p2 = PE.op(mms(*[mm(b2[:, 128 * q_:128 * q_ + 128], WT[:, q_, :], SS[:, q_, :]) for q_ in range(2)]),
                   [wt, ss])
        p1 = PE.op(mms(*[mm(b1[:, 128 * q_:128 * q_ + 128], GQ[:, h0 + q_, 128:256], SS[:, q_, :])
                         for q_ in range(2)]), [ss])
        for q_ in range(2):
            v1 = DV.op(tt(VN[:, 2 * q_ + 1, :], VN[:, 2 * q_ + 1, :], b2[:, 128 * q_:128 * q_ + 128], SUB), [p2, vn])
            qs = AC.op(act(QS[:, q_, :], b1[:, 128 * q_:128 * q_ + 128], ACT.Copy, scale=eg[:, 1, h0 + q_:h0 + q_ + 1]),
                       [p1, tk["eg"]])
        yield
        p2 = PE.op(mms(*[mm(b2[:, 128 * u:128 * u + 128], QK[:, u, :], VN[:, u, :]) for u in range(4)]), [v1])
        O = XT
        o4 = b2[:, :].rearrange("p (h n d) -> p h n d", h=2, n=2)
        Ov = O.rearrange("p (h n) d -> p h n d", h=2)
        o0 = DV.op(cp(Ov[:, :, 0, :], o4[:, :, 0, :]), [p2])
        o1 = DV.op(tt(Ov[:, :, 1, :], o4[:, :, 1, :], QS[:, 0:2, :], ADD), [p2, qs])
        sq = GP.op(tt(fl(VB), fl(O), fl(O), MUL), [o0, o1])
        r = DV.op(red(oss, VB, ADD), [sq])
        r = AC.op(act(orr, oss, ACT.Sqrt, bias=eps_c, scale=1.0 / 128), [r, t_eps])
        r = DV.op(recip(orr, orr), [r])
        for u, h, n, c in U:
            og = DV.op(stt(O[:, u, :], O[:, u, :], orr[:, u:u + 1], ZS[:, n, 128 * h:128 * h + 128], MUL, MUL),
                       [r, sq, *tk[("zs", h // 4)]])
        yield
        p1 = PE.op(mms(*[tp(b1[:, 128 * u:128 * u + 128], O[:, u, :], ident) for u in range(4)]), [og, qs])
        si, s_, w = stage()
        e = DV.op(ts(s_, b1[:, :], col("gn", 0), MUL, 0.5, MUL), [p1, *w])
        give(b1, e)
        give(b2, o1)
        o = split_out(YA, h0, s_, [e])
        unstage(si, o)
        lane_free[lane] = [p1, o]
        tk[("ya", bt)] = o
        yield

    for blk in range(2):
        for kind, c0 in (("q", 0), ("k", 1024), ("v", 2048)):
            def need(blk=blk, kind=kind):
                if kind == "q":
                    for hp in (2 * blk, 2 * blk + 1):
                        jobs.append(moba(hp))
                if blk == 1 and kind == "k":
                    pass
            add(t["w_in"][0], c0 + 512 * blk, 512, KT, "CM", h_ops, conv_block(kind, blk), need)
        if blk == 0:
            add(t["w_in"][0], 3072, 16, KT, "TM", h_ops, evac_bd)

    def z_evac(blk):
        def evac(ps, tok):
            f = []
            for i in range(2):
                si, s_, w = stage()
                e = copy_out(s_, ps[i][:, :], [tok, *w])
                f.append(e)
                jobs.insert(0, job(si, s_, e, i))
            return f

        def job(si, s_, e, i):
            z_ = ZS[:, i, 512 * blk:512 * blk + 512]
            a = AC.op(act(z_, s_, ACT.Tanh, scale=0.5), [e, *early])
            r = DV.op(stt(z_, z_, 1.0, s_, ADD, MUL), [a])
            unstage(si, r)
            tk.setdefault(("zs", blk), []).append(r)
            yield
        return evac

    for blk in range(2):
        def need(blk=blk):
            if blk == 1:
                finish_all()
                jobs.append(gdn(0))
                jobs.append(gdn(1))
        add(t["w_in"][0], 3088 + 512 * blk, 512, KT, "TM", h_ops, z_evac(blk), need)

    def gb_evac(blk):
        def evac(ps, tok):
            f = []
            for hf in range(2):
                f.append(AC.op(act(GBT[:, 4 * blk + 2 * hf:4 * blk + 2 * hf + 2, :].rearrange("p a s -> p (a s)"),
                                   ps[hf][:, :], ACT.Tanh, scale=0.5), [tok, *[x for hp in range(4)
                                                                            for x in tk[("moba_read", hp)]]]))
            tk[("gb", blk)] = f
            return f
        return evac

    for blk in range(4):
        def need(blk=blk):
            if blk == 0:
                jobs.append(gdn(2))
                jobs.append(gdn(3))
        add(t["w_in"][0], 9232 + 512 * blk, 512, KT, "CM", h_ops, gb_evac(blk), need)

    merge = {}

    def ga_evac(blk):
        def evac(ps, tok):
            f = []
            for hf in range(2):
                si, s_, w = stage()
                e = AC.op(act(s_, ps[hf][:, :], ACT.Tanh, scale=0.5), [tok, *w])
                f.append(e)
                merge[(blk, hf)] = (si, s_, e)
            return f
        return evac

    def ya_evac(blk):
        def evac(ps, tok):
            f = []
            for hf in range(2):
                si, s_, e = merge[(blk, hf)]
                m = DV.op(stt(s_, s_, 1.0, ps[hf][:, :], ADD, MUL), [tok, e])
                merge[(blk, hf)] = (si, s_, m)
                f.append(m)
            return f
        return evac

    def yb_evac(blk):
        def evac(ps, tok):
            f = []
            for hf in range(2):
                si, s_, m = merge[(blk, hf)]
                k = 4 * blk + 2 * hf
                g = GBT[:, k:k + 2, :].rearrange("p a s -> p (a s)")
                y = DV.op(stt(g, g, 1.0, ps[hf][:, :], ADD, MUL), [tok, *tk[("gb", blk)]])
                f.append(y)
                y = GP.op(tt(s_, s_, g, ADD), [y, m])
                hv, lv = (v[:, k:k + 2, :].rearrange("p a s -> p (a s)") for v in (MHI, MLO))
                a = AC.op(act(hv, s_, ACT.Copy), [y])
                l = DV.op(tt(lv, s_, hv, SUB), [a])
                unstage(si, l)
                tk.setdefault("merged", []).append(l)
            return f
        return evac

    def y_ops(Y, name):
        return lambda: ((lambda k: Y[:, k, 0, :]), (lambda k: Y[:, k, 1, :]), [tk[(name, i)] for i in range(4)])

    for blk in range(4):
        add(t["w_in"][0], 7184 + 512 * blk, 512, KT, "CM", h_ops, ga_evac(blk))
        add(t["w_branch_a"][0], 512 * blk, 512, 8, "CM", y_ops(YA, "ya"), ya_evac(blk),
            finish_all if blk == 0 else None)
        add(t["w_branch_b"][0], 512 * blk, 512, 8, "CM", y_ops(YB, "yb"), yb_evac(blk))

    def resid(blk, half):
        def evac(ps, tok):
            f = []
            for i in range(2):
                xs = X[:, i, 512 * blk:512 * blk + 512]
                e = DV.op(stt(xs, ps[i][:, :], half, xs, MUL, ADD), [tok, *state["sq_read"]])
                f.append(e)
                state["x"][i][blk] = e
                state["sq"].append(sumsq(i, blk, [e]))
            return f
        return evac

    def m_ops():
        state["h_free"] = []
        state["sq"] = []
        state["sq_read"] = []
        return (lambda k: MHI[:, k, :]), (lambda k: MLO[:, k, :]), tk["merged"]

    first = [True]

    def m_ops1():
        if first[0]:
            first[0] = False
            state["sq"], state["sq_read"] = [], []
        return (lambda k: MHI[:, k, :]), (lambda k: MLO[:, k, :]), tk["merged"]

    for blk in range(4):
        add(t["w_out"][0], 512 * blk, 512, KT, "TM", m_ops1, resid(blk, 0.5))

    AHI, ALO = carve(0, FT, S, dt=BF16), carve(5632, FT, S, dt=BF16)
    SG = carve(11264, 4, S)
    B0, B1 = carve(12288, 8, 128), carve(13312, 8, 256)

    def ffn_need():
        norm_to_h(lambda k: col("ln2", k), None, state["sq"], [t_vt])

    fst = {"sg": [], "sgr": [], "uv": []}

    def up_evac(val, j):
        def evac(ps, tok):
            f = []
            for hf in range(2):
                si, s_, w = stage()
                e = copy_out(s_, ps[hf][:, :], [tok, *w])
                f.append(e)
                jobs.insert(0, job(si, s_, e, hf))
            return f

        def job(si, s_, e, hf):
            s2, s2_, w2 = stage()
            dst = s2_
            for q_ in range(2):
                ch = (FT if val else 0) + 4 * j + 2 * hf + q_
                x_ = s_[:, 256 * q_:256 * q_ + 256]
                y_ = dst[:, 256 * q_:256 * q_ + 256]
                wt = lambda i: col("fconv", 88 * i + ch)
                c_ = DV.op(ts(y_, x_, wt(2), MUL, col("fbias", ch), ADD), [e, *w2])
                for i in range(2):
                    sh = 2 - i
                    c_ = DV.op(stt(y_[:, sh:S], x_[:, 0:S - sh], wt(i), y_[:, sh:S], MUL, ADD), [c_])
            g = SG[:, 2 * hf:2 * hf + 2, :].rearrange("p a s -> p (a s)")
            if not val:
                a = AC.op(act(s_, dst, ACT.Tanh, scale=0.5), [c_])
                r = DV.op(stt(g, s_, 1.0, dst, ADD, MUL), [a, fst.get(("free", hf))])
                fst[("sg", hf)] = r
                unstage(si, r)
                unstage(s2, r)
            else:
                r = GP.op(tt(s2_, s2_, g, MUL), [c_, fst[("sg", hf)]])
                fst[("free", hf)] = r
                k = 4 * j + 2 * hf
                hv, lv = (v[:, k:k + 2, :].rearrange("p a s -> p (a s)") for v in (AHI, ALO))
                a = AC.op(act(hv, s2_, ACT.Copy), [r])
                l = DV.op(tt(lv, s2_, hv, SUB), [a])
                unstage(si, c_)
                unstage(s2, l)
                tk.setdefault("act", []).append(l)
            yield
        return evac

    for j in range(11):
        add(t["w_up"][0], 512 * j, 512, KT, "CM", h_ops, up_evac(False, j), ffn_need if j == 0 else None)
        add(t["w_up"][0], DFF + 512 * j, 512, KT, "CM", h_ops, up_evac(True, j))

    first2 = [True]

    def a_ops():
        if first2[0]:
            first2[0] = False
            state["sq"], state["sq_read"] = [], []
        return (lambda k: AHI[:, k, :]), (lambda k: ALO[:, k, :]), tk["act"]

    for blk in range(4):
        add(t["w_down"][0], 512 * blk, 512, FT, "TM", a_ops, resid(blk, 0.5), finish_all if blk == 0 else None)

    RB = carve(17408, 32, 8)
    REL = carve(17664, 2, S, dt=I32)
    RELF = carve(18176, 2, S)
    MSK = carve(18688, 2, S)
    PR = carve(19200, S, dt=I32)
    PCI = carve(19456, 2, dt=I32)
    s_rb = Slot(sem("in_bias"))

    def bias_job():
        after = [state["ffn_ready"]]
        SP.dma(RB, t["rel_bias_2"].rearrange("b h -> (b h)").partition_broadcast(128), s_rb, after)
        SP.dma(PR, t["positions_2"].rearrange("a s -> (a s)").partition_broadcast(128), s_rb, after)
        for i in range(2):
            r = SP.dma(PCI[:, i:i + 1], t["positions_2"][0, 128 * i:128 * i + 128].unsqueeze(1), s_rb, after)
        yield
        q = DV.op(lambda e: e.tensor_single_scalar(PR, PR, -1, ALU.bitwise_xor), [r])
        for i in range(2):
            q1 = GP.op(tt(REL[:, i, :], PR, PCI[:, i:i + 1].to_broadcast([128, S]), ADD), [q])
        q1 = DV.op(cp(RELF, REL), [q1])
        rbf = RB.rearrange("p b h -> p (b h)")
        d_ = None
        DLT = carve(19460, 31, 8)
        d_ = DV.op(tt(DLT, RB[:, 1:32, :], RB[:, 0:31, :], SUB), [r])
        for h in range(8):
            b0 = DV.op(ts(B0[:, h, :], RELF[:, 0, 0:128], 0.0, MUL, RB[:, 0, h:h + 1], ADD), [q1, r])
            b1 = DV.op(ts(B1[:, h, :], RELF[:, 1, :], 0.0, MUL, RB[:, 0, h:h + 1], ADD), [q1, r])
        yield
        thr = thresholds()
        last = {}
        for b in range(31):
            m = DV.op(ts(MSK, RELF, float(thr[b] - 1), ALU.is_ge), [q1, *last.values()])
            for h in range(8):
                last[h] = DV.op(stt(B0[:, h, :], MSK[:, 0, 0:128], DLT[:, b, h:h + 1], B0[:, h, :], MUL, ADD),
                                [m, d_, b0, last.get(h)])
                last[(1, h)] = DV.op(stt(B1[:, h, :], MSK[:, 1, :], DLT[:, b, h:h + 1], B1[:, h, :], MUL, ADD),
                                     [m, d_, b1, last.get((1, h))])
                if h % 3 == 2:
                    yield
        tk["bias"] = list(last.values())
        yield

    QA, KA, VA = carve(0, 8, S), carve(2048, S), carve(2304, 2, 128)
    KI, QI = carve(2560, S), carve(2816, 8, S)
    QB, KB, VBB = carve(4864, 8, S), carve(6912, 8, S), carve(8960, 2, GW)
    YA2 = carve(0, 8, 2, S, dt=BF16)
    YB2 = carve(2816, 8, 2, S, dt=BF16)
    YAF, YBF = QA, QI
    MN0, MN1 = carve(11008, 128), carve(11136, S)
    IW = carve(11392, 2, S)
    IT = carve(11904, 384)
    DM = carve(17408, 8, 384)
    W2 = 17408 + 3072

    def layer2(L):
        dm = {}
        WIN = t["w_in_2"][L]

        def start():
            if L == 0:
                r = rstd_of(state["sq"])
                fn = carve(0, D)
                f = SP.dma(fn, t["final_norm"].partition_broadcast(128), s_fn, [r])
                state["sq"] = []
                for i in range(2):
                    for j in range(4):
                        xs = X[:, i, 512 * j:512 * j + 512]
                        e = DV.op(stt(xs, xs, rst[:, 2 + i:3 + i], fn[:, 512 * j:512 * j + 512], MUL, MUL), [f, r])
                        state["x"][i][j] = e
                        state["sq"].append(sumsq(i, j, [e, r]))
                state["fn_read"] = e
                dm["dm"] = SP.dma(DM, t["dm"].rearrange("p (h s) -> p h s", h=8), s_dm, tk["bias"])
                tk["dm"] = dm["dm"]
            g = DV.op(stt(gsc, modcm[:, L, 16:32], 1.0, cols("ng", 16 * L, 16), ADD, MUL),
                      [mod_done[(L, b)] for b in range(8)] + state["gsc_free"])
            norm_to_h(lambda k: gsc[:, k:k + 1], lambda k: modcm[:, L, k:k + 1], state["sq"], [g])
            state["gsc_free"] = [state["h"][-1]]
            gate_loaded[L] = SP.dma(GB, t["b_mod_2"][L, 4096:6144].partition_broadcast(128), s_gb[L], state["gb_free"])
            ready[0] = [state["h"][-1], state.get("fn_read")]

        ready = [[]]

        def ki_evac(ps, tok):
            e = copy_out(KI, ps[0][:, 0:256], [tok, *ready[0]])
            tk["ki"] = e
            return [e]

        def wi_evac(ps, tok):
            e = [copy_out(wi[:, i, :], ps[i][:, 0:16], [tok]) for i in range(2)]
            tk["wi"] = e
            return e

        def qi_evac(blk):
            def evac(ps, tok):
                f = [copy_out(QI[:, 4 * blk + 2 * hf:4 * blk + 2 * hf + 2, :].rearrange("p a s -> p (a s)"),
                              ps[hf][:, :], [tok, *ready[0]]) for hf in range(2)]
                tk[("qi", blk)] = f
                return f
            return evac

        def indexer():
            a0 = carve(W2, 2, 128)
            a1 = carve(W2 + 256, 2, 256)
            g0 = g1 = None
            for ti in range(8):
                b0, w0 = take()
                b1, w1 = take()
                fs = []
                for hh, bk in ((0, b0), (1, b1)):
                    pp = slice(64 * hh, 64 * hh + 64)
                    fs.append(mm(bk[:, 0:128], QI[pp, ti, 0:128], KI[pp, 0:128]))
                    fs.append(mm(bk[:, 128:384], QI[pp, ti, 128:256], KI[pp, :]))
                p = PE.op(mms(*fs), [*tk[("qi", ti // 4)], tk["ki"], *w0, *w1])
                if ti == 0:
                    x0, x1, w = a0, a1, [*lane_free[0], *lane_free[1]]
                else:
                    si, s_, w = stage()
                    sj, t_, w3 = stage()
                    x0 = s_[:, 0:256].rearrange("p (h s) -> p h s", h=2)
                    x1 = t_.rearrange("p (h s) -> p h s", h=2)
                    w = [*w, *w3]
                ev = []
                for hh, bk in ((0, b0), (1, b1)):
                    DV.op(ts(x0[:, hh, :], bk[:, 0:128], 0.0, MAX, wi[:, 0, 2 * ti + hh:2 * ti + hh + 1], MUL),
                          [p, *tk["wi"], *w])
                    ev.append(DV.op(ts(x1[:, hh, :], bk[:, 128:384], 0.0, MAX,
                                       wi[:, 1, 2 * ti + hh:2 * ti + hh + 1], MUL), [p]))
                e0, e1 = ev
                if ti == 0:
                    g0 = g1 = e1
                else:
                    g0 = GP.op(tt(a0, a0, x0, ADD), [e1, g0])
                    g1 = GP.op(tt(a1, a1, x1, ADD), [e1, g1])
                    unstage(si, g0)
                    unstage(sj, g1)
                give(b0, e0)
                give(b1, e1)
                yield
            tk["qi_read"] = p
            r0, r1 = IW[:, 0, 0:128], IW[:, 1, :]
            q0 = DV.op(tt(r0, a0[:, 0, :], a0[:, 1, :], ADD), [g0, *ready[0]])
            q1 = DV.op(tt(r1, a1[:, 0, :], a1[:, 1, :], ADD), [g1])
            q0 = DV.op(tt(r0, r0, causal[:, 128:256], ADD), [q0])
            q1 = DV.op(tt(r1, r1, causal, ADD), [q1])
            mxa, mxb = mx8, sm[:, 344:352]
            for it in range(8):
                x0 = DV.op(lambda e: e.max(mxa, r0), [q0])
                x1 = DV.op(lambda e: e.max(mxb, r1), [q1])
                q0 = DV.op(lambda e: e.match_replace(r0, mxa, r0, -3e38), [x0])
                q1 = DV.op(lambda e: e.match_replace(r1, mxb, r1, -3e38), [x1])
                if it % 2:
                    yield
            q0 = DV.op(ts(MN0, r0, -2e38, ALU.is_gt, NEG, MUL), [q0])
            q1 = DV.op(ts(MN1, r1, -2e38, ALU.is_gt, NEG, MUL), [q1])
            q0 = DV.op(tt(MN0, MN0, causal[:, 128:256], ADD), [q0])
            q1 = DV.op(tt(MN1, MN1, causal, ADD), [q1])
            tk["sel"] = [q0, q1]
            lane_free[0] = lane_free[1] = [q0, q1]
            yield

        def headnorm(dst, name, gain, nh, blk):
            def evac(ps, tok):
                f = []
                for hf in range((nh + 1) // 2):
                    si, s_, w = stage()
                    m = 512 if nh > 1 else 256
                    e = copy_out(s_[:, 0:m], ps[hf][:, 0:m], [tok, *w])
                    f.append(e)
                    jobs.insert(0, job(si, s_, e, hf, m))
                return f

            def job(si, s_, e, hf, m):
                s2, s2_, w2 = stage()
                g = GP.op(tt(s2_[:, 0:m], s_[:, 0:m], s_[:, 0:m], MUL), [e, *w2])
                b, w = take()
                p = PE.op(mm(b[:, 0:m], on128, s2_[:, 0:m]), [g, *w])
                a = AC.op(act(s2_[:, 0:m], b[:, 0:m], ACT.Sqrt, bias=eps_c), [p, t_eps])
                give(b, a)
                r = DV.op(recip(s2_[:, 0:m], s2_[:, 0:m]), [a])
                d = dst if nh == 1 else dst[:, 4 * blk + 2 * hf:4 * blk + 2 * hf + 2, :].rearrange("p a s -> p (a s)")
                r = DV.op(stt(d, s_[:, 0:m], gain, s2_[:, 0:m], MUL, MUL), [r, *ready[0]])
                unstage(si, r)
                unstage(s2, r)
                tk[(name, 2 * blk + hf)] = r
                yield
            return evac

        def va_evac(ps, tok):
            e = [copy_out(VA[:, i, :], ps[i][:, 0:128], [tok, *ready[0]]) for i in range(2)]
            tk["va"] = e
            return e

        def sparse(hp):
            h0 = 2 * hp
            base = W2
            L0, L1 = carve(base, 2, 128), carve(base + 256, 2, 256)
            mcol, rcol = lane_sm[0][:, 0:4], lane_sm[0][:, 4:8]
            lw = lane_free[0]
            g0 = GP.op(tt(L0, B0[:, h0:h0 + 2, :], mid(MN0, 2), ADD), [*tk["sel"], *tk["bias"], *lw])
            g1 = GP.op(tt(L1, B1[:, h0:h0 + 2, :], mid(MN1, 2), ADD), [*tk["sel"], *tk["bias"], *lw])
            b0, w0 = take()
            b1, w1 = take()
            fs = []
            for h in range(2):
                fs.append(mm(b0[:, 128 * h:128 * h + 128], QA[:, h0 + h, 0:128], KA[:, 0:128]))
                fs.append(mm(b1[:, 256 * h:256 * h + 256], QA[:, h0 + h, 128:256], KA))
            p = PE.op(mms(*fs), [tk[("qa", hp)], tk[("ka", 0)], *w0, *w1])
            e0 = DV.op(stt(L0, b0[:, 0:256].rearrange("p (h s) -> p h s", h=2), 128.0 ** -0.5, L0, MUL, ADD), [p, g0])
            e1 = DV.op(stt(L1, b1[:, :].rearrange("p (h s) -> p h s", h=2), 128.0 ** -0.5, L1, MUL, ADD), [p, g1])
            give(b0, e0)
            give(b1, e1)
            yield
            n0, n1 = softmax_rows(L0, L1, e0, e1, 2, mcol, rcol, 1.0, [])
            yield
            PT0, PT1, pt, cc = attend_pv(L0, L1, n0, n1, None, None, 0, base)
            yield
            b, w = take()
            fs = []
            for h in range(2):
                fs.append(mm(b[:, 256 * h:256 * h + 256], VA[:, 0, :], PT0[:, h, :], start=(h == 0), stop=False))
                fs.append(mm(b[:, 256 * h + 128:256 * h + 256], VA[:, 1, :], PT1[:, h, :], start=False, stop=True))
            p = PE.op(mms(*fs), [*cc, *w, *tk["va"]])
            e = copy_out(YAF[:, h0:h0 + 2, :].rearrange("p a s -> p (a s)"), b[:, :], [p])
            give(b, e)
            lane_free[0] = [p]
            tk[("yaf", hp)] = e
            yield

        def rot(dst, name, blk):
            def evac(ps, tok):
                f = []
                for hf in range(2):
                    si, s_, w = stage()
                    e = copy_out(s_, ps[hf][:, :], [tok, *w])
                    f.append(e)
                    jobs.insert(0, job(si, s_, e, 2 * blk + hf))
                return f

            def job(si, s_, e, hp):
                d = dst[:, 2 * hp:2 * hp + 2, :]
                sv = s_.rearrange("p (h s) -> p h s", h=2)
                s2, s2_, w2 = stage()
                s2v = s2_.rearrange("p (h s) -> p h s", h=2)
                m = DV.op(tt(d, sv, mid(cs[:, 2, :], 2), MUL), [e, *ready[0]])
                x_ = DV.op(tt(s2v[0:64], sv[64:128], mid(cs[64:128, 3, :], 2), MUL), [e, *w2])
                x_ = DV.op(tt(s2v[64:128], sv[0:64], mid(cs[0:64, 3, :], 2), MUL), [e, *w2])
                g = GP.op(tt(d, d, s2v, ADD), [m, x_])
                unstage(si, x_)
                unstage(s2, g)
                tk[(name, hp)] = g
                yield
            return evac

        def vb_evac(blk):
            def evac(ps, tok):
                f = [copy_out(VBB[:, i, 512 * blk:512 * blk + 512], ps[i][:, :], [tok, *ready[0]]) for i in range(2)]
                tk[("vb", blk)] = f
                return f
            return evac

        def retain(hp):
            h0 = 2 * hp
            base = W2 + 1792
            si, s_, w = stage()
            sj, t_, w3 = stage()
            S0, S1 = s_.rearrange("p (h s) -> p h s", h=2), t_[:, 0:256].rearrange("p (h s) -> p h s", h=2)
            b0, w0 = take()
            b1, w1 = take()
            fs = []
            for h in range(2):
                fs.append(mm(b0[:, 256 * h:256 * h + 256], KB[:, h0 + h, 0:128], QB[:, h0 + h, :]))
                fs.append(mm(b1[:, 128 * h:128 * h + 128], KB[:, h0 + h, 128:256], QB[:, h0 + h, 128:256]))
            p = PE.op(mms(*fs), [tk[("qb", hp)], tk[("kb", hp)], *w0, *w1])
            e0 = DV.op(tt(S0, b0[:, :].rearrange("p (h s) -> p h s", h=2), DM[:, h0:h0 + 2, 0:256], MUL),
                       [p, tk["dm"], *w])
            e1 = DV.op(tt(S1, b1[:, 0:256].rearrange("p (h s) -> p h s", h=2), DM[:, h0:h0 + 2, 256:384], MUL),
                       [p, tk["dm"], *w3])
            give(b0, e0)
            give(b1, e1)
            yield
            b, w = take()
            fs = []
            for h in range(2):
                sl = slice(128 * (h0 + h), 128 * (h0 + h) + 128)
                fs.append(mm(b[:, 256 * h:256 * h + 256], VBB[:, 0, sl], S0[:, h, :], start=(h == 0), stop=False))
                fs.append(mm(b[:, 256 * h + 128:256 * h + 256], VBB[:, 1, sl], S1[:, h, :], start=False, stop=True))
            p = PE.op(mms(*fs), [e0, e1, *w, *tk[("vb", hp // 2)]])
            c_ = copy_out(s_, b[:, :], [p])
            give(b, c_)
            yield
            b, w = take()
            p = PE.op(mm(b[:, :], on128, s_), [c_, *w])
            x_ = DV.op(tt(s_, s_, b[:, :], SUB), [p])
            give(b, x_)
            g = GP.op(tt(t_, s_, s_, MUL), [x_])
            yield
            b, w = take()
            p = PE.op(mm(b[:, :], on128, t_), [g, *w])
            a = AC.op(act(t_, b[:, :], ACT.Sqrt, bias=eps_c), [p, t_eps])
            give(b, a)
            r = DV.op(recip(t_, t_), [a])
            for h in range(2):
                y = DV.op(stt(YBF[:, h0 + h, :], s_[:, 256 * h:256 * h + 256], col("rn", 8 * L + h0 + h),
                              t_[:, 256 * h:256 * h + 256], MUL, MUL), [r, tk["qi_read"]])
            unstage(si, y)
            unstage(sj, y)
            tk[("ybf", hp)] = y
            yield

        def g_evac(src, dst, name, sname, blk):
            def evac(ps, tok):
                f = []
                for hf in range(2):
                    hp = 2 * blk + hf
                    si, s_, w = stage()
                    sj, t_, w3 = stage()
                    a = AC.op(act(t_, ps[hf][:, :], ACT.Tanh, scale=0.5), [tok, *w3])
                    r = DV.op(stt(t_, t_, 1.0, ps[hf][:, :], ADD, MUL), [a])
                    f.append(r)
                    y = DV.op(tt(s_, src[:, 2 * hp:2 * hp + 2, :].rearrange("p a s -> p (a s)"), t_, MUL),
                              [r, tk[(sname, hp)], *w])
                    unstage(sj, y)
                    o = split_out(dst, 2 * hp, s_, [y])
                    unstage(si, o)
                    tk.setdefault((name, L), []).append(o)
                return f
            return evac

        add(WIN, 3328, 128, KT, "CM", h_ops, ki_evac, start, dup=True)
        add(WIN, 3392, 16, KT, "TM", h_ops, wi_evac)
        add(WIN, 2304, 512, KT, "CM", h_ops, qi_evac(0))
        add(WIN, 2816, 512, KT, "CM", h_ops, qi_evac(1))
        add(WIN, 1024, 128, KT, "CM", h_ops, headnorm(KA, "ka", col("kn", L), 1, 0),
            lambda: jobs.append(indexer()))
        add(WIN, 0, 512, KT, "CM", h_ops, headnorm(QA, "qa", col("qn", L), 4, 0))
        add(WIN, 512, 512, KT, "CM", h_ops, headnorm(QA, "qa", col("qn", L), 4, 1))
        add(WIN, 1152, 128, KT, "TM", h_ops, va_evac)

        def spawn(gen):
            def need():
                for g in gen:
                    jobs.append(g)
            return need

        def chain(fns):
            for f in fns:
                yield from f()

        def need_sparse():
            finish_all()
            jobs.append(chain([lambda hp=hp: sparse(hp) for hp in range(4)]))

        for blk in range(2):
            add(WIN, 3408 + 512 * blk, 512, KT, "CM", h_ops, rot(QB, "qb", blk), need_sparse if blk == 0 else None)
            add(WIN, 4432 + 512 * blk, 512, KT, "CM", h_ops, rot(KB, "kb", blk))
            add(WIN, 5456 + 512 * blk, 512, KT, "TM", h_ops, vb_evac(blk))

        def need_ret():
            finish_all()
            jobs.append(chain([lambda hp=hp: retain(hp) for hp in range(4)]))

        for blk in range(2):
            add(WIN, 1280 + 512 * blk, 512, KT, "CM", h_ops, g_evac(YAF, YA2, "y2a", "yaf", blk),
                need_ret if blk == 0 else None)
        for blk in range(2):
            add(WIN, 6480 + 512 * blk, 512, KT, "CM", h_ops, g_evac(YBF, YB2, "y2b", "ybf", blk),
                finish_all if blk == 0 else None)

        begun = [False]

        def o_ops():
            if not begun[0]:
                begun[0] = True
                state["sq"] = []
                state["gb_free"] = []
            return ((lambda k: YA2[:, k, 0, :] if k < 8 else YB2[:, k - 8, 0, :]),
                    (lambda k: YA2[:, k, 1, :] if k < 8 else YB2[:, k - 8, 1, :]),
                    tk[("y2a", L)] + tk[("y2b", L)])

        def o_evac(blk):
            def evac(ps, tok):
                f = []
                for i in range(2):
                    xs = X[:, i, 512 * blk:512 * blk + 512]
                    si, s_, w = stage()
                    e = DV.op(stt(s_, ps[i][:, :], 0.5, GB[:, 512 * blk:512 * blk + 512], MUL, MUL),
                              [tok, mod_done[(L, 8 + blk)], *w])
                    f.append(e)
                    x_ = GP.op(tt(xs, xs, s_, ADD), [e])
                    unstage(si, x_)
                    state["x"][i][blk] = x_
                    state["gb_free"] = state["gb_free"] + [e]
                    if L == 0:
                        state["sq"].append(sumsq(i, blk, [x_]))
                    else:
                        SP.dma(out[0, 128 * i:128 * i + 128, 512 * blk:512 * blk + 512], xs, s_out, [x_])
                return f
            return evac

        for blk in range(4):
            add(t["w_out_2"][L], 512 * blk, 512, KT, "TM", o_ops, o_evac(blk))

    state["gsc_free"] = []
    state["gb_free"] = []
    marks = {}
    for L in range(2):
        marks[L] = len(chunks)
        layer2(L)

    up0 = next(i for i, c in enumerate(chunks) if c[1]["need"] is ffn_need)

    def spread(items, lo, hi):
        n = len(items)
        return [(lo + (hi - lo) * (i + 1) // (n + 1), it) for i, it in enumerate(items)]

    puts = []
    puts += spread([c for b in range(8) for c in add_mod(0, b)], up0 + 8, marks[0] - 8)
    puts += spread([c for b in range(8, 12) for c in add_mod(0, b)], marks[0] + 8, marks[0] + 32)
    puts += spread([c for b in range(8) for c in add_mod(1, b)], marks[0] + 33, marks[1] - 4)
    puts += spread([c for b in range(8, 12) for c in add_mod(1, b)], marks[1] + 8, marks[1] + 50)
    by = {}
    for at, c in puts:
        by.setdefault(at, []).append(c)
    merged = []
    for i, c in enumerate(chunks):
        merged += by.get(i, [])
        merged.append(c)
    chunks[:] = merged

    for j in range(R1):
        send(j)
    at = 0
    for b in blocks:
        if b["need"] is ffn_need:
            finish_all()
        while chunks[at][1] is not b:
            ensure(at)
            at += 1
        at = run_block(b, at)
        if b["need"] is ffn_need:
            state["ffn_ready"] = state["h"][-1]
            jobs.append(bias_job())
    finish_all()
    SP.wait([(s_out.sem, s_out.n)])

    block = ctx.enter_context(nc.Block())

    @block.sync
    def _(e):
        SP.emit(e)

    @block.tensor
    def _(e):
        PE.emit(e)

    @block.scalar
    def _(e):
        AC.emit(e)

    @block.vector
    def _(e):
        DV.emit(e)

    @block.gpsimd
    def _(e):
        GP.emit(e)


_INS = ["x", "positions", "ln1", "w_in", "gdn_conv", "gdn_a_log", "gdn_dt_bias", "gdn_norm", "w_branch_a",
        "w_branch_b", "w_out", "ln2", "w_up", "ffn_conv", "ffn_conv_bias", "w_down", "final_norm", "c_2",
        "positions_2", "rel_bias_2", "norm_gain_2", "w_mod_2", "b_mod_2", "w_in_2", "q_norm_gain_2",
        "k_norm_gain_2", "ret_norm_gain_2", "w_out_2"]


def kernel(**inputs):
    import numpy as _np
    import concourse.bacc as _bacc
    from concourse import mybir as _mybir
    from concourse.bass_utils import run_bass_kernel_spmd as _run

    nc = _bacc.Bacc("TRN2", target_bir_lowering=False, num_devices=1)
    arrays, aps = {}, {}
    for name in _INS:
        a = _np.ascontiguousarray(inputs[name])
        arrays[f"in_{name}"] = a
        aps[name] = nc.dram_tensor(f"in_{name}", a.shape, _mybir.dt.from_np(a.dtype), kind="ExternalInput").ap()
    for name, a in (("cst", constants()), ("dm", decay())):
        arrays[f"in_{name}"] = a
        aps[name] = nc.dram_tensor(f"in_{name}", a.shape, _mybir.dt.from_np(a.dtype), kind="ExternalInput").ap()
    out = nc.dram_tensor("out_0", (1, 256, 2048), _mybir.dt.float32, kind="ExternalOutput").ap()
    build(nc, aps, out)
    r = _run(nc, [arrays], core_ids=[0])
    return r.results[0]["out_0"]
```

```python
import math
from contextlib import ExitStack

import concourse.bass as bass
from concourse import mybir
import numpy as np

F32 = mybir.dt.float32
BF16 = mybir.dt.bfloat16
I32 = mybir.dt.int32
ALU = mybir.AluOpType
ACT = mybir.ActivationFunctionType
AX = mybir.AxisListType.X
ADD, SUB, MUL, MAX, MIN = ALU.add, ALU.subtract, ALU.mult, ALU.max, ALU.min

D = 2048
S = 256
KT = D // 128
GW = 1024
DFF = 5632
FT = DFF // 128
EPS = 1e-6
NEG = -1e30
R1 = 3
R2 = 4
LOOK = 3
NSTG = 7
CH = 2048

ROPE1 = 16
THETA1 = 500000.0
THETA2 = 10000.0
TWO_PI = [6.25, 0.03125, 0.0019350051879882812, 3.0199159819567e-07]

C_ID, C_TRI, C_ONE, C_ON128, C_CAUS, C_GMASK, C_PERM = 0, 128, 256, 384, 512, 768, 896
C_INV1, C_INV2, C_SG1, C_SG2, C_THR, NCONST = 928, 929, 930, 931, 932, 936
C_LEV = NCONST
NLOAD = NCONST + 7 * 128


def constants():
    c = np.zeros((128, NLOAD), np.float32)
    i = np.arange(128)
    c[:, C_ID:C_ID + 128] = np.eye(128)
    c[:, C_TRI:C_TRI + 128] = i[:, None] <= i[None, :]
    c[:, C_ONE:C_ONE + 128] = 1.0
    c[:, C_ON128:C_ON128 + 128] = 1.0 / 128
    c[:, C_CAUS + 128:C_CAUS + 256] = np.where(i[None, :] <= i[:, None], 0.0, NEG)
    c[:, C_GMASK:C_GMASK + 128] = np.where(i[None, :] >= i[:, None], 0.0, NEG)
    for l in range(7):
        b = 1 << l
        same = (i[:, None] // (2 * b)) == (i[None, :] // (2 * b))
        low = (i[:, None] % (2 * b)) < b
        up = (i[None, :] % (2 * b)) >= b
        c[:, C_LEV + 128 * l:C_LEV + 128 * l + 128] = same & low & up
    for m in range(32):
        c[(m + 16) % 32, C_PERM + m] = 1.0
    h1 = np.arange(16, dtype=np.float32)
    inv1 = (np.float32(THETA1) ** (-h1 / np.float32(16))).astype(np.float32)
    c[0:16, C_INV1] = inv1
    c[16:32, C_INV1] = inv1
    c[0:16, C_SG1] = -1.0
    c[16:32, C_SG1] = 1.0
    h2 = np.arange(64, dtype=np.float32)
    inv2 = (np.float32(THETA2) ** (-h2 / np.float32(64))).astype(np.float32)
    c[0:64, C_INV2] = inv2
    c[64:128, C_INV2] = inv2
    c[0:64, C_SG2] = 1.0
    c[64:128, C_SG2] = -1.0
    c[:, C_THR] = np.tile(np.array([-4e9] + [v - 1.0 for v in thresholds()], np.float32), 4)
    return c


def decay():
    h = np.arange(8, dtype=np.float32)
    lg = np.log1p(-np.exp2(-5.0 - h)).astype(np.float32)
    j = np.arange(128)
    out = np.zeros((128, 8, 256), np.float32)
    for hh in range(8):
        d0 = np.arange(256)[None, :] - j[:, None]
        out[:, hh, 0:256] = np.where(d0 >= 0, np.exp(lg[hh] * np.maximum(d0, 0)), 0.0)
    return (out * np.float32(128.0 ** -0.5)).astype(np.float32).reshape(128, 2048)


def thresholds():
    out = list(range(1, 17))
    for b in range(17, 32):
        out.append(int(math.ceil(16.0 * 8.0 ** ((b - 16) / 16.0) - 1e-9)))
    return out


class Queue:

    def __init__(self, sem):
        self.sem, self.n, self.todo, self.seen = sem, 0, [], {}

    def wait(self, toks):
        for t in toks:
            if t is None:
                continue
            sem, v = t
            if self.seen.get(id(sem), 0) < v:
                self.seen[id(sem)] = v
                self.todo.append((0, sem, v))

    def op(self, fn, after=(), sig=True):
        self.wait(after)
        if sig:
            self.n += 1
            self.todo.append((1, fn, self.sem))
            return (self.sem, self.n)
        self.todo.append((2, fn, None))
        return None

    def dma(self, out, in_, slot, after=()):
        self.wait(after)
        slot.n += 16
        sem = slot.sem
        self.todo.append((2, lambda e: e.dma_start(out, in_).then_inc(sem, 16), None))
        return (sem, slot.n)

    def emit(self, e):
        for kind, a, b in self.todo:
            if kind == 0:
                e.wait_ge(a, b)
            elif kind == 1:
                a(e).then_inc(b, 1)
            else:
                a(e)


class Slot:
    def __init__(self, sem):
        self.sem, self.n = sem, 0


def mm(o, l, r, start=True, stop=True):
    return lambda e: e.matmul(o, l, r, start=start, stop=stop, skip_group_check=True)


def mms(*fns):
    def run(e):
        for f in fns:
            last = f(e)
        return last
    return run


def tp(o, i, ident):
    return lambda e: e.transpose(o, i, ident)


def act(o, i, f, bias=None, scale=1.0, acc=None):
    if bias is None:
        if acc is None:
            return lambda e: e.activation(o, i, f, scale=scale)
        return lambda e: e.activation(o, i, f, scale=scale, accum_out=acc)
    if acc is None:
        return lambda e: e.activation(o, i, f, bias=bias, scale=scale)
    return lambda e: e.activation(o, i, f, bias=bias, scale=scale, accum_out=acc)


def cp(o, i):
    return lambda e: e.tensor_copy(o, i)


def tt(o, a, b, op):
    return lambda e: e.tensor_tensor(o, a, b, op)


def ts(o, a, s1, op0, s2=None, op1=None):
    if op1 is None:
        return lambda e: e.tensor_scalar(o, a, s1, None, op0)
    return lambda e: e.tensor_scalar(o, a, s1, s2, op0, op1)


def stt(o, a, s, b, op0, op1):
    return lambda e: e.scalar_tensor_tensor(o, a, s, b, op0, op1)


def red(o, a, op):
    return lambda e: e.tensor_reduce(o, a, AX, op)


def recip(o, a):
    return lambda e: e.reciprocal(o, a)


def mid(a, n):
    return a.unsqueeze(1).to_broadcast([a.shape[0], n, a.shape[1]])


def rep(a, n):
    return a.unsqueeze(2).to_broadcast([a.shape[0], a.shape[1], n])


def build(nc, t, out):
    ctx = ExitStack()
    with ctx:
        program(nc, t, out, ctx)


def program(nc, t, out, ctx):
    def sb(name, shape, dt=F32):
        return ctx.enter_context(nc.sbuf_tensor(name, shape, dt))

    def sem(name):
        return ctx.enter_context(nc.semaphore(name))

    bank = [ctx.enter_context(nc.psum_tensor(f"ps{i}", [128, 512], F32)) for i in range(8)]
    PE, AC, DV, GP, SP = (Queue(sem(f"done_{n}")) for n in ("pe", "act", "dve", "pool", "sp"))

    ring = sb("ring", [128, R1, CH])
    whi = sb("whi", [128, R2, CH], BF16)
    wlo = sb("wlo", [128, R2, CH], BF16)
    X = sb("X", [128, 2, D])
    hhi = sb("hhi", [128, KT, S], BF16)
    hlo = sb("hlo", [128, KT, S], BF16)
    cst = sb("cst", [128, NCONST])
    VT = sb("VT", [128, 648])
    cs = sb("cs", [128, 2, S])
    lev = sb("lev", [128, 7, 128], BF16)
    stg = sb("stg", [128, NSTG, 512])
    sm = sb("sm", [128, 512])
    modcm = sb("modcm", [128, 2, 32])
    AR = sb("AR", [128, 22528])
    arp = [0]

    def carve(at, *shape, dt=F32):
        n = 1
        for s_ in shape:
            n *= s_
        w = (n + 1) // 2 if dt == BF16 else n
        v = AR[:, at:at + w]
        if dt != F32:
            v = v.bitcast(dt)
        if len(shape) == 1:
            return v
        names = "abcd"[:len(shape)]
        kw = {names[i]: shape[i] for i in range(1, len(shape))}
        return v.rearrange(f"p ({' '.join(names)}) -> p {' '.join(names)}", **kw)

    ident = cst[:, C_ID:C_ID + 128]
    tri = cst[:, C_TRI:C_TRI + 128]
    ones = cst[:, C_ONE:C_ONE + 128]
    on128 = cst[:, C_ON128:C_ON128 + 128]
    causal = cst[:, C_CAUS:C_CAUS + 256]
    gmask = cst[:, C_GMASK:C_GMASK + 128]

    ssq = sm[:, 0:8]
    ssf = sm[:, 352:360]
    rst = sm[:, 8:12]
    rs2 = sm[:, 360:364]
    eps_c = sm[:, 12:13]
    eps4_c = sm[:, 13:14]
    eps512_c = sm[:, 14:15]
    bd = sm[:, 16:48].rearrange("p (n c) -> p n c", n=2)
    gd = sm[:, 48:64].rearrange("p (n c) -> p n c", n=2)
    bet = sm[:, 64:80].rearrange("p (n c) -> p n c", n=2)
    gcn = sm[:, 80:96].rearrange("p (n c) -> p n c", n=2)
    eg = sm[:, 96:112].rearrange("p (n c) -> p n c", n=2)
    alog = sm[:, 112:120]
    dtb = sm[:, 120:128]
    tA = sm[:, 128:144].rearrange("p (n c) -> p n c", n=2)
    tB = sm[:, 144:160].rearrange("p (n c) -> p n c", n=2)
    c2 = sm[:, 160:176]
    wi = sm[:, 176:208].rearrange("p (n c) -> p n c", n=2)
    gsc = sm[:, 208:224]
    posc = sm[:, 224:226]
    beg = sm[:, 232:240]
    lane_sm = [sm[:, 240 + 48 * i:288 + 48 * i] for i in range(2)]
    mx8 = sm[:, 336:344]

    s_x, s_c, s_v = Slot(sem("in_x")), Slot(sem("in_const")), Slot(sem("in_vec"))
    s_row, s_out, s_dm, s_gb = Slot(sem("in_rows")), Slot(sem("out")), Slot(sem("in_decay")), [Slot(sem(f"in_gate{i}")) for i in range(2)]
    s_fn = Slot(sem("in_final_norm"))
    vst = carve(0, 6, 128)
    t_x = [SP.dma(X[:, i, :], t["x"][0, 128 * i:128 * i + 128, :], s_x) for i in range(2)][-1]
    t_cst = SP.dma(cst[:, :], t["cst"][:, 0:NCONST], s_c)
    vec = {}
    vrow = [0]

    def vload(name, src):
        n = src.shape[0]
        vec[name] = vrow[0]
        done = 0
        tok = None
        while done < n:
            r = vrow[0]
            k = min(n - done, 128 - r % 128)
            tok = AC.dma(vst[r % 128:r % 128 + k, r // 128, :], src[done:done + k, :], s_v)
            done += k
            vrow[0] += k
        return tok

    vload("ln1", t["ln1"].rearrange("a (t p) -> (a t) p", p=128))
    vload("ln2", t["ln2"].rearrange("a (t p) -> (a t) p", p=128))
    vload("conv", t["gdn_conv"].rearrange("a i (t p) -> (a i t) p", p=128))
    vload("fconv", t["ffn_conv"].rearrange("a i (t p) -> (a i t) p", p=128))
    vload("fbias", t["ffn_conv_bias"].rearrange("a (t p) -> (a t) p", p=128))
    vload("c", t["c_2"].rearrange("a (t p) -> (a t) p", p=128))
    vload("ng", t["norm_gain_2"].rearrange("a (t p) -> (a t) p", p=128))
    vload("bmod", t["b_mod_2"].rearrange("a (t p) -> (a t) p", p=128))
    vload("gn", t["gdn_norm"])
    vload("qn", t["q_norm_gain_2"])
    vload("kn", t["k_norm_gain_2"])
    t_v = vload("rn", t["ret_norm_gain_2"].rearrange("a (t p) -> (a t) p", p=128))

    def col(name, i):
        c = vec[name] + i
        return VT[:, c:c + 1]

    def cols(name, i, n):
        c = vec[name] + i
        return VT[:, c:c + n]

    pos_i = carve(1024, S, dt=I32)
    AC.dma(alog, t["gdn_a_log"].rearrange("a h -> (a h)").partition_broadcast(128), s_row)
    AC.dma(dtb, t["gdn_dt_bias"].rearrange("a h -> (a h)").partition_broadcast(128), s_row)
    levf = carve(3328, 7, 128)
    AC.dma(levf, t["cst"][:, C_LEV:NLOAD].rearrange("p (l n) -> p l n", l=7), s_row)
    t_row = AC.dma(pos_i, t["positions"].rearrange("a s -> (a s)").partition_broadcast(128), s_row)

    main = [[bank[0], bank[1]], [bank[2], bank[3]]]
    main_free = [[], []]
    bg_free = [(bank[i], []) for i in range(4, 8)]

    def take():
        assert bg_free, "no background bank"
        return bg_free.pop(0)

    def give(b, *toks):
        bg_free.append((b, list(toks)))

    stg_free = [(i, []) for i in range(NSTG)]

    def stage():
        assert stg_free, "no staging buffer"
        i, w = stg_free.pop(0)
        return i, stg[:, i, :], w

    def unstage(i, *toks):
        stg_free.append((i, list(toks)))

    t0 = DV.op(lambda e: e.memset(eps_c, EPS))
    t0 = DV.op(lambda e: e.memset(eps4_c, 4 * EPS))
    t_eps = DV.op(lambda e: e.memset(eps512_c, 512 * EPS))

    state = {"h": None, "x": [[t_x] * 4, [t_x] * 4], "sq": [], "sqf": []}

    def sumsq(i, j, after, dst=ssq):
        k, s_, w = stage()
        tk = AC.op(act(s_, X[:, i, 512 * j:512 * j + 512], ACT.Square, acc=dst[:, 4 * i + j:4 * i + j + 1]),
                   [*after, *w])
        unstage(k, tk)
        return tk

    def rstd_of(toks):
        r = DV.op(red(rst[:, 0:2], ssq.rearrange("p (i j) -> p i j", i=2), ADD), toks)
        r = AC.op(act(rst[:, 0:2], rst[:, 0:2], ACT.Sqrt, bias=eps_c, scale=1.0 / D), [r, t_eps])
        return DV.op(recip(rst[:, 2:4], rst[:, 0:2]), [r])

    def norm_to_h(scale, shift, r, after):
        dg = []
        dgt = []
        kd_, dbuf, w = stage()
        for i in range(2):
            dg.append(dbuf[:, 128 * i:128 * i + 128])
            dgt.append(DV.op(ts(dg[i], ident, rst[:, 2 + i:3 + i], MUL), [r, *w]))
        toks = []
        last_pe = None
        for k2 in range(KT // 2):
            b, w = take()
            fs = []
            for kk in range(2):
                for i in range(2):
                    k = 2 * k2 + kk
                    fs.append(mm(b[:, 256 * kk + 128 * i:256 * kk + 128 * i + 128],
                                 X[:, i, 128 * k:128 * k + 128], dg[i]))
            p = PE.op(mms(*fs), [*dgt, *w, *[x for xs in state["x"] for x in xs]])
            last_pe = p
            si, s_, w2 = stage()
            for kk in range(2):
                k = 2 * k2 + kk
                if shift is None:
                    e = DV.op(ts(s_[:, 256 * kk:256 * kk + 256], b[:, 256 * kk:256 * kk + 256], scale(k), MUL),
                              [p, *w2, *after])
                else:
                    e = DV.op(ts(s_[:, 256 * kk:256 * kk + 256], b[:, 256 * kk:256 * kk + 256], scale(k), MUL,
                                 shift(k), ADD), [p, *w2, *after])
            give(b, e)
            hv = hhi[:, 2 * k2:2 * k2 + 2, :].rearrange("p a s -> p (a s)")
            lv = hlo[:, 2 * k2:2 * k2 + 2, :].rearrange("p a s -> p (a s)")
            a = AC.op(act(hv, s_, ACT.Copy), [e])
            l = DV.op(tt(lv, s_, hv, SUB), [a])
            unstage(si, l)
            toks.append(l)
        unstage(kd_, last_pe)
        state["h"] = toks
        return last_pe

    chunks = []
    blocks = []

    def add(w, c0, n, kt, orient, lhs, evac, need=None, dup=False):
        b = dict(w=w, c0=c0, n=n, kt=kt, orient=orient, lhs=lhs, evac=evac, need=need, dup=dup)
        blocks.append(b)
        per = min(kt, CH // n)
        k = 0
        while k < kt:
            m = min(per, kt - k)
            chunks.append(("w", b, k, m))
            k += m
        return b

    slots = [Slot(sem(f"ring{i}")) for i in range(R1)]
    ring_free = [[] for _ in range(R1)]
    ring_tok = {}
    w_free = [[] for _ in range(R2)]
    w_tok = {}
    sent = [0]
    split = [0]
    wn = [0]
    wslot = {}

    def send(j):
        if j >= len(chunks):
            return
        kind, b, k, m = chunks[j]
        i = j % R1
        n = b["n"]
        dst = ring[:, i, 0:m * n].rearrange("p (k n) -> p k n", n=n)
        src = b["w"][128 * k:128 * (k + m), :].rearrange("(k p) n -> p k n", p=128)
        if b["dup"]:
            h = n // 2
            SP.dma(dst[:, :, 0:h], src[:, :, b["c0"]:b["c0"] + h], slots[i], ring_free[i])
            ring_tok[j] = SP.dma(dst[:, :, h:n], src[:, :, b["c0"]:b["c0"] + h], slots[i])
        else:
            ring_tok[j] = SP.dma(dst, src[:, :, b["c0"]:b["c0"] + n], slots[i], ring_free[i])

    short, long = [], []

    def step_jobs():
        for q, n in ((short, len(short)), (long, 2)):
            for g in q[:n]:
                try:
                    next(g)
                except StopIteration:
                    q.remove(g)

    def finish_all():
        while short or long:
            step_jobs()

    def split_chunk(j):
        kind, b, k, m = chunks[j]
        i = j % R1
        n = m * b["n"]
        if kind == "mod":
            ring_free[i] = [mod_step(b, k, m, ring[:, i, 0:n].rearrange("p (k n) -> p k n", n=b["n"]), ring_tok[j])]
        else:
            q = wn[0] % R2
            wn[0] += 1
            wslot[j] = q
            a = AC.op(act(whi[:, q, 0:n], ring[:, i, 0:n], ACT.Copy), [ring_tok[j], *w_free[q]])
            l = DV.op(tt(wlo[:, q, 0:n], ring[:, i, 0:n], whi[:, q, 0:n], SUB), [a])
            ring_free[i] = [l]
            w_free[q] = None
            w_tok[j] = l
        send(j + R1)

    def ensure(j):
        while split[0] <= min(j, len(chunks) - 1):
            split_chunk(split[0])
            split[0] += 1

    pair = [0]

    def run_block(b, j0):
        if b["need"] is not None:
            b["need"]()
        cur = pair[0] % 2
        pair[0] += 1
        ps = main[cur]
        free = main_free[cur]
        n, kt = b["n"], b["kt"]
        lhi, llo, ltok = b["lhs"]
        j = j0
        tok = None
        while True:
            ahead, q = 0, j
            while q + 1 < len(chunks) and ahead < LOOK:
                q += 1
                if chunks[q][0] == "w":
                    ahead += 1
            ensure(q)
            kind, cb, k0, m = chunks[j]
            if kind == "mod":
                j += 1
                continue
            assert cb is b
            q = wslot[j]
            wh = whi[:, q, 0:m * n].rearrange("p (k n) -> p k n", n=n)
            wl = wlo[:, q, 0:m * n].rearrange("p (k n) -> p k n", n=n)
            parts = [(0, m)] if m < 4 else [(i, min(m, i + (m + 1) // 2)) for i in range(0, m, (m + 1) // 2)]
            for pi, (ka, kb) in enumerate(parts):
                fs = []
                aft = [w_tok[j]]
                if k0 + ka == 0:
                    aft += list(free)
                for kk in range(ka, kb):
                    k = k0 + kk
                    last = k == kt - 1
                    aft += ltok(k)
                    if b["orient"] == "TM":
                        for i in range(2):
                            o = ps[i][:, 0:n]
                            a = slice(128 * i, 128 * i + 128)
                            fs.append(mm(o, lhi(k)[:, a], wh[:, kk, :], start=(k == 0), stop=False))
                            fs.append(mm(o, lhi(k)[:, a], wl[:, kk, :], start=False, stop=False))
                            fs.append(mm(o, llo(k)[:, a], wh[:, kk, :], start=False, stop=last))
                    else:
                        for ct in range(n // 128):
                            o = ps[ct // 2][:, 256 * (ct % 2):256 * (ct % 2) + 256]
                            a = slice(128 * ct, 128 * ct + 128)
                            fs.append(mm(o, wh[:, kk, a], lhi(k), start=(k == 0 and ct % 2 == 0), stop=False))
                            fs.append(mm(o, wh[:, kk, a], llo(k), start=False, stop=False))
                            fs.append(mm(o, wl[:, kk, a], lhi(k), start=False, stop=last))
                tok = PE.op(mms(*fs), aft)
                if k0 + kb < kt:
                    if pi == len(parts) - 1:
                        w_free[q] = [tok]
                    step_jobs()
            w_free[q] = [tok]
            j += 1
            if k0 + m == kt:
                break
        main_free[cur] = b["evac"](ps, tok)
        step_jobs()
        return j

    macc = sb("macc", [128, 2, 512])
    mst = {"free": [[], []], "tok": None, "c": None, "n": 0}
    mod_done = {}
    GB = carve(12288 + 3072, D)

    def add_mod(layer, blk):
        b = dict(w=t["w_mod_2"][layer], c0=512 * blk, n=512, kt=KT, dup=False, layer=layer, blk=blk)
        return [("mod", b, 4 * q, 4) for q in range(4)]

    def mod_step(b, k0, m, w, tok):
        i = mst["n"] % 2
        a = macc[:, i, :]
        last = None
        for kk in range(m):
            k = k0 + kk
            if k == 0:
                assert mst["free"][i] is not None
                last = DV.op(ts(a, w[:, 0, :], c2[:, 0:1], MUL), [tok, *mst["free"][i], mst["c"]])
                mst["free"][i] = None
            else:
                last = DV.op(stt(a, w[:, kk, :], c2[:, k:k + 1], a, MUL, ADD), [tok, mst["tok"]])
            mst["tok"] = last
        if k0 + m == KT:
            mst["n"] += 1
            short.append(mod_end(b, i, last))
        return last

    def mod_end(b, i, tok):
        L, blk = b["layer"], b["blk"]
        a = macc[:, i, :]
        for _ in range(8):
            yield
        p, w = take()
        if blk < 8:
            t_ = PE.op(mms(*[mm(p[:, j:j + 1], a[:, 128 * j:128 * j + 128], ones[:, 0:1]) for j in range(4)]),
                       [tok, *w])
            e = DV.op(tt(modcm[:, L, 4 * blk:4 * blk + 4], p[:, 0:4], cols("bmod", 48 * L + 4 * blk, 4), ADD), [t_])
        else:
            g = GB[:, 512 * (blk - 8):512 * (blk - 8) + 512]
            t_ = PE.op(mm(p[:, :], ones, a), [tok, *w])
            e = DV.op(tt(g, p[:, :], g, ADD), [t_, gate_loaded[L]])
        mst["free"][i] = [t_]
        give(p, e)
        mod_done[(L, blk)] = e

    gate_loaded = {}

    def copy_out(dst, src, after, scale=1.0):
        return AC.op(act(dst, src, ACT.Copy, scale=scale), after)

    h_ops = ((lambda k: hhi[:, k, :]), (lambda k: hlo[:, k, :]), (lambda k: [state["h"][k // 2]]))

    GQ, GK, GV = carve(0, 8, S), carve(2048, 8, S), carve(4096, 8, S)
    MQ, MK, MV = carve(6144, 8, S), carve(8192, 8, S), carve(10240, 2, GW)
    ZS = carve(12288, 2, GW)
    GBT = carve(8192, KT, S)
    YA = carve(4096, 8, 2, S, dt=BF16)
    YB = carve(6144, 8, 2, S, dt=BF16)
    MHI, MLO = carve(0, KT, S, dt=BF16), carve(2048, KT, S, dt=BF16)
    LANE = [14336, 14336 + 4096]

    tk = {}
    ROPEW = [carve(15360 + 256 * i, S) for i in range(4)]

    def rope_table(posint, inv, sgn, after, work):
        posf, a, n_, r_ = work
        q = DV.op(cp(posf, posint), after)
        q = DV.op(ts(a, posf, inv, MUL), [q, t_cst])
        q = DV.op(ts(n_, a, 1.0 / (2 * math.pi), MUL, 12582912.0, ADD), [q])
        q = DV.op(ts(n_, n_, 12582912.0, SUB), [q])
        src = a
        for c in TWO_PI:
            q = DV.op(stt(r_, n_, -c, src, MUL, ADD), [q])
            src = r_
        q0 = DV.op(ts(r_, r_, math.pi, MIN, -math.pi, MAX), [q])
        q = DV.op(ts(a, r_, math.pi / 2, ADD), [q0])
        q = DV.op(ts(n_, a, math.pi, ALU.is_gt, -2 * math.pi, MUL), [q])
        q = DV.op(tt(a, a, n_, ADD), [q])
        q = DV.op(ts(a, a, math.pi, MIN, -math.pi, MAX), [q])
        q1 = AC.op(act(cs[:, 1, :], r_, ACT.Sin), [q0])
        q = AC.op(act(cs[:, 0, :], a, ACT.Sin), [q])
        q2 = DV.op(ts(cs[:, 1, :], cs[:, 1, :], sgn, MUL), [q1])
        return [q, q2]

    sq0 = [sumsq(i, j, [t_x]) for i in range(2) for j in range(4)]
    nrow = vrow[0]
    t_vt = []
    for k in range((nrow + 127) // 128):
        r = min(128, nrow - 128 * k)
        b, w = take()
        t_ = PE.op(tp(b[:, 0:r], vst[0:r, k, :], ident[0:r, 0:r]), [t_cst, t_v, *w])
        e_ = AC.op(act(VT[:, 128 * k:128 * k + r], b[:, 0:r], ACT.Copy), [t_])
        give(b, e_)
        t_vt.append(e_)
    t_vt = t_vt[-1]
    r_ = rstd_of(sq0)
    norm_to_h(lambda k: col("ln1", k), None, r_, [t_vt])
    t_lev = AC.op(act(lev[:, :, :], levf, ACT.Copy), [t_row])
    t_rope = rope_table(pos_i, cst[:, C_INV1:C_INV1 + 1], cst[:, C_SG1:C_SG1 + 1], [t_row, t_cst],
                        [carve(1280 + 256 * i, S) for i in range(4)])
    q = AC.op(act(gsc, cols("c", 0, 16), ACT.Tanh, scale=0.5), [t_vt])
    q = DV.op(stt(c2, gsc, 1.0, cols("c", 0, 16), ADD, MUL), [q])
    mst["c"] = DV.op(ts(c2, c2, 0.5, MUL), [q])
    early = [*t_rope, t_vt, mst["c"], t_lev]

    def swap_rope(dst, blk):
        def evac(ps, tok):
            free = []
            for hf in range(2):
                si, s_, w = stage()
                e = copy_out(s_, ps[hf][:, :], [tok, *w])
                free.append(e)
                short.append(job(si, s_, e, 4 * blk + 2 * hf))
            return free

        def job(si, s_, e, h):
            sv = s_.rearrange("p (h s) -> p h s", h=2)
            d = dst[:, h:h + 2, :]
            m = DV.op(tt(d, sv, mid(cs[:, 0, :], 2), MUL), [e, *early])
            yield
            b, w = take()
            p = PE.op(mm(b[0:32, :], cst[0:32, C_PERM:C_PERM + 32], s_[0:32, :]), [e, *w])
            s2, s2_, w2 = stage()
            u = DV.op(tt(s2_[0:32, :].rearrange("p (h s) -> p h s", h=2),
                         b[0:32, :].rearrange("p (h s) -> p h s", h=2), mid(cs[0:32, 1, :], 2), MUL), [p, *w2])
            give(b, u)
            v = DV.op(tt(d[0:32, :, :], d[0:32, :, :], s2_[0:32, :].rearrange("p (h s) -> p h s", h=2), ADD), [u, m])
            unstage(si, m, p)
            unstage(s2, v)
            tk[("rope", id(dst), h // 2)] = v
            yield
        return evac

    def tm_copy(dst, c0, name, idx):
        def evac(ps, tok):
            f = [copy_out(dst[:, i, c0:c0 + 512], ps[i][:, :], [tok, *early]) for i in range(2)]
            tk[(name, idx)] = f
            return f
        return evac

    for blk in range(2):
        add(t["w_in"][0], 4112 + 512 * blk, 512, KT, "CM", h_ops, swap_rope(MQ, blk))
        add(t["w_in"][0], 5136 + 512 * blk, 512, KT, "CM", h_ops, swap_rope(MK, blk))
        add(t["w_in"][0], 6160 + 512 * blk, 512, KT, "TM", h_ops, tm_copy(MV, 512 * blk, "mv", blk))

    def softmax_rows(L0, L1, e0, e1, n, mcol, rcol, scale):
        a0 = DV.op(red(mcol[:, 0:n], L0, MAX), [e0])
        a1 = DV.op(red(mcol[:, n:2 * n], L1, MAX), [e1])
        a = DV.op(ts(mcol, mcol, -scale, MUL), [a0, a1])
        yield
        for h in range(n):
            x0 = AC.op(act(L0[:, h, :], L0[:, h, :], ACT.Exp, bias=mcol[:, h:h + 1], scale=scale,
                           acc=rcol[:, h:h + 1]), [a])
            x1 = AC.op(act(L1[:, h, :], L1[:, h, :], ACT.Exp, bias=mcol[:, n + h:n + h + 1], scale=scale,
                           acc=rcol[:, n + h:n + h + 1]), [a])
        yield
        r = DV.op(recip(rcol, rcol), [x1])
        n0 = GP.op(tt(L0, L0, rep(rcol[:, 0:n], 128), MUL), [r])
        n1 = DV.op(tt(L1, L1, rep(rcol[:, n:2 * n], 256), MUL), [r])
        return n0, n1

    lane_free = [[], []]

    def split_out(dst, h, src, after):
        sv = src.rearrange("p (h s) -> p h s", h=2)
        a = AC.op(act(dst[:, h:h + 2, 0, :], sv, ACT.Copy), after)
        yield
        return DV.op(tt(dst[:, h:h + 2, 1, :], sv, dst[:, h:h + 2, 0, :], SUB), [a])

    def attend_pv(L0, L1, n0, n1, v0, v1, lane, base):
        b0, w0 = take()
        b1, w1 = take()
        PT0, PT1 = carve(base + 1024, 2, 256), carve(base + 1536, 2, 128)
        fs = []
        for h in range(2):
            fs.append(tp(b0[:, 256 * h:256 * h + 128], L0[:, h, :], ident))
            fs.append(tp(b0[:, 256 * h + 128:256 * h + 256], L1[:, h, 0:128], ident))
            fs.append(tp(b1[:, 128 * h:128 * h + 128], L1[:, h, 128:256], ident))
        p = PE.op(mms(*fs), [n0, n1, *w0, *w1])
        c0 = copy_out(PT0, b0[:, :].rearrange("p (h s) -> p h s", h=2), [p, *lane_free[lane]])
        c1 = copy_out(PT1, b1[:, 0:256].rearrange("p (h s) -> p h s", h=2), [p])
        give(b0, c0)
        give(b1, c1)
        return PT0, PT1, p, [c0, c1]

    def moba(hp):
        lane = hp % 2
        base = LANE[lane]
        h0 = 2 * hp
        L0, L1 = carve(base, 2, 128), carve(base + 256, 2, 256)
        sml = lane_sm[lane]
        mcol, rcol = sml[:, 0:4], sml[:, 4:8]
        b0, w0 = take()
        b1, w1 = take()
        fs = []
        for h in range(2):
            fs.append(mm(b0[:, 128 * h:128 * h + 128], MQ[:, h0 + h, 0:128], MK[:, h0 + h, 0:128]))
            fs.append(mm(b1[:, 256 * h:256 * h + 256], MQ[:, h0 + h, 128:256], MK[:, h0 + h, :]))
        p = PE.op(mms(*fs), [tk[("rope", id(MQ), hp)], tk[("rope", id(MK), hp)], *w0, *w1])
        e0 = DV.op(tt(L0, b0[:, 0:256].rearrange("p (h s) -> p h s", h=2), mid(causal[:, 128:256], 2), ADD),
                   [p, *lane_free[lane]])
        e1 = DV.op(tt(L1, b1[:, :].rearrange("p (h s) -> p h s", h=2), mid(causal, 2), ADD), [p, *lane_free[lane]])
        give(b0, e0)
        give(b1, e1)
        yield
        n0, n1 = yield from softmax_rows(L0, L1, e0, e1, 2, mcol, rcol, 128.0 ** -0.5)
        yield
        PT0, PT1, pt, cc = attend_pv(L0, L1, n0, n1, None, None, lane, base)
        yield
        b, w = take()
        fs = []
        for h in range(2):
            sl = slice(128 * (h0 + h), 128 * (h0 + h) + 128)
            fs.append(mm(b[:, 256 * h:256 * h + 256], MV[:, 0, sl], PT0[:, h, :], start=(h == 0), stop=False))
            fs.append(mm(b[:, 256 * h + 128:256 * h + 256], MV[:, 1, sl], PT1[:, h, :], start=False, stop=True))
        p = PE.op(mms(*fs), [*cc, *w, *tk[("mv", h0 // 4)]])
        si, s_, w = stage()
        e = copy_out(s_, b[:, :], [p, *w])
        give(b, e)
        o = yield from split_out(YB, h0, s_, [e])
        unstage(si, o)
        lane_free[lane] = [p]
        tk[("yb", hp)] = o
        tk[("moba_read", hp)] = [p]
        yield

    def conv_block(kind, blk):
        dst = {"q": GQ, "k": GK, "v": GV}[kind]
        ch0 = {"q": 0, "k": 8, "v": 16}[kind]

        def evac(ps, tok):
            free = []
            for hf in range(2):
                si, s_, w = stage()
                e = copy_out(s_, ps[hf][:, :], [tok, *w])
                free.append(e)
                short.append(job(si, s_, e, 4 * blk + 2 * hf))
            return free

        def job(si, s_, e, h):
            d = dst[:, h:h + 2, :]
            for q_ in range(2):
                x_ = s_[:, 256 * q_:256 * q_ + 256]
                y_ = d[:, q_, :]
                wt = lambda i: col("conv", 24 * i + ch0 + h + q_)
                c_ = DV.op(ts(y_, x_, wt(3), MUL), [e, *early])
                for i in range(3):
                    sh = 3 - i
                    c_ = DV.op(stt(y_[:, sh:S], x_[:, 0:S - sh], wt(i), y_[:, sh:S], MUL, ADD), [c_])
            unstage(si, c_)
            yield
            dv = d.rearrange("p h s -> p (h s)")
            s2, s2_, w2 = stage()
            a = AC.op(act(s2_, dv, ACT.Tanh, scale=0.5), [c_, *w2])
            yield
            f = DV.op(stt(dv, s2_, 1.0, dv, ADD, MUL), [a])
            if kind == "v":
                unstage(s2, f)
                tk[("gv", h // 2)] = f
                return
            g = GP.op(tt(s2_, dv, dv, MUL), [f])
            yield
            b, w = take()
            p = PE.op(mm(b[:, :], ones, s2_), [g, *w])
            if kind == "q":
                a = AC.op(act(s2_, b[:, :], ACT.Sqrt, bias=eps512_c, scale=128.0), [p, t_eps])
            else:
                a = AC.op(act(s2_, b[:, :], ACT.Sqrt, bias=eps4_c, scale=1.0), [p, t_eps])
            give(b, a)
            yield
            r = DV.op(recip(s2_, s2_), [a])
            m = GP.op(tt(dv, dv, s2_, MUL), [r])
            unstage(s2, m)
            tk[("g" + kind, h // 2)] = m
        return evac

    def evac_bd(ps, tok):
        es = [copy_out(bd[:, i, :], ps[i][:, 0:16], [tok]) for i in range(2)]
        short.append(job_bd(es))
        return es

    def job_bd(es):
        a = AC.op(act(bet, bd[:, :, 0:8], ACT.Tanh, scale=0.5), es)
        tk["bet"] = DV.op(ts(bet, bet, 1.0, ADD, 0.5, MUL), [a])
        z = DV.op(tt(tA, bd[:, :, 8:16], mid(dtb, 2), ADD), [*es, t_row])
        n_ = DV.op(ts(tB, tA, -1.0, MUL), [z])
        n_ = DV.op(tt(tB, tB, tA, MAX), [n_])
        n_ = AC.op(act(tB, tB, ACT.Exp, scale=-1.0), [n_])
        n_ = AC.op(act(tB, tB, ACT.Ln, bias=ones[:, 0:1]), [n_, t_cst])
        z = DV.op(ts(tA, tA, 0.0, MAX), [z, n_])
        z = DV.op(tt(tA, tA, tB, ADD), [z])
        ea = AC.op(act(alog, alog, ACT.Exp), [t_row])
        g = DV.op(stt(gd, tA, -1.0, mid(alog, 2), MUL, MUL), [z, ea])
        tk["g"] = g
        yield
        b, w = take()
        p = PE.op(mm(b[:, 0:16], tri, gd.rearrange("p n c -> p (n c)")), [g, *w])
        v = DV.op(ts(gcn, b[:, 0:16].rearrange("p (n c) -> p n c", n=2), -1.0, MUL), [p])
        give(b, v)
        x_ = AC.op(act(eg, gcn, ACT.Exp, scale=-1.0), [v])
        tk["gcn"] = v
        tk["eg"] = x_
        tk["beg"] = DV.op(tt(beg, bet[:, 1, :], eg[:, 1, :], MUL), [x_, tk["bet"]])
        yield

    def gdn(bt):
        lane = bt % 2
        base = LANE[lane]
        h0 = 2 * bt
        GM, AT, XT, XX, PP, AL, QK, VB = (carve(base + 512 * i, 4, 128) for i in range(8))
        KX = GM
        sml = lane_sm[lane]
        gl, ekd, oss, orr = sml[:, 0:2], sml[:, 2:4], sml[:, 4:8], sml[:, 8:12]
        U = [(u, h0 + u // 2, u % 2, slice(128 * (u % 2), 128 * (u % 2) + 128)) for u in range(4)]
        fl = lambda a: a.rearrange("p a b -> p (a b)")
        lw = lane_free[lane]
        B = lambda b, u: b[:, 128 * u:128 * u + 128]
        b1, w1 = take()
        b2, w2 = take()
        p1 = PE.op(mms(*[mm(B(b1, u), gd[:, n, h:h + 1].to_broadcast([128, 128]), tri) for u, h, n, c in U]),
                   [tk["g"], *w1])
        p2 = PE.op(mms(*[mm(B(b2, u), bet[:, n, h:h + 1].to_broadcast([128, 128]), ident) for u, h, n, c in U]),
                   [tk["bet"], *w2])
        for u, h, n, c in U:
            m = DV.op(stt(GM[:, u, :], B(b1, u), gcn[:, n, h:h + 1], gmask, ADD, ADD), [p1, tk["gcn"], *lw])
        gl_t = DV.op(cp(gl, b1[:, :].rearrange("p (a b) -> p a b", a=4)[:, 0:4:2, 127]), [p1])
        br = copy_out(fl(PP), b2[:, :], [p2, *lw])
        give(b1, gl_t)
        give(b2, br)
        yield
        ex = AC.op(act(fl(GM), fl(GM), ACT.Exp), [m])
        for q_ in range(2):
            ek = AC.op(act(ekd[:, q_:q_ + 1], gcn[:, 0, h0 + q_:h0 + q_ + 1], ACT.Exp, bias=gl[:, q_:q_ + 1]), [gl_t])
        yield
        b1, w1 = take()
        b2, w2 = take()
        p1 = PE.op(mms(*[mm(B(b1, u), GK[:, h, c], GK[:, h, c]) for u, h, n, c in U]), [tk[("gk", bt)], *w1])
        p2 = PE.op(mms(*[mm(B(b2, u), GK[:, h, c], GQ[:, h, c]) for u, h, n, c in U]), [tk[("gq", bt)], *w2])
        a = DV.op(tt(fl(AT), b1[:, :], fl(GM), MUL), [p1, ex, *lw])
        qk = DV.op(tt(fl(QK), b2[:, :], fl(GM), MUL), [p2, ex, *lw])
        at = GP.op(tt(fl(AT), fl(AT), fl(PP), MUL), [a, br])
        al = GP.op(tt(AL, AT, mid(lev[:, 0, :], 4), MUL), [at, *early, *lw])
        give(b1, a)
        give(b2, qk)
        yield
        b1, w1 = take()
        b2, w2 = take()
        p1 = PE.op(mms(*[tp(B(b1, u), GV[:, h, c], ident) for u, h, n, c in U]), [tk[("gv", bt)], *w1])
        p2 = PE.op(mms(*[tp(B(b2, u), GK[:, h, c], ident) for u, h, n, c in U]), w2)
        for u, h, n, c in U:
            vb = DV.op(ts(VB[:, u, :], B(b1, u), bet[:, n, h:h + 1], MUL, 0.5, MUL), [p1, tk["bet"], *lw])
            sc = ekd[:, u // 2:u // 2 + 1] if n == 0 else beg[:, h:h + 1]
            kx = DV.op(ts(KX[:, u, :], B(b2, u), sc, MUL), [p2, ek, qk, a, tk["beg"]])
        give(b1, vb)
        give(b2, kx)
        xt = DV.op(tt(XT, mid(ident, 4), AL, SUB), [al, *lw])
        al_free = xt
        yield
        al = GP.op(tt(AL, AT, mid(lev[:, 1, :], 4), MUL), [al_free])
        b1, w1 = take()
        p1 = PE.op(mms(*[tp(B(b1, u), XT[:, u, :], ident) for u in range(4)]), [xt, *w1])
        xx = copy_out(fl(XX), b1[:, :], [p1, *lw])
        give(b1, xx)
        pz = None
        for l in range(1, 7):
            yield
            b1, w1 = take()
            p1 = PE.op(mms(*[mm(B(b1, u), AL[:, u, :], XX[:, u, :]) for u in range(4)]), [al, xx, *w1])
            pp = copy_out(fl(PP), b1[:, :], [p1, at, pz])
            give(b1, pp)
            if l < 6:
                al = GP.op(tt(AL, AT, mid(lev[:, l + 1, :], 4), MUL), [p1])
            else:
                al = p1
            yield
            b1, w1 = take()
            p1 = PE.op(mms(*[mm(B(b1, u), PP[:, u, :], XT[:, u, :]) for u in range(4)]), [pp, xt, *w1])
            pz = p1
            if l < 6:
                b2, w2 = take()
                pz = PE.op(mms(*[mm(B(b2, u), XT[:, u, :], PP[:, u, :]) for u in range(4)]), w2)
            xt = DV.op(tt(fl(XT), fl(XT), b1[:, :], SUB), [p1, pz])
            give(b1, xt)
            if l < 6:
                xx = DV.op(tt(fl(XX), fl(XX), b2[:, :], SUB), [pz])
                give(b2, xx)
        yield
        VN, WT, SS, QS = AT, XX, AL, PP
        b1, w1 = take()
        b2, w2 = take()
        p1 = PE.op(mms(*[mm(B(b1, u), XT[:, u, :], VB[:, u, :]) for u in range(4)]), [xt, vb, *w1])
        p2 = PE.op(mms(*[mm(B(b2, q_), KX[:, 2 * q_ + 1, :], XT[:, 2 * q_ + 1, :]) for q_ in range(2)]), [kx, *w2])
        vn = copy_out(fl(VN), b1[:, :], [p1, al])
        wt = copy_out(fl(WT)[:, 0:256], b2[:, 0:256], [p2])
        give(b1, vn)
        give(b2, wt)
        yield
        b1, w1 = take()
        p1 = PE.op(mms(*[mm(B(b1, q_), KX[:, 2 * q_, :], VN[:, 2 * q_, :]) for q_ in range(2)]), [vn, *w1])
        ss = copy_out(fl(SS)[:, 0:256], b1[:, 0:256], [p1, al])
        give(b1, ss)
        yield
        b1, w1 = take()
        b2, w2 = take()
        p2 = PE.op(mms(*[mm(B(b2, q_), WT[:, q_, :], SS[:, q_, :]) for q_ in range(2)]), [wt, ss, *w2])
        p1 = PE.op(mms(*[mm(B(b1, q_), GQ[:, h0 + q_, 128:256], SS[:, q_, :]) for q_ in range(2)]), w1)
        for q_ in range(2):
            v1 = DV.op(tt(VN[:, 2 * q_ + 1, :], VN[:, 2 * q_ + 1, :], B(b2, q_), SUB), [p2, vn])
            qs = AC.op(act(QS[:, q_, :], B(b1, q_), ACT.Copy, scale=eg[:, 1, h0 + q_:h0 + q_ + 1]), [p1, tk["eg"]])
        give(b1, qs)
        give(b2, v1)
        yield
        b2, w2 = take()
        p2 = PE.op(mms(*[mm(B(b2, u), QK[:, u, :], VN[:, u, :]) for u in range(4)]), [v1, *w2])
        O = XT
        o4 = b2[:, :].rearrange("p (h n d) -> p h n d", h=2, n=2)
        Ov = O.rearrange("p (h n) d -> p h n d", h=2)
        o0 = DV.op(cp(Ov[:, :, 0, :], o4[:, :, 0, :]), [p2])
        o1 = DV.op(tt(Ov[:, :, 1, :], o4[:, :, 1, :], QS[:, 0:2, :], ADD), [p2, qs])
        give(b2, o1)
        sq = GP.op(tt(fl(VB), fl(O), fl(O), MUL), [o0, o1])
        yield
        r = DV.op(red(oss, VB, ADD), [sq])
        yield
        r = AC.op(act(orr, oss, ACT.Sqrt, bias=eps_c, scale=1.0 / 128), [r, t_eps])
        yield
        r = DV.op(recip(orr, orr), [r])
        for u, h, n, c in U:
            og = DV.op(stt(O[:, u, :], O[:, u, :], orr[:, u:u + 1], ZS[:, n, 128 * h:128 * h + 128], MUL, MUL),
                       [r, sq, *tk[("zs", h // 4)]])
        yield
        b1, w1 = take()
        p1 = PE.op(mms(*[tp(B(b1, u), O[:, u, :], ident) for u in range(4)]), [og, *w1])
        si, s_, w = stage()
        e = DV.op(ts(s_, b1[:, :], col("gn", 0), MUL, 0.5, MUL), [p1, *w])
        give(b1, e)
        yield
        o = yield from split_out(YA, h0, s_, [e])
        unstage(si, o)
        lane_free[lane] = [p1, o]
        tk[("ya", bt)] = o

    def z_evac(blk):
        def evac(ps, tok):
            f = []
            for i in range(2):
                si, s_, w = stage()
                e = copy_out(s_, ps[i][:, :], [tok, *w])
                f.append(e)
                short.append(job(si, s_, e, i))
            return f

        def job(si, s_, e, i):
            z_ = ZS[:, i, 512 * blk:512 * blk + 512]
            a = AC.op(act(z_, s_, ACT.Tanh, scale=0.5), [e, *early])
            r = DV.op(stt(z_, z_, 1.0, s_, ADD, MUL), [a])
            unstage(si, r)
            tk.setdefault(("zs", blk), []).append(r)
            yield
        return evac

    def launch(*gens):
        return lambda: long.extend(gens)

    def qkv(blk, need):
        for kind, c0 in (("q", 0), ("k", 1024), ("v", 2048)):
            add(t["w_in"][0], c0 + 512 * blk, 512, KT, "CM", h_ops, conv_block(kind, blk), need)
            need = None

    add(t["w_in"][0], 3072, 16, KT, "TM", h_ops, evac_bd, launch(moba(0), moba(1), moba(2), moba(3)))
    qkv(0, None)
    for blk in range(2):
        add(t["w_in"][0], 3088 + 512 * blk, 512, KT, "TM", h_ops, z_evac(blk), launch(gdn(0), gdn(1)) if blk else None)
    qkv(1, None)

    def gb_evac(blk):
        def evac(ps, tok):
            f = []
            for hf in range(2):
                f.append(AC.op(act(GBT[:, 4 * blk + 2 * hf:4 * blk + 2 * hf + 2, :].rearrange("p a s -> p (a s)"),
                                   ps[hf][:, :], ACT.Tanh, scale=0.5), [tok, *[x for hp in range(4)
                                                                            for x in tk[("moba_read", hp)]]]))
            tk[("gb", blk)] = f
            return f
        return evac

    for blk in range(4):
        add(t["w_in"][0], 9232 + 512 * blk, 512, KT, "CM", h_ops, gb_evac(blk),
            launch(gdn(2), gdn(3)) if blk == 1 else None)

    merge = {}

    def ga_evac(blk):
        def evac(ps, tok):
            f = []
            for hf in range(2):
                si, s_, w = stage()
                e = AC.op(act(s_, ps[hf][:, :], ACT.Tanh, scale=0.5), [tok, *w])
                f.append(e)
                merge[(blk, hf)] = (si, s_, e)
            return f
        return evac

    def ya_evac(blk):
        def evac(ps, tok):
            f = []
            for hf in range(2):
                si, s_, e = merge[(blk, hf)]
                m = DV.op(stt(s_, s_, 1.0, ps[hf][:, :], ADD, MUL), [tok, e])
                merge[(blk, hf)] = (si, s_, m)
                f.append(m)
            return f
        return evac

    def yb_evac(blk):
        def evac(ps, tok):
            f = []
            for hf in range(2):
                si, s_, m = merge[(blk, hf)]
                k = 4 * blk + 2 * hf
                g = GBT[:, k:k + 2, :].rearrange("p a s -> p (a s)")
                y = DV.op(stt(g, g, 1.0, ps[hf][:, :], ADD, MUL), [tok, *tk[("gb", blk)]])
                f.append(y)
                short.append(job(si, s_, GP.op(tt(s_, s_, g, ADD), [y, m]), k))
            return f

        def job(si, s_, y, k):
            hv, lv = (v[:, k:k + 2, :].rearrange("p a s -> p (a s)") for v in (MHI, MLO))
            yield
            a = AC.op(act(hv, s_, ACT.Copy), [y])
            yield
            l = DV.op(tt(lv, s_, hv, SUB), [a])
            unstage(si, l)
            tk[("merged", k // 2)] = l
        return evac

    def y_ops(Y, name):
        return (lambda k: Y[:, k, 0, :]), (lambda k: Y[:, k, 1, :]), (lambda k: [tk[(name, k // 2)]])

    for blk in range(4):
        add(t["w_in"][0], 7184 + 512 * blk, 512, KT, "CM", h_ops, ga_evac(blk))
        add(t["w_branch_a"][0], 512 * blk, 512, 8, "CM", y_ops(YA, "ya"), ya_evac(blk),
            finish_all if blk == 0 else None)
        add(t["w_branch_b"][0], 512 * blk, 512, 8, "CM", y_ops(YB, "yb"), yb_evac(blk))

    def resid(blk, half):
        def evac(ps, tok):
            f = []
            for i in range(2):
                xs = X[:, i, 512 * blk:512 * blk + 512]
                e = DV.op(stt(xs, ps[i][:, :], half, xs, MUL, ADD), [tok])
                f.append(e)
                state["x"][i][blk] = e
                state["sq"].append(sumsq(i, blk, [e]))
            return f
        return evac

    m_ops = ((lambda k: MHI[:, k, :]), (lambda k: MLO[:, k, :]), (lambda k: [tk[("merged", k // 2)]]))

    def clear_sq():
        state["sq"] = []

    for blk in range(4):
        add(t["w_out"][0], 512 * blk, 512, KT, "TM", m_ops, resid(blk, 0.5), clear_sq if blk == 0 else None)

    AHI, ALO = carve(0, FT, S, dt=BF16), carve(5632, FT, S, dt=BF16)
    SG = carve(11264, 4, S)
    B0, B1 = carve(12288, 8, 128), carve(13312, 8, 256)

    def ffn_need():
        norm_to_h(lambda k: col("ln2", k), None, rstd_of(state["sq"]), [t_vt])
        long.append(bias_job([state["h"][-1]]))
        long.append(rope2_job([state["h"][-1]]))

    fst = {"sg": [], "sgr": [], "uv": []}

    def up_evac(val, j):
        def evac(ps, tok):
            f = []
            for hf in range(2):
                si, s_, w = stage()
                e = copy_out(s_, ps[hf][:, :], [tok, *w])
                f.append(e)
                short.append(job(si, s_, e, hf))
            return f

        def job(si, s_, e, hf):
            s2, s2_, w2 = stage()
            dst = s2_
            for q_ in range(2):
                ch = (FT if val else 0) + 4 * j + 2 * hf + q_
                x_ = s_[:, 256 * q_:256 * q_ + 256]
                y_ = dst[:, 256 * q_:256 * q_ + 256]
                wt = lambda i: col("fconv", 88 * i + ch)
                c_ = DV.op(ts(y_, x_, wt(2), MUL, col("fbias", ch), ADD), [e, *w2])
                for i in range(2):
                    sh = 2 - i
                    c_ = DV.op(stt(y_[:, sh:S], x_[:, 0:S - sh], wt(i), y_[:, sh:S], MUL, ADD), [c_])
            g = SG[:, 2 * hf:2 * hf + 2, :].rearrange("p a s -> p (a s)")
            if not val:
                yield
                a = AC.op(act(s_, dst, ACT.Tanh, scale=0.5), [c_])
                yield
                r = DV.op(stt(g, s_, 1.0, dst, ADD, MUL), [a, fst.get(("free", hf))])
                fst[("sg", hf)] = r
                unstage(si, r)
                unstage(s2, r)
            else:
                unstage(si, c_)
                r = GP.op(tt(s2_, s2_, g, MUL), [c_, fst[("sg", hf)]])
                fst[("free", hf)] = r
                k = 4 * j + 2 * hf
                hv, lv = (v[:, k:k + 2, :].rearrange("p a s -> p (a s)") for v in (AHI, ALO))
                yield
                a = AC.op(act(hv, s2_, ACT.Copy), [r])
                yield
                l = DV.op(tt(lv, s2_, hv, SUB), [a])
                unstage(s2, l)
                tk[("act", k // 2)] = l
        return evac

    for j in range(11):
        add(t["w_up"][0], 512 * j, 512, KT, "CM", h_ops, up_evac(False, j), ffn_need if j == 0 else None)
        add(t["w_up"][0], DFF + 512 * j, 512, KT, "CM", h_ops, up_evac(True, j))

    a_ops = ((lambda k: AHI[:, k, :]), (lambda k: ALO[:, k, :]), (lambda k: [tk[("act", k // 2)]]))

    def down_evac(blk):
        def evac(ps, tok):
            f = []
            for i in range(2):
                xs = X[:, i, 512 * blk:512 * blk + 512]
                e = DV.op(stt(xs, ps[i][:, :], 0.5, xs, MUL, ADD), [tok])
                f.append(e)
                q = sumsq(i, blk, [e])
                state["sq"].append(q)
                x_ = DV.op(tt(xs, xs, GB[:, 512 * blk:512 * blk + 512], MUL), [q, fn_tok[0]])
                state["x"][i][blk] = x_
                state["sqf"].append(sumsq(i, blk, [x_], ssf))
            return f
        return evac

    fn_tok = [None]

    def down_need():
        state["sq"] = []
        fn_tok[0] = SP.dma(GB, t["final_norm"].partition_broadcast(128), s_fn, [state["h"][-1]])

    for blk in range(4):
        add(t["w_down"][0], 512 * blk, 512, FT, "TM", a_ops, down_evac(blk), down_need if blk == 0 else None)

    REL = carve(17408, 16, 128, dt=I32)
    STEP = carve(19456, 16, 128)
    PQR = carve(21504, S, dt=I32)
    PKC = carve(21760, 64, dt=I32)
    RBP, RBM = carve(21824, 8), carve(21832, 8)
    RBW = carve(21840, 4, 8)
    s_rb = Slot(sem("in_bias"))

    def bias_job(after):
        z = GP.op(lambda e: e.memset(RBM, 0.0), after)
        z = GP.op(lambda e: e.memset(RBW, 0.0), after)
        pos2 = t["positions_2"].rearrange("a s -> (a s)")
        SP.dma(PQR, pos2.partition_broadcast(128), s_rb, [z])
        for g in range(4):
            pp = slice(32 * g, 32 * g + 32)
            SP.dma(RBP[pp, :], t["rel_bias_2"], s_rb)
            SP.dma(RBM[32 * g + 1:32 * g + 32, :], t["rel_bias_2"][0:31, :], s_rb)
            for kb in range(2):
                r = SP.dma(PKC[pp, 32 * kb:32 * kb + 32],
                           pos2[128 * kb + 32 * g:128 * kb + 32 * g + 32].partition_broadcast(32), s_rb)
        for _ in range(6):
            yield
        d = DV.op(tt(RBP, RBP, RBM, SUB), [r])
        q = DV.op(lambda e: e.tensor_single_scalar(PKC, PKC, -1, ALU.bitwise_xor), [r])
        for g in range(4):
            pp = slice(32 * g, 32 * g + 32)
            w_ = DV.op(cp(RBW[pp, g, :], RBP[pp, :]), [d, z])
        rbw = RBW.rearrange("p g h -> p (g h)")
        pm = m = None
        ends = []
        for qt, kb in ((0, 0), (1, 0), (1, 1)):
            for jh in range(2):
                a = GP.op(tt(REL, mid(PQR[:, 128 * qt:128 * qt + 128], 16),
                             rep(PKC[:, 32 * kb + 16 * jh:32 * kb + 16 * jh + 16], 128), ADD), [q, r, m])
                yield
                yield
                m = DV.op(ts(STEP, REL, cst[:, C_THR:C_THR + 1], ALU.is_ge), [a, pm])
                yield
                b, w = take()
                pm = PE.op(mms(*[mm(b[:, 32 * j:32 * j + 32], STEP[:, j, :], rbw) for j in range(16)]), [m, w_, *w])
                dst = B0 if qt == 0 else B1
                c0 = 128 * kb + 16 * jh
                for g in range(4):
                    e = AC.op(act(dst[:, :, c0 + 32 * g:c0 + 32 * g + 16],
                                  b[:, :].rearrange("p (j g h) -> p g h j", g=4, h=8)[:, g, :, :], ACT.Copy), [pm])
                give(b, e)
                ends.append(e)
                yield
        tk["bias"] = ends

    def rope2_job(after):
        tk["rope2"] = rope_table(PQR, cst[:, C_INV2:C_INV2 + 1], cst[:, C_SG2:C_SG2 + 1],
                                 [(s_rb.sem, s_rb.n), *after], ROPEW)
        yield

    QA, KA, VA = carve(0, 8, S), carve(2048, S), carve(2304, 2, 128)
    KI, QI = carve(2560, S), carve(2816, 8, S)
    QB, KB, VBB = carve(4864, 8, S), carve(6912, 8, S), carve(8960, 2, GW)
    YA2 = carve(0, 8, 2, S, dt=BF16)
    YB2 = carve(2816, 8, 2, S, dt=BF16)
    YAF, YBF = QA, QI
    MN0, MN1 = carve(11008, 128), carve(11136, S)
    IW = carve(11392, 2, S)
    IT = carve(11904, 384)
    DM = carve(17408, 8, 256)
    W2 = 17408 + 2048

    def layer2(L):
        dm = {}
        WIN = t["w_in_2"][L]

        def start():
            r = rstd_of(state["sq"])
            if L == 0:
                q = DV.op(red(rs2[:, 0:2], ssf.rearrange("p (i j) -> p i j", i=2), ADD), state["sqf"])
                q = DV.op(tt(rs2[:, 0:2], rs2[:, 0:2], rst[:, 2:4], MUL), [q, r])
                q = DV.op(tt(rs2[:, 0:2], rs2[:, 0:2], rst[:, 2:4], MUL), [q])
                q = AC.op(act(rs2[:, 0:2], rs2[:, 0:2], ACT.Sqrt, bias=eps_c, scale=1.0 / D), [q])
                q = DV.op(recip(rs2[:, 2:4], rs2[:, 0:2]), [q])
                r1 = DV.op(cp(rs2[:, 0:2], rst[:, 2:4]), [q])
                r = DV.op(tt(rst[:, 2:4], rst[:, 2:4], rs2[:, 2:4], MUL), [q, r1])
                tk["dm"] = SP.dma(DM, t["dm"].rearrange("p (h s) -> p h s", h=8), s_dm, tk["bias"] + tk["rope2"])
            g = DV.op(stt(gsc, modcm[:, L, 16:32], 1.0, cols("ng", 16 * L, 16), ADD, MUL),
                      [mod_done[(L, b)] for b in range(8)] + state["gsc_free"])
            pe = norm_to_h(lambda k: gsc[:, k:k + 1], lambda k: modcm[:, L, k:k + 1], r, [g])
            state["gsc_free"] = [state["h"][-1]]
            gate_loaded[L] = SP.dma(GB, t["b_mod_2"][L, 4096:6144].partition_broadcast(128), s_gb[L],
                                    state["gb_free"] + [state["h"][-1]])
            ready[0] = [state["h"][-1]]
            if L == 0:
                short.append(scale_x(pe, r1))

        def scale_x(pe, r1):
            for i in range(2):
                for j in range(4):
                    xs = X[:, i, 512 * j:512 * j + 512]
                    state["x"][i][j] = DV.op(ts(xs, xs, rs2[:, i:i + 1], MUL), [pe, r1])
                    yield

        ready = [[]]

        def ki_evac(ps, tok):
            e = copy_out(KI, ps[0][:, 0:256], [tok, *ready[0]])
            tk["ki"] = e
            return [e]

        def wi_evac(ps, tok):
            e = [copy_out(wi[:, i, :], ps[i][:, 0:16], [tok]) for i in range(2)]
            tk["wi"] = e
            return e

        def qi_evac(blk):
            def evac(ps, tok):
                f = [copy_out(QI[:, 4 * blk + 2 * hf:4 * blk + 2 * hf + 2, :].rearrange("p a s -> p (a s)"),
                              ps[hf][:, :], [tok, *ready[0]]) for hf in range(2)]
                tk[("qi", blk)] = f
                return f
            return evac

        def indexer():
            a0 = carve(W2, 2, 128)
            a1 = carve(W2 + 256, 2, 256)
            g0 = g1 = None
            for ti in range(8):
                b0, w0 = take()
                b1, w1 = take()
                fs = []
                for hh, bk in ((0, b0), (1, b1)):
                    pp = slice(64 * hh, 64 * hh + 64)
                    fs.append(mm(bk[:, 0:128], QI[pp, ti, 0:128], KI[pp, 0:128]))
                    fs.append(mm(bk[:, 128:384], QI[pp, ti, 128:256], KI[pp, :]))
                p = PE.op(mms(*fs), [*tk[("qi", ti // 4)], tk["ki"], *w0, *w1])
                if ti == 0:
                    x0, x1, w = a0, a1, [*lane_free[0], *lane_free[1]]
                else:
                    si, s_, w = stage()
                    sj, t_, w3 = stage()
                    x0 = s_[:, 0:256].rearrange("p (h s) -> p h s", h=2)
                    x1 = t_.rearrange("p (h s) -> p h s", h=2)
                    w = [*w, *w3]
                ev = []
                for hh, bk in ((0, b0), (1, b1)):
                    DV.op(ts(x0[:, hh, :], bk[:, 0:128], 0.0, MAX, wi[:, 0, 2 * ti + hh:2 * ti + hh + 1], MUL),
                          [p, *tk["wi"], *w])
                    ev.append(DV.op(ts(x1[:, hh, :], bk[:, 128:384], 0.0, MAX,
                                       wi[:, 1, 2 * ti + hh:2 * ti + hh + 1], MUL), [p]))
                e0, e1 = ev
                if ti == 0:
                    g0 = g1 = e1
                else:
                    g0 = GP.op(tt(a0, a0, x0, ADD), [e1, g0])
                    g1 = GP.op(tt(a1, a1, x1, ADD), [e1, g1])
                    unstage(si, g0)
                    unstage(sj, g1)
                give(b0, e0)
                give(b1, e1)
                yield
            tk["qi_read"] = p
            r0, r1 = IW[:, 0, 0:128], IW[:, 1, :]
            q0 = DV.op(tt(r0, a0[:, 0, :], a0[:, 1, :], ADD), [g0, *ready[0]])
            q1 = DV.op(tt(r1, a1[:, 0, :], a1[:, 1, :], ADD), [g1])
            q0 = DV.op(tt(r0, r0, causal[:, 128:256], ADD), [q0])
            q1 = DV.op(tt(r1, r1, causal, ADD), [q1])
            mxa, mxb = mx8, sm[:, 344:352]
            for it in range(8):
                x0 = DV.op(lambda e: e.max(mxa, r0), [q0])
                x1 = DV.op(lambda e: e.max(mxb, r1), [q1])
                q0 = DV.op(lambda e: e.match_replace(r0, mxa, r0, -3e38), [x0])
                q1 = DV.op(lambda e: e.match_replace(r1, mxb, r1, -3e38), [x1])
                if it % 2:
                    yield
            q0 = DV.op(ts(MN0, r0, -2e38, ALU.is_gt, NEG, MUL), [q0])
            q1 = DV.op(ts(MN1, r1, -2e38, ALU.is_gt, NEG, MUL), [q1])
            q0 = DV.op(tt(MN0, MN0, causal[:, 128:256], ADD), [q0])
            q1 = DV.op(tt(MN1, MN1, causal, ADD), [q1])
            tk["sel"] = [q0, q1]
            lane_free[0] = lane_free[1] = [q0, q1]
            yield

        def headnorm(dst, name, gain, nh, blk):
            def evac(ps, tok):
                f = []
                for hf in range((nh + 1) // 2):
                    si, s_, w = stage()
                    m = 512 if nh > 1 else 256
                    e = copy_out(s_[:, 0:m], ps[hf][:, 0:m], [tok, *w])
                    f.append(e)
                    short.append(job(si, s_, e, hf, m))
                return f

            def job(si, s_, e, hf, m):
                s2, s2_, w2 = stage()
                g = GP.op(tt(s2_[:, 0:m], s_[:, 0:m], s_[:, 0:m], MUL), [e, *w2])
                yield
                b, w = take()
                p = PE.op(mm(b[:, 0:m], on128, s2_[:, 0:m]), [g, *w])
                a = AC.op(act(s2_[:, 0:m], b[:, 0:m], ACT.Sqrt, bias=eps_c), [p, t_eps])
                give(b, a)
                yield
                r = DV.op(recip(s2_[:, 0:m], s2_[:, 0:m]), [a])
                d = dst if nh == 1 else dst[:, 4 * blk + 2 * hf:4 * blk + 2 * hf + 2, :].rearrange("p a s -> p (a s)")
                r = DV.op(stt(d, s_[:, 0:m], gain, s2_[:, 0:m], MUL, MUL), [r, *ready[0]])
                unstage(si, r)
                unstage(s2, r)
                tk[(name, 2 * blk + hf)] = r
                yield
            return evac

        def va_evac(ps, tok):
            e = [copy_out(VA[:, i, :], ps[i][:, 0:128], [tok, *ready[0]]) for i in range(2)]
            tk["va"] = e
            return e

        def sparse(hp):
            h0 = 2 * hp
            base = W2
            L0, L1 = carve(base, 2, 128), carve(base + 256, 2, 256)
            mcol, rcol = lane_sm[0][:, 0:4], lane_sm[0][:, 4:8]
            lw = lane_free[0]
            g0 = GP.op(tt(L0, B0[:, h0:h0 + 2, :], mid(MN0, 2), ADD), [*tk["sel"], *tk["bias"], *lw])
            g1 = GP.op(tt(L1, B1[:, h0:h0 + 2, :], mid(MN1, 2), ADD), [*tk["sel"], *tk["bias"], *lw])
            b0, w0 = take()
            b1, w1 = take()
            fs = []
            for h in range(2):
                fs.append(mm(b0[:, 128 * h:128 * h + 128], QA[:, h0 + h, 0:128], KA[:, 0:128]))
                fs.append(mm(b1[:, 256 * h:256 * h + 256], QA[:, h0 + h, 128:256], KA))
            p = PE.op(mms(*fs), [tk[("qa", hp)], tk[("ka", 0)], *w0, *w1])
            e0 = DV.op(stt(L0, b0[:, 0:256].rearrange("p (h s) -> p h s", h=2), 128.0 ** -0.5, L0, MUL, ADD), [p, g0])
            e1 = DV.op(stt(L1, b1[:, :].rearrange("p (h s) -> p h s", h=2), 128.0 ** -0.5, L1, MUL, ADD), [p, g1])
            give(b0, e0)
            give(b1, e1)
            yield
            n0, n1 = yield from softmax_rows(L0, L1, e0, e1, 2, mcol, rcol, 1.0)
            yield
            PT0, PT1, pt, cc = attend_pv(L0, L1, n0, n1, None, None, 0, base)
            yield
            b, w = take()
            fs = []
            for h in range(2):
                fs.append(mm(b[:, 256 * h:256 * h + 256], VA[:, 0, :], PT0[:, h, :], start=(h == 0), stop=False))
                fs.append(mm(b[:, 256 * h + 128:256 * h + 256], VA[:, 1, :], PT1[:, h, :], start=False, stop=True))
            p = PE.op(mms(*fs), [*cc, *w, *tk["va"]])
            e = copy_out(YAF[:, h0:h0 + 2, :].rearrange("p a s -> p (a s)"), b[:, :], [p])
            give(b, e)
            lane_free[0] = [p]
            tk[("yaf", hp)] = e
            yield

        def rot(dst, name, blk):
            def evac(ps, tok):
                f = []
                for hf in range(2):
                    si, s_, w = stage()
                    e = copy_out(s_, ps[hf][:, :], [tok, *w])
                    f.append(e)
                    short.append(job(si, s_, e, 2 * blk + hf))
                return f

            def job(si, s_, e, hp):
                d = dst[:, 2 * hp:2 * hp + 2, :]
                sv = s_.rearrange("p (h s) -> p h s", h=2)
                s2, s2_, w2 = stage()
                s2v = s2_.rearrange("p (h s) -> p h s", h=2)
                m = DV.op(tt(d, sv, mid(cs[:, 0, :], 2), MUL), [e, *ready[0], *tk["rope2"]])
                x_ = DV.op(tt(s2v[0:64], sv[64:128], mid(cs[64:128, 1, :], 2), MUL), [e, *w2])
                x_ = DV.op(tt(s2v[64:128], sv[0:64], mid(cs[0:64, 1, :], 2), MUL), [e, *w2])
                g = GP.op(tt(d, d, s2v, ADD), [m, x_])
                unstage(si, x_)
                unstage(s2, g)
                tk[(name, hp)] = g
                yield
            return evac

        def vb_evac(blk):
            def evac(ps, tok):
                f = [copy_out(VBB[:, i, 512 * blk:512 * blk + 512], ps[i][:, :], [tok, *ready[0]]) for i in range(2)]
                tk[("vb", blk)] = f
                return f
            return evac

        def retain(hp):
            h0 = 2 * hp
            base = W2 + 1792
            si, s_, w = stage()
            sj, t_, w3 = stage()
            S0, S1 = s_.rearrange("p (h s) -> p h s", h=2), t_[:, 0:256].rearrange("p (h s) -> p h s", h=2)
            b0, w0 = take()
            b1, w1 = take()
            fs = []
            for h in range(2):
                fs.append(mm(b0[:, 256 * h:256 * h + 256], KB[:, h0 + h, 0:128], QB[:, h0 + h, :]))
                fs.append(mm(b1[:, 128 * h:128 * h + 128], KB[:, h0 + h, 128:256], QB[:, h0 + h, 128:256]))
            p = PE.op(mms(*fs), [tk[("qb", hp)], tk[("kb", hp)], *w0, *w1])
            e0 = DV.op(tt(S0, b0[:, :].rearrange("p (h s) -> p h s", h=2), DM[:, h0:h0 + 2, 0:256], MUL),
                       [p, tk["dm"], *w])
            e1 = DV.op(tt(S1, b1[:, 0:256].rearrange("p (h s) -> p h s", h=2), DM[:, h0:h0 + 2, 0:128], MUL),
                       [p, tk["dm"], *w3])
            give(b0, e0)
            give(b1, e1)
            yield
            b, w = take()
            fs = []
            for h in range(2):
                sl = slice(128 * (h0 + h), 128 * (h0 + h) + 128)
                fs.append(mm(b[:, 256 * h:256 * h + 256], VBB[:, 0, sl], S0[:, h, :], start=(h == 0), stop=False))
                fs.append(mm(b[:, 256 * h + 128:256 * h + 256], VBB[:, 1, sl], S1[:, h, :], start=False, stop=True))
            p = PE.op(mms(*fs), [e0, e1, *w, *tk[("vb", hp // 2)]])
            c_ = copy_out(s_, b[:, :], [p])
            give(b, c_)
            yield
            b, w = take()
            p = PE.op(mm(b[:, :], on128, s_), [c_, *w])
            yield
            x_ = DV.op(tt(s_, s_, b[:, :], SUB), [p])
            give(b, x_)
            g = GP.op(tt(t_, s_, s_, MUL), [x_])
            yield
            b, w = take()
            p = PE.op(mm(b[:, :], on128, t_), [g, *w])
            a = AC.op(act(t_, b[:, :], ACT.Sqrt, bias=eps_c), [p, t_eps])
            give(b, a)
            yield
            r = DV.op(recip(t_, t_), [a])
            for h in range(2):
                y = DV.op(stt(YBF[:, h0 + h, :], s_[:, 256 * h:256 * h + 256], col("rn", 8 * L + h0 + h),
                              t_[:, 256 * h:256 * h + 256], MUL, MUL), [r, tk["qi_read"]])
            unstage(si, y)
            unstage(sj, y)
            tk[("ybf", hp)] = y
            yield

        def g_evac(src, dst, name, sname, blk):
            def evac(ps, tok):
                f = []
                for hf in range(2):
                    hp = 2 * blk + hf
                    si, s_, w = stage()
                    sj, t_, w3 = stage()
                    a = AC.op(act(t_, ps[hf][:, :], ACT.Tanh, scale=0.5), [tok, *w3])
                    r = DV.op(stt(t_, t_, 1.0, ps[hf][:, :], ADD, MUL), [a])
                    f.append(r)
                    short.append(job(hp, si, s_, sj, t_, r, w))
                return f

            def job(hp, si, s_, sj, t_, r, w):
                y = GP.op(tt(s_, src[:, 2 * hp:2 * hp + 2, :].rearrange("p a s -> p (a s)"), t_, MUL),
                          [r, tk[(sname, hp)], *w])
                unstage(sj, y)
                yield
                o = yield from split_out(dst, 2 * hp, s_, [y])
                unstage(si, o)
                tk[(name, hp)] = o
            return evac

        add(WIN, 3328, 128, KT, "CM", h_ops, ki_evac, start, dup=True)
        add(WIN, 3392, 16, KT, "TM", h_ops, wi_evac)
        add(WIN, 2304, 512, KT, "CM", h_ops, qi_evac(0))
        add(WIN, 2816, 512, KT, "CM", h_ops, qi_evac(1))
        add(WIN, 1024, 128, KT, "CM", h_ops, headnorm(KA, "ka", col("kn", L), 1, 0),
            launch(indexer()))
        add(WIN, 0, 512, KT, "CM", h_ops, headnorm(QA, "qa", col("qn", L), 4, 0))
        add(WIN, 512, 512, KT, "CM", h_ops, headnorm(QA, "qa", col("qn", L), 4, 1))
        add(WIN, 1152, 128, KT, "TM", h_ops, va_evac)

        def chain(f):
            for hp in range(4):
                yield from f(hp)

        for blk in range(2):
            add(WIN, 3408 + 512 * blk, 512, KT, "CM", h_ops, rot(QB, "qb", blk),
                launch(retain(0), retain(1)) if blk else launch(chain(sparse)))
            add(WIN, 4432 + 512 * blk, 512, KT, "CM", h_ops, rot(KB, "kb", blk))
            add(WIN, 5456 + 512 * blk, 512, KT, "TM", h_ops, vb_evac(blk))
        for blk in range(2):
            add(WIN, 1280 + 512 * blk, 512, KT, "CM", h_ops, g_evac(YAF, YA2, "y2a", "yaf", blk),
                None if blk else launch(retain(2), retain(3)))
        for blk in range(2):
            add(WIN, 6480 + 512 * blk, 512, KT, "CM", h_ops, g_evac(YBF, YB2, "y2b", "ybf", blk))

        def begin():
            state["sq"] = []
            state["gb_free"] = []

        o_ops = ((lambda k: YA2[:, k, 0, :] if k < 8 else YB2[:, k - 8, 0, :]),
                 (lambda k: YA2[:, k, 1, :] if k < 8 else YB2[:, k - 8, 1, :]),
                 (lambda k: [tk[("y2a", k // 2)]] if k < 8 else [tk[("y2b", k // 2 - 4)]]))

        def o_evac(blk):
            def evac(ps, tok):
                f = []
                for i in range(2):
                    xs = X[:, i, 512 * blk:512 * blk + 512]
                    si, s_, w = stage()
                    e = DV.op(stt(s_, ps[i][:, :], 0.5, GB[:, 512 * blk:512 * blk + 512], MUL, MUL),
                              [tok, mod_done[(L, 8 + blk)], *w])
                    f.append(e)
                    x_ = DV.op(tt(xs, xs, s_, ADD), [e, state["x"][i][blk]])
                    unstage(si, x_)
                    state["x"][i][blk] = x_
                    state["gb_free"] = state["gb_free"] + [e]
                    if L == 0:
                        state["sq"].append(sumsq(i, blk, [x_]))
                    else:
                        SP.dma(out[0, 128 * i:128 * i + 128, 512 * blk:512 * blk + 512], xs, s_out, [x_])
                return f
            return evac

        for blk in range(4):
            add(t["w_out_2"][L], 512 * blk, 512, KT, "TM", o_ops, o_evac(blk), begin if blk == 0 else None)

    state["gsc_free"] = []
    state["gb_free"] = []
    marks = {}
    for L in range(2):
        marks[L] = len(chunks)
        layer2(L)

    up0 = next(i for i, c in enumerate(chunks) if c[1]["need"] is ffn_need)

    def spread(items, lo, hi):
        n = len(items)
        return [(lo + (hi - lo) * (i + 1) // (n + 1), it) for i, it in enumerate(items)]

    nsp = [c for L in range(2) for b in range(8) for c in add_mod(L, b)]
    puts = spread(nsp, 12, marks[0] - 12)
    puts += spread([c for b in range(8, 12) for c in add_mod(0, b)], marks[0] + 8, marks[1] - 24)
    puts += spread([c for b in range(8, 12) for c in add_mod(1, b)], marks[1] + 8, len(chunks) - 24)
    by = {}
    for at, c in puts:
        by.setdefault(at, []).append(c)
    merged = []
    for i, c in enumerate(chunks):
        merged += by.get(i, [])
        merged.append(c)
    chunks[:] = merged

    for j in range(R1):
        send(j)
    at = 0
    for b in blocks:
        at = run_block(b, at)
    finish_all()
    SP.wait([(s_out.sem, s_out.n)])

    block = ctx.enter_context(nc.Block())

    @block.sync
    def _(e):
        SP.emit(e)

    @block.tensor
    def _(e):
        PE.emit(e)

    @block.scalar
    def _(e):
        AC.emit(e)

    @block.vector
    def _(e):
        DV.emit(e)

    @block.gpsimd
    def _(e):
        GP.emit(e)


_INS = ["x", "positions", "ln1", "w_in", "gdn_conv", "gdn_a_log", "gdn_dt_bias", "gdn_norm", "w_branch_a",
        "w_branch_b", "w_out", "ln2", "w_up", "ffn_conv", "ffn_conv_bias", "w_down", "final_norm", "c_2",
        "positions_2", "rel_bias_2", "norm_gain_2", "w_mod_2", "b_mod_2", "w_in_2", "q_norm_gain_2",
        "k_norm_gain_2", "ret_norm_gain_2", "w_out_2"]


def kernel(**inputs):
    import numpy as _np
    import concourse.bacc as _bacc
    from concourse import mybir as _mybir
    from concourse.bass_utils import run_bass_kernel_spmd as _run

    nc = _bacc.Bacc("TRN2", target_bir_lowering=False, num_devices=1)
    arrays, aps = {}, {}
    for name in _INS:
        a = _np.ascontiguousarray(inputs[name])
        arrays[f"in_{name}"] = a
        aps[name] = nc.dram_tensor(f"in_{name}", a.shape, _mybir.dt.from_np(a.dtype), kind="ExternalInput").ap()
    for name, a in (("cst", constants()), ("dm", decay())):
        arrays[f"in_{name}"] = a
        aps[name] = nc.dram_tensor(f"in_{name}", a.shape, _mybir.dt.from_np(a.dtype), kind="ExternalInput").ap()
    out = nc.dram_tensor("out_0", (1, 256, 2048), _mybir.dt.float32, kind="ExternalOutput").ap()
    build(nc, aps, out)
    r = _run(nc, [arrays], core_ids=[0])
    return r.results[0]["out_0"]
```

```python
import math
from contextlib import ExitStack

import concourse.bass as bass
from concourse import mybir
import numpy as np

F32 = mybir.dt.float32
BF16 = mybir.dt.bfloat16
I32 = mybir.dt.int32
ALU = mybir.AluOpType
ACT = mybir.ActivationFunctionType
AX = mybir.AxisListType.X
ADD, SUB, MUL, MAX, MIN = ALU.add, ALU.subtract, ALU.mult, ALU.max, ALU.min

D = 2048
S = 256
KT = D // 128
GW = 1024
DFF = 5632
FT = DFF // 128
EPS = 1e-6
NEG = -1e30
R1 = 3
R2 = 4
LOOK = 3
NSTG = 7
CH = 2048

ROPE1 = 16
THETA1 = 500000.0
THETA2 = 10000.0
TWO_PI = [6.25, 0.03125, 0.0019350051879882812, 3.0199159819567e-07]

C_ID, C_TRI, C_ONE, C_ON128, C_CAUS, C_GMASK, C_PERM = 0, 128, 256, 384, 512, 768, 896
C_INV1, C_INV2, C_SG1, C_SG2, C_THR, NCONST = 928, 929, 930, 931, 932, 936
C_LEV = NCONST
NLOAD = NCONST + 7 * 128


def constants():
    c = np.zeros((128, NLOAD), np.float32)
    i = np.arange(128)
    c[:, C_ID:C_ID + 128] = np.eye(128)
    c[:, C_TRI:C_TRI + 128] = i[:, None] <= i[None, :]
    c[:, C_ONE:C_ONE + 128] = 1.0
    c[:, C_ON128:C_ON128 + 128] = 1.0 / 128
    c[:, C_CAUS + 128:C_CAUS + 256] = np.where(i[None, :] <= i[:, None], 0.0, NEG)
    c[:, C_GMASK:C_GMASK + 128] = np.where(i[None, :] >= i[:, None], 0.0, NEG)
    for l in range(7):
        b = 1 << l
        same = (i[:, None] // (2 * b)) == (i[None, :] // (2 * b))
        low = (i[:, None] % (2 * b)) < b
        up = (i[None, :] % (2 * b)) >= b
        c[:, C_LEV + 128 * l:C_LEV + 128 * l + 128] = same & low & up
    for m in range(32):
        c[(m + 16) % 32, C_PERM + m] = 1.0
    h1 = np.arange(16, dtype=np.float32)
    inv1 = (np.float32(THETA1) ** (-h1 / np.float32(16))).astype(np.float32)
    c[0:16, C_INV1] = inv1
    c[16:32, C_INV1] = inv1
    c[0:16, C_SG1] = -1.0
    c[16:32, C_SG1] = 1.0
    h2 = np.arange(64, dtype=np.float32)
    inv2 = (np.float32(THETA2) ** (-h2 / np.float32(64))).astype(np.float32)
    c[0:64, C_INV2] = inv2
    c[64:128, C_INV2] = inv2
    c[0:64, C_SG2] = 1.0
    c[64:128, C_SG2] = -1.0
    c[:, C_THR] = np.tile(np.array([-4e9] + [v - 1.0 for v in thresholds()], np.float32), 4)
    return c


def decay():
    h = np.arange(8, dtype=np.float32)
    lg = np.log1p(-np.exp2(-5.0 - h)).astype(np.float32)
    j = np.arange(128)
    out = np.zeros((128, 8, 256), np.float32)
    for hh in range(8):
        d0 = np.arange(256)[None, :] - j[:, None]
        out[:, hh, 0:256] = np.where(d0 >= 0, np.exp(lg[hh] * np.maximum(d0, 0)), 0.0)
    return (out * np.float32(128.0 ** -0.5)).astype(np.float32).reshape(128, 2048)


def thresholds():
    out = list(range(1, 17))
    for b in range(17, 32):
        out.append(int(math.ceil(16.0 * 8.0 ** ((b - 16) / 16.0) - 1e-9)))
    return out


class Queue:

    def __init__(self, sem):
        self.sem, self.n, self.todo, self.seen = sem, 0, [], {}

    def wait(self, toks):
        for t in toks:
            if t is None:
                continue
            sem, v = t
            if self.seen.get(id(sem), 0) < v:
                self.seen[id(sem)] = v
                self.todo.append((0, sem, v))

    def op(self, fn, after=(), sig=True):
        self.wait(after)
        if sig:
            self.n += 1
            self.todo.append((1, fn, self.sem))
            return (self.sem, self.n)
        self.todo.append((2, fn, None))
        return None

    def dma(self, out, in_, slot, after=()):
        self.wait(after)
        slot.n += 16
        sem = slot.sem
        self.todo.append((2, lambda e: e.dma_start(out, in_).then_inc(sem, 16), None))
        return (sem, slot.n)

    def emit(self, e):
        for kind, a, b in self.todo:
            if kind == 0:
                e.wait_ge(a, b)
            elif kind == 1:
                a(e).then_inc(b, 1)
            else:
                a(e)


class Slot:
    def __init__(self, sem):
        self.sem, self.n = sem, 0


def mm(o, l, r, start=True, stop=True):
    return lambda e: e.matmul(o, l, r, start=start, stop=stop, skip_group_check=True)


def mms(*fns):
    def run(e):
        for f in fns:
            last = f(e)
        return last
    return run


def tp(o, i, ident):
    return lambda e: e.transpose(o, i, ident)


def act(o, i, f, bias=None, scale=1.0, acc=None):
    if bias is None:
        if acc is None:
            return lambda e: e.activation(o, i, f, scale=scale)
        return lambda e: e.activation(o, i, f, scale=scale, accum_out=acc)
    if acc is None:
        return lambda e: e.activation(o, i, f, bias=bias, scale=scale)
    return lambda e: e.activation(o, i, f, bias=bias, scale=scale, accum_out=acc)


def cp(o, i):
    return lambda e: e.tensor_copy(o, i)


def tt(o, a, b, op):
    return lambda e: e.tensor_tensor(o, a, b, op)


def ts(o, a, s1, op0, s2=None, op1=None):
    if op1 is None:
        return lambda e: e.tensor_scalar(o, a, s1, None, op0)
    return lambda e: e.tensor_scalar(o, a, s1, s2, op0, op1)


def stt(o, a, s, b, op0, op1):
    return lambda e: e.scalar_tensor_tensor(o, a, s, b, op0, op1)


def red(o, a, op):
    return lambda e: e.tensor_reduce(o, a, AX, op)


def recip(o, a):
    return lambda e: e.reciprocal(o, a)


def mid(a, n):
    return a.unsqueeze(1).to_broadcast([a.shape[0], n, a.shape[1]])


def rep(a, n):
    return a.unsqueeze(2).to_broadcast([a.shape[0], a.shape[1], n])


def build(nc, t, out):
    ctx = ExitStack()
    with ctx:
        program(nc, t, out, ctx)


def program(nc, t, out, ctx):
    def sb(name, shape, dt=F32):
        return ctx.enter_context(nc.sbuf_tensor(name, shape, dt))

    def sem(name):
        return ctx.enter_context(nc.semaphore(name))

    bank = [ctx.enter_context(nc.psum_tensor(f"ps{i}", [128, 512], F32)) for i in range(8)]
    PE, AC, DV, GP, SP = (Queue(sem(f"done_{n}")) for n in ("pe", "act", "dve", "pool", "sp"))

    ring = sb("ring", [128, R1, CH])
    whi = sb("whi", [128, R2, CH], BF16)
    wlo = sb("wlo", [128, R2, CH], BF16)
    X = sb("X", [128, 2, D])
    hh = sb("hh", [128, KT, S])
    hb = hh[:, :, :].rearrange("p k s -> p (k s)").bitcast(BF16).rearrange("p (k c s) -> p k c s", c=2, s=S)
    hhi, hlo = hb[:, :, 0, :], hb[:, :, 1, :]
    cst = sb("cst", [128, NCONST])
    VT = sb("VT", [128, 648])
    cs = sb("cs", [128, 2, S])
    lev = sb("lev", [128, 7, 128], BF16)
    stg = sb("stg", [128, NSTG, 512])
    sm = sb("sm", [128, 512])
    modcm = sb("modcm", [128, 2, 32])
    AR = sb("AR", [128, 22528])
    arp = [0]

    def carve(at, *shape, dt=F32):
        n = 1
        for s_ in shape:
            n *= s_
        w = (n + 1) // 2 if dt == BF16 else n
        v = AR[:, at:at + w]
        if dt != F32:
            v = v.bitcast(dt)
        if len(shape) == 1:
            return v
        names = "abcd"[:len(shape)]
        kw = {names[i]: shape[i] for i in range(1, len(shape))}
        return v.rearrange(f"p ({' '.join(names)}) -> p {' '.join(names)}", **kw)

    ident = cst[:, C_ID:C_ID + 128]
    tri = cst[:, C_TRI:C_TRI + 128]
    ones = cst[:, C_ONE:C_ONE + 128]
    on128 = cst[:, C_ON128:C_ON128 + 128]
    causal = cst[:, C_CAUS:C_CAUS + 256]
    gmask = cst[:, C_GMASK:C_GMASK + 128]

    ssq = sm[:, 0:8]
    ssf = sm[:, 352:360]
    rst = sm[:, 8:12]
    rs2 = sm[:, 360:364]
    eps_c = sm[:, 12:13]
    eps4_c = sm[:, 13:14]
    eps512_c = sm[:, 14:15]
    bd = sm[:, 16:48].rearrange("p (n c) -> p n c", n=2)
    gd = sm[:, 48:64].rearrange("p (n c) -> p n c", n=2)
    bet = sm[:, 64:80].rearrange("p (n c) -> p n c", n=2)
    gcn = sm[:, 80:96].rearrange("p (n c) -> p n c", n=2)
    eg = sm[:, 96:112].rearrange("p (n c) -> p n c", n=2)
    alog = sm[:, 112:120]
    dtb = sm[:, 120:128]
    tA = sm[:, 128:144].rearrange("p (n c) -> p n c", n=2)
    tB = sm[:, 144:160].rearrange("p (n c) -> p n c", n=2)
    c2 = sm[:, 160:176]
    wi = sm[:, 176:208].rearrange("p (n c) -> p n c", n=2)
    gsc = sm[:, 208:224]
    posc = sm[:, 224:226]
    beg = sm[:, 232:240]
    lane_sm = [sm[:, 240 + 48 * i:288 + 48 * i] for i in range(2)]
    mx8 = sm[:, 336:344]
    eps128_c = sm[:, 15:16]
    rk, rq = sm[:, 364:380], sm[:, 380:396]
    qr = sm[:, 396:412].rearrange("p (h n) -> p h n", n=2)
    ret_sm = [sm[:, 412 + 12 * i:424 + 12 * i] for i in range(4)]

    s_x = [Slot(sem(f"in_x{i}")) for i in range(2)]
    s_c, s_v0, s_v = Slot(sem("in_const")), Slot(sem("in_vec0")), Slot(sem("in_vec"))
    s_row, s_out, s_dm, s_gb = Slot(sem("in_rows")), Slot(sem("out")), Slot(sem("in_decay")), [Slot(sem(f"in_gate{i}")) for i in range(2)]
    s_fn = Slot(sem("in_final_norm"))
    vst = carve(0, 6, 128)
    t_x = [SP.dma(X[:, 0, :], t["x"][0, 0:128, :], s_x[0]), None]
    t_cst = SP.dma(cst[:, :], t["cst"][:, 0:NCONST], s_c)
    vec = {}
    vrow = [0]

    def vplace(name, src):
        vec[name] = vrow[0]
        vrow[0] += src.shape[0]
        return vec[name], src

    def vload(place, slot):
        r0, src = place
        n, done = src.shape[0], 0
        while done < n:
            r = r0 + done
            k = min(n - done, 128 - r % 128)
            tok = SP.dma(vst[r % 128:r % 128 + k, r // 128, :], src[done:done + k, :], slot)
            done += k
        return tok

    vecs = [vplace(*v) for v in (
        ("ln1", t["ln1"].rearrange("a (t p) -> (a t) p", p=128)),
        ("ln2", t["ln2"].rearrange("a (t p) -> (a t) p", p=128)),
        ("conv", t["gdn_conv"].rearrange("a i (t p) -> (a i t) p", p=128)),
        ("fconv", t["ffn_conv"].rearrange("a i (t p) -> (a i t) p", p=128)),
        ("fbias", t["ffn_conv_bias"].rearrange("a (t p) -> (a t) p", p=128)),
        ("c", t["c_2"].rearrange("a (t p) -> (a t) p", p=128)),
        ("ng", t["norm_gain_2"].rearrange("a (t p) -> (a t) p", p=128)),
        ("bmod", t["b_mod_2"].rearrange("a (t p) -> (a t) p", p=128)),
        ("gn", t["gdn_norm"]), ("qn", t["q_norm_gain_2"]), ("kn", t["k_norm_gain_2"]),
        ("rn", t["ret_norm_gain_2"].rearrange("a (t p) -> (a t) p", p=128)))]
    t_v0 = [vload(v, s_v0) for v in vecs[:3]][-1]
    assert vec["fconv"] == 128
    t_x[1] = SP.dma(X[:, 1, :], t["x"][0, 128:256, :], s_x[1])

    def col(name, i):
        c = vec[name] + i
        return VT[:, c:c + 1]

    def cols(name, i, n):
        c = vec[name] + i
        return VT[:, c:c + n]

    pos_i = carve(1024, S, dt=I32)
    levf = carve(3328, 7, 128)

    def later_loads():
        SP.dma(alog, t["gdn_a_log"].rearrange("a h -> (a h)").partition_broadcast(128), s_row)
        SP.dma(dtb, t["gdn_dt_bias"].rearrange("a h -> (a h)").partition_broadcast(128), s_row)
        SP.dma(levf, t["cst"][:, C_LEV:NLOAD].rearrange("p (l n) -> p l n", l=7), s_row)
        row = SP.dma(pos_i, t["positions"].rearrange("a s -> (a s)").partition_broadcast(128), s_row)
        return row, [vload(v, s_v) for v in vecs[3:]][-1]

    main = [[bank[0], bank[1]], [bank[2], bank[3]]]
    main_free = [[], []]
    bg_free = [(bank[i], []) for i in range(4, 8)]

    def take():
        assert bg_free, "no background bank"
        return bg_free.pop(0)

    def give(b, *toks):
        bg_free.append((b, list(toks)))

    stg_buf = [stg[:, i, :] for i in range(NSTG)]
    stg_free = [(i, []) for i in range(NSTG)]

    def stage():
        assert stg_free, "no staging buffer"
        i, w = stg_free.pop(0)
        return i, stg_buf[i], w

    def more_stages(bufs, after):
        for v in bufs:
            stg_buf.append(v)
            stg_free.append((len(stg_buf) - 1, list(after)))

    def unstage(i, *toks):
        stg_free.append((i, list(toks)))

    t0 = DV.op(lambda e: e.memset(eps_c, EPS))
    t0 = DV.op(lambda e: e.memset(eps4_c, 4 * EPS))
    t0 = DV.op(lambda e: e.memset(eps128_c, 128 * EPS))
    t_eps = DV.op(lambda e: e.memset(eps512_c, 512 * EPS))

    state = {"h": None, "x": [[t_x[i]] * 4 for i in range(2)], "sq": [], "sqf": [], "xt": [None] * (KT // 2), "xp": []}

    def sumsq(i, j, after, dst=ssq):
        k, s_, w = stage()
        tk = AC.op(act(s_, X[:, i, 512 * j:512 * j + 512], ACT.Square, acc=dst[:, 4 * i + j:4 * i + j + 1]),
                   [*after, *w])
        unstage(k, tk)
        return tk

    def sqrt_ahead():
        AC.op(act(sm[:, 460:461], eps_c, ACT.Sqrt), [t_eps])

    def rstd_of(toks):
        r = DV.op(red(rst[:, 0:2], ssq.rearrange("p (i j) -> p i j", i=2), ADD), toks)
        r = AC.op(act(rst[:, 0:2], rst[:, 0:2], ACT.Sqrt, bias=eps_c, scale=1.0 / D), [r, t_eps])
        return DV.op(recip(rst[:, 2:4], rst[:, 0:2]), [r])

    def xpose(j, eng=None):
        for k in (4 * j, 4 * j + 2):
            b, w = take()
            p = PE.op(mms(*[tp(b[:, 256 * kk + 128 * i:256 * kk + 128 * i + 128],
                               X[:, i, 128 * (k + kk):128 * (k + kk) + 128], ident)
                            for i in range(2) for kk in range(2)]),
                      [state["x"][0][j], state["x"][1][j], t_cst, *w])
            dst = hh[:, k:k + 2, :].rearrange("p a s -> p (a s)")
            if eng is None:
                e = AC.op(act(dst, b[:, :], ACT.Copy), [p])
            else:
                e = eng.op(cp(dst, b[:, :]), [p])
            give(b, e)
            state["xt"][k // 2] = e
            state["xlast"] = p
            yield

    def delayed(n, g):
        yield n
        yield from g

    def xpose_later(j):
        g = delayed(2, xpose(j))
        state["xp"].append(g)
        short.append(g)

    def norm_to_h(scale, shift, r, after, meanwhile=None):
        for g in state["xp"]:
            for _ in g:
                pass
        state["xp"] = []
        kd_, dbuf, w = stage()
        dg = [dbuf[:, 128 * i:128 * i + 128] for i in range(2)]
        dgt = [DV.op(ts(dg[i], ident, rst[:, 2 + i:3 + i], MUL), [r, t_cst, *w]) for i in range(2)]
        b, w = take()
        bc = b[:, 0:256]
        p = PE.op(mms(*[mm(b[:, 128 * i:128 * i + 128], ones, dg[i]) for i in range(2)]), [*dgt, *w])
        unstage(kd_, p)
        toks = []

        def lo_part(si, s_, k, a):
            if shift is None:
                l = GP.op(tt(hlo[:, k:k + 2, :], s_.rearrange("p (a s) -> p a s", a=2), hhi[:, k:k + 2, :], SUB), [a])
            else:
                for kk in range(2):
                    l = DV.op(stt(hlo[:, k + kk, :], s_[:, 256 * kk:256 * kk + 256], shift(k + kk),
                                  hhi[:, k + kk, :], ADD, SUB), [a])
            unstage(si, l)
            toks.append(l)

        last = None
        for k in range(0, KT, 2):
            si, s_, w = stage()
            for kk in range(2):
                e = DV.op(stt(s_[:, 256 * kk:256 * kk + 256], hh[:, k + kk, :], scale(k + kk), bc, MUL, MUL),
                          [p, state["xt"][k // 2], *w, *after])
            if shift is None:
                a = AC.op(act(hhi[:, k:k + 2, :], s_.rearrange("p (a s) -> p a s", a=2), ACT.Copy), [e])
            else:
                for kk in range(2):
                    a = AC.op(act(hhi[:, k + kk, :], s_[:, 256 * kk:256 * kk + 256], ACT.Identity,
                                  bias=shift(k + kk)), [e])
            if last is not None:
                lo_part(*last)
            last = (si, s_, k, a)
            if meanwhile is not None and k in meanwhile:
                ensure(*meanwhile[k])
        give(b, e)
        lo_part(*last)
        state["h"] = toks

    chunks = []
    blocks = []

    def add(w, c0, n, kt, orient, lhs, evac, need=None, dup=False):
        b = dict(w=w, c0=c0, n=n, kt=kt, orient=orient, lhs=lhs, evac=evac, need=need, dup=dup)
        blocks.append(b)
        per = min(kt, CH // n)
        k = 0
        while k < kt:
            m = min(per, kt - k)
            chunks.append(("w", b, k, m))
            k += m
        return b

    slots = [Slot(sem(f"ring{i}")) for i in range(R1)]
    ring_free = [[] for _ in range(R1)]
    ring_tok = {}
    w_free = [[] for _ in range(R2)]
    w_tok = {}
    sent = [0]
    split = [0, 0]
    wn = [0]
    wslot = {}

    def send(j):
        if j >= len(chunks):
            return
        kind, b, k, m = chunks[j]
        i = j % R1
        n = b["n"]
        dst = ring[:, i, 0:m * n].rearrange("p (k n) -> p k n", n=n)
        src = b["w"][128 * k:128 * (k + m), :].rearrange("(k p) n -> p k n", p=128)
        if b["dup"]:
            h = n // 2
            SP.dma(dst[:, :, 0:h], src[:, :, b["c0"]:b["c0"] + h], slots[i], ring_free[i])
            ring_tok[j] = SP.dma(dst[:, :, h:n], src[:, :, b["c0"]:b["c0"] + h], slots[i])
        else:
            ring_tok[j] = SP.dma(dst, src[:, :, b["c0"]:b["c0"] + n], slots[i], ring_free[i])

    short, long = [], []

    pause = {}

    def step_jobs():
        for q, n in ((short, len(short)), (long, 2)):
            for g in q[:n]:
                if pause.get(id(g), 0) > 0:
                    pause[id(g)] -= 1
                    continue
                try:
                    pause[id(g)] = (next(g) or 1) - 1
                except StopIteration:
                    q.remove(g)

    def finish_all():
        while short or long:
            step_jobs()

    def halves(m):
        h = (m + 1) // 2
        return [(0, m)] if m < 4 else [(0, h), (h, m)]

    def split_part(j, pi):
        kind, b, k, m = chunks[j]
        i = j % R1
        n = b["n"]
        ka, kb = halves(m)[pi]
        end = kb == m
        if kind == "mod":
            w = ring[:, i, ka * n:kb * n].rearrange("p (k n) -> p k n", n=n)
            ring_free[i] = [mod_step(b, k + ka, kb - ka, w, ring_tok[j])]
        else:
            if pi == 0:
                wslot[j] = wn[0] % R2
                wn[0] += 1
            q = wslot[j]
            sl = slice(ka * n, kb * n)
            a = AC.op(act(whi[:, q, sl], ring[:, i, sl], ACT.Copy), [ring_tok[j], *w_free[q]])
            l = DV.op(tt(wlo[:, q, sl], ring[:, i, sl], whi[:, q, sl], SUB), [a])
            ring_free[i] = [l]
            if end:
                w_free[q] = None
            w_tok[(j, pi)] = l
        if end:
            send(j + R1)

    def ensure(j, pi):
        if j >= len(chunks):
            j, pi = len(chunks) - 1, 1
        while tuple(split) <= (j, min(pi, len(halves(chunks[j][3])) - 1)):
            split_part(*split)
            split[1] += 1
            if split[1] == len(halves(chunks[split[0]][3])):
                split[0], split[1] = split[0] + 1, 0
            if split[0] == len(chunks):
                break

    pair = [0]

    def run_block(b, j0):
        if b["need"] is not None:
            b["need"]()
        cur = pair[0] % 2
        pair[0] += 1
        ps = main[cur]
        free = main_free[cur]
        n, kt = b["n"], b["kt"]
        lhi, llo, ltok = b["lhs"]
        j = j0
        tok = None
        while True:
            ahead, q = 0, j
            while q + 1 < len(chunks) and ahead < LOOK:
                q += 1
                if chunks[q][0] == "w":
                    ahead += 1
            kind, cb, k0, m = chunks[j]
            if kind == "mod":
                j += 1
                continue
            assert cb is b
            ahead = q
            ensure(ahead, 0)
            q = wslot[j]
            wh = whi[:, q, 0:m * n].rearrange("p (k n) -> p k n", n=n)
            wl = wlo[:, q, 0:m * n].rearrange("p (k n) -> p k n", n=n)
            parts = halves(m)
            for pi, (ka, kb) in enumerate(parts):
                fs = []
                if pi == len(parts) - 1:
                    ensure(ahead, 1)
                aft = [w_tok[(j, pi)]]
                if k0 + ka == 0:
                    aft += list(free)
                for kk in range(ka, kb):
                    k = k0 + kk
                    last = k == kt - 1
                    aft += ltok(k)
                    if b["orient"] == "TM":
                        for i in range(2):
                            o = ps[i][:, 0:n]
                            a = slice(128 * i, 128 * i + 128)
                            fs.append(mm(o, lhi(k)[:, a], wh[:, kk, :], start=(k == 0), stop=False))
                            fs.append(mm(o, lhi(k)[:, a], wl[:, kk, :], start=False, stop=False))
                            fs.append(mm(o, llo(k)[:, a], wh[:, kk, :], start=False, stop=last))
                    else:
                        for ct in range(n // 128):
                            o = ps[ct // 2][:, 256 * (ct % 2):256 * (ct % 2) + 256]
                            a = slice(128 * ct, 128 * ct + 128)
                            fs.append(mm(o, wh[:, kk, a], lhi(k), start=(k == 0 and ct % 2 == 0), stop=False))
                            fs.append(mm(o, wh[:, kk, a], llo(k), start=False, stop=False))
                            fs.append(mm(o, wl[:, kk, a], lhi(k), start=False, stop=last))
                tok = PE.op(mms(*fs), aft)
                if k0 + kb < kt:
                    if pi == len(parts) - 1:
                        w_free[q] = [tok]
                    step_jobs()
            w_free[q] = [tok]
            j += 1
            if k0 + m == kt:
                break
        main_free[cur] = b["evac"](ps, tok)
        step_jobs()
        return j

    macc = sb("macc", [128, 2, 512])
    mst = {"free": [[], []], "tok": None, "c": None, "n": 0}
    mod_done = {}
    GB = carve(12288 + 3072, D)

    def add_mod(layer, blk):
        b = dict(w=t["w_mod_2"][layer], c0=512 * blk, n=512, kt=KT, dup=False, layer=layer, blk=blk)
        return [("mod", b, 4 * q, 4) for q in range(4)]

    def mod_step(b, k0, m, w, tok):
        i = mst["n"] % 2
        a = macc[:, i, :]
        last = None
        for kk in range(m):
            k = k0 + kk
            if k == 0:
                assert mst["free"][i] is not None
                last = DV.op(ts(a, w[:, 0, :], c2[:, 0:1], MUL), [tok, *mst["free"][i], mst["c"]])
                mst["free"][i] = None
            else:
                last = DV.op(stt(a, w[:, kk, :], c2[:, k:k + 1], a, MUL, ADD), [tok, mst["tok"]])
            mst["tok"] = last
        if k0 + m == KT:
            mst["n"] += 1
            short.append(mod_end(b, i, last))
        return last

    def mod_end(b, i, tok):
        L, blk = b["layer"], b["blk"]
        a = macc[:, i, :]
        yield 8
        p, w = take()
        if blk < 8:
            t_ = PE.op(mms(*[mm(p[:, j:j + 1], a[:, 128 * j:128 * j + 128], ones[:, 0:1]) for j in range(4)]),
                       [tok, *w])
            e = DV.op(tt(modcm[:, L, 4 * blk:4 * blk + 4], p[:, 0:4], cols("bmod", 48 * L + 4 * blk, 4), ADD), [t_])
        else:
            g = GB[:, 512 * (blk - 8):512 * (blk - 8) + 512]
            t_ = PE.op(mm(p[:, :], ones, a), [tok, *w])
            e = DV.op(tt(g, p[:, :], g, ADD), [t_, gate_loaded[L]])
        mst["free"][i] = [t_]
        give(p, e)
        mod_done[(L, blk)] = e

    gate_loaded = {}

    def copy_out(dst, src, after, scale=1.0):
        return AC.op(act(dst, src, ACT.Copy, scale=scale), after)

    h_ops = ((lambda k: hhi[:, k, :]), (lambda k: hlo[:, k, :]), (lambda k: [state["h"][k // 2]]))

    GQ, GK, GV = carve(0, 8, S), carve(2048, 8, S), carve(4096, 8, S)
    MQ, MK, MV = carve(6144, 8, S), carve(8192, 8, S), carve(10240, 2, GW)
    ZS = carve(12288, 2, GW)
    GBT = carve(8192, KT, S)
    YA = carve(4096, 8, 2, S, dt=BF16)
    YB = carve(6144, 8, 2, S, dt=BF16)
    MHI, MLO = carve(0, KT, S, dt=BF16), carve(2048, KT, S, dt=BF16)
    LANE = [14336, 14336 + 4096]

    tk = {}
    ROPEW = [carve(15360 + 256 * i, S) for i in range(4)]

    def rope_table(posint, inv, sgn, after, work):
        posf, a, n_, r_ = work
        q = DV.op(cp(posf, posint), after)
        q = DV.op(ts(a, posf, inv, MUL), [q, t_cst])
        q = DV.op(ts(n_, a, 1.0 / (2 * math.pi), MUL, 12582912.0, ADD), [q])
        q = DV.op(ts(n_, n_, 12582912.0, SUB), [q])
        src = a
        for c in TWO_PI:
            q = DV.op(stt(r_, n_, -c, src, MUL, ADD), [q])
            src = r_
        q0 = DV.op(ts(r_, r_, math.pi, MIN, -math.pi, MAX), [q])
        q = DV.op(ts(a, r_, math.pi / 2, ADD), [q0])
        q = DV.op(ts(n_, a, math.pi, ALU.is_gt, -2 * math.pi, MUL), [q])
        q = DV.op(tt(a, a, n_, ADD), [q])
        q = DV.op(ts(a, a, math.pi, MIN, -math.pi, MAX), [q])
        q1 = AC.op(act(cs[:, 1, :], r_, ACT.Sin), [q0])
        q = AC.op(act(cs[:, 0, :], a, ACT.Sin), [q])
        q2 = DV.op(ts(cs[:, 1, :], cs[:, 1, :], sgn, MUL), [q1])
        return [q, q2]

    early = []
    setup = {}

    def vt_columns(k, after):
        r = min(128, vrow[0] - 128 * k)
        b, w = take()
        t_ = PE.op(tp(b[:, 0:r], vst[0:r, k, :], ident[0:r, 0:r]), [t_cst, *after, *w])
        e_ = AC.op(act(VT[:, 128 * k:128 * k + r], b[:, 0:r], ACT.Copy), [t_])
        give(b, e_)
        return e_

    def first_norm():
        sq0 = [sumsq(i, j, [t_x[i]]) for i in range(2) for j in range(4)]
        vt0 = vt_columns(0, [t_v0])
        for j in range(2):
            for _ in xpose(j, DV):
                pass
        r = rstd_of(sq0)
        for j in range(2, 4):
            for _ in xpose(j, DV):
                pass
        setup["row"], setup["v"] = later_loads()
        norm_to_h(lambda k: col("ln1", k), None, r, [vt0], {0: (0, 0), 2: (0, 1), 6: (1, 0), 8: (1, 1), 12: (2, 1)})
        early.append(vt0)
        short.append(setup_job(setup["row"], setup["v"]))

    def setup_job(row, tv):
        yield 2
        for k in range(1, (vrow[0] + 127) // 128):
            vt = vt_columns(k, [tv])
            if k % 2 == 0:
                yield
        early.append(vt)
        yield
        early.append(AC.op(act(lev[:, :, :], levf, ACT.Copy), [row]))
        q = AC.op(act(gsc, cols("c", 0, 16), ACT.Tanh, scale=0.5), [vt])
        q = DV.op(stt(c2, gsc, 1.0, cols("c", 0, 16), ADD, MUL), [q])
        mst["c"] = DV.op(ts(c2, c2, 0.5, MUL), [q])
        early.append(mst["c"])
        yield
        early.extend(rope_table(pos_i, cst[:, C_INV1:C_INV1 + 1], cst[:, C_SG1:C_SG1 + 1], [row, t_cst],
                                [carve(1280 + 256 * i, S) for i in range(4)]))
        setup["done"] = True

    def swap_rope(dst, blk):
        def evac(ps, tok):
            free = []
            assert "done" in setup
            for hf in range(2):
                si, s_, w = stage()
                e = copy_out(s_, ps[hf][:, :], [tok, *w])
                free.append(e)
                short.append(job(si, s_, e, 4 * blk + 2 * hf))
            return free

        def job(si, s_, e, h):
            sv = s_.rearrange("p (h s) -> p h s", h=2)
            d = dst[:, h:h + 2, :]
            m = DV.op(tt(d, sv, mid(cs[:, 0, :], 2), MUL), [e, *early])
            yield 2
            b, w = take()
            p = PE.op(mm(b[0:32, :], cst[0:32, C_PERM:C_PERM + 32], s_[0:32, :]), [e, *w])
            s2, s2_, w2 = stage()
            u = DV.op(tt(s2_[0:32, :].rearrange("p (h s) -> p h s", h=2),
                         b[0:32, :].rearrange("p (h s) -> p h s", h=2), mid(cs[0:32, 1, :], 2), MUL), [p, *w2])
            give(b, u)
            v = DV.op(tt(d[0:32, :, :], d[0:32, :, :], s2_[0:32, :].rearrange("p (h s) -> p h s", h=2), ADD), [u, m])
            unstage(si, m, p)
            unstage(s2, v)
            tk[("rope", id(dst), h // 2)] = v
            yield
        return evac

    def tm_copy(dst, c0, name, idx):
        def evac(ps, tok):
            f = [copy_out(dst[:, i, c0:c0 + 512], ps[i][:, :], [tok, *early]) for i in range(2)]
            tk[(name, idx)] = f
            return f
        return evac

    for blk in range(2):
        add(t["w_in"][0], 4112 + 512 * blk, 512, KT, "CM", h_ops, swap_rope(MQ, blk), None if blk else first_norm)
        add(t["w_in"][0], 5136 + 512 * blk, 512, KT, "CM", h_ops, swap_rope(MK, blk))
        add(t["w_in"][0], 6160 + 512 * blk, 512, KT, "TM", h_ops, tm_copy(MV, 512 * blk, "mv", blk))

    def softmax_rows(L0, L1, e0, e1, n, mcol, rcol, scale):
        a0 = DV.op(red(mcol[:, 0:n], L0, MAX), [e0])
        a1 = DV.op(red(mcol[:, n:2 * n], L1, MAX), [e1])
        a = DV.op(ts(mcol, mcol, -scale, MUL), [a0, a1])
        yield
        for h in range(n):
            x0 = AC.op(act(L0[:, h, :], L0[:, h, :], ACT.Exp, bias=mcol[:, h:h + 1], scale=scale,
                           acc=rcol[:, h:h + 1]), [a])
            x1 = AC.op(act(L1[:, h, :], L1[:, h, :], ACT.Exp, bias=mcol[:, n + h:n + h + 1], scale=scale,
                           acc=rcol[:, n + h:n + h + 1]), [a])
        yield
        r = DV.op(recip(rcol, rcol), [x1])
        n0 = GP.op(tt(L0, L0, rep(rcol[:, 0:n], 128), MUL), [r])
        n1 = DV.op(tt(L1, L1, rep(rcol[:, n:2 * n], 256), MUL), [r])
        return n0, n1

    lane_free = [[], []]

    def split_out(dst, h, src, after):
        sv = src.rearrange("p (h s) -> p h s", h=2)
        a = AC.op(act(dst[:, h:h + 2, 0, :], sv, ACT.Copy), after)
        yield
        return DV.op(tt(dst[:, h:h + 2, 1, :], sv, dst[:, h:h + 2, 0, :], SUB), [a])

    def attend_pv(L0, L1, n0, n1, v0, v1, lane, base):
        b0, w0 = take()
        b1, w1 = take()
        PT0, PT1 = carve(base + 1024, 2, 256), carve(base + 1536, 2, 128)
        fs = []
        for h in range(2):
            fs.append(tp(b0[:, 256 * h:256 * h + 128], L0[:, h, :], ident))
            fs.append(tp(b0[:, 256 * h + 128:256 * h + 256], L1[:, h, 0:128], ident))
            fs.append(tp(b1[:, 128 * h:128 * h + 128], L1[:, h, 128:256], ident))
        p = PE.op(mms(*fs), [n0, n1, *w0, *w1])
        c0 = copy_out(PT0, b0[:, :].rearrange("p (h s) -> p h s", h=2), [p, *lane_free[lane]])
        c1 = copy_out(PT1, b1[:, 0:256].rearrange("p (h s) -> p h s", h=2), [p])
        give(b0, c0)
        give(b1, c1)
        return PT0, PT1, p, [c0, c1]

    def moba(hp):
        lane = hp % 2
        base = LANE[lane]
        h0 = 2 * hp
        L0, L1 = carve(base, 2, 128), carve(base + 256, 2, 256)
        sml = lane_sm[lane]
        mcol, rcol = sml[:, 0:4], sml[:, 4:8]
        b0, w0 = take()
        b1, w1 = take()
        fs = []
        for h in range(2):
            fs.append(mm(b0[:, 128 * h:128 * h + 128], MQ[:, h0 + h, 0:128], MK[:, h0 + h, 0:128]))
            fs.append(mm(b1[:, 256 * h:256 * h + 256], MQ[:, h0 + h, 128:256], MK[:, h0 + h, :]))
        p = PE.op(mms(*fs), [tk[("rope", id(MQ), hp)], tk[("rope", id(MK), hp)], *w0, *w1])
        e0 = DV.op(tt(L0, b0[:, 0:256].rearrange("p (h s) -> p h s", h=2), mid(causal[:, 128:256], 2), ADD),
                   [p, *lane_free[lane]])
        e1 = DV.op(tt(L1, b1[:, :].rearrange("p (h s) -> p h s", h=2), mid(causal, 2), ADD), [p, *lane_free[lane]])
        give(b0, e0)
        give(b1, e1)
        yield
        n0, n1 = yield from softmax_rows(L0, L1, e0, e1, 2, mcol, rcol, 128.0 ** -0.5)
        yield 4
        PT0, PT1, pt, cc = attend_pv(L0, L1, n0, n1, None, None, lane, base)
        yield 2
        b, w = take()
        fs = []
        for h in range(2):
            sl = slice(128 * (h0 + h), 128 * (h0 + h) + 128)
            fs.append(mm(b[:, 256 * h:256 * h + 256], MV[:, 0, sl], PT0[:, h, :], start=(h == 0), stop=False))
            fs.append(mm(b[:, 256 * h + 128:256 * h + 256], MV[:, 1, sl], PT1[:, h, :], start=False, stop=True))
        p = PE.op(mms(*fs), [*cc, *w, *tk[("mv", h0 // 4)]])
        si, s_, w = stage()
        e = copy_out(s_, b[:, :], [p, *w])
        give(b, e)
        o = yield from split_out(YB, h0, s_, [e])
        unstage(si, o)
        lane_free[lane] = [p]
        tk[("yb", hp)] = o
        tk[("moba_read", hp)] = [p]
        yield

    def conv_block(kind, blk):
        dst = {"q": GQ, "k": GK, "v": GV}[kind]
        ch0 = {"q": 0, "k": 8, "v": 16}[kind]

        def evac(ps, tok):
            free = []
            for hf in range(2):
                si, s_, w = stage()
                e = copy_out(s_, ps[hf][:, :], [tok, *w])
                free.append(e)
                short.append(job(si, s_, e, 4 * blk + 2 * hf))
            return free

        def job(si, s_, e, h):
            d = dst[:, h:h + 2, :]
            for q_ in range(2):
                x_ = s_[:, 256 * q_:256 * q_ + 256]
                y_ = d[:, q_, :]
                wt = lambda i: col("conv", 24 * i + ch0 + h + q_)
                c_ = DV.op(ts(y_, x_, wt(3), MUL), [e, *early])
                for i in range(3):
                    sh = 3 - i
                    c_ = DV.op(stt(y_[:, sh:S], x_[:, 0:S - sh], wt(i), y_[:, sh:S], MUL, ADD), [c_])
            unstage(si, c_)
            yield
            dv = d.rearrange("p h s -> p (h s)")
            s2, s2_, w2 = stage()
            a = AC.op(act(s2_, dv, ACT.Tanh, scale=0.5), [c_, *w2])
            yield
            f = DV.op(stt(dv, s2_, 1.0, dv, ADD, MUL), [a])
            if kind == "v":
                unstage(s2, f)
                tk[("gv", h // 2)] = f
                return
            g = GP.op(tt(s2_, dv, dv, MUL), [f])
            yield 3
            b, w = take()
            p = PE.op(mms(*[mm(b[:, u:u + 1], s2_[:, 128 * u:128 * u + 128], ones[:, 0:1]) for u in range(4)]), [g, *w])
            yield 2
            if kind == "q":
                a = AC.op(act(s2_[:, 0:4], b[:, 0:4], ACT.Sqrt, bias=eps512_c, scale=128.0), [p, t_eps])
            else:
                a = AC.op(act(s2_[:, 0:4], b[:, 0:4], ACT.Sqrt, bias=eps4_c, scale=1.0), [p, t_eps])
            give(b, a)
            yield
            r = DV.op(recip((rq if kind == "q" else rk)[:, 2 * h:2 * h + 4], s2_[:, 0:4]), [a])
            unstage(s2, r)
            tk[("g" + kind, h // 2)] = r
        return evac

    def evac_bd(ps, tok):
        es = [copy_out(bd[:, i, :], ps[i][:, 0:16], [tok]) for i in range(2)]
        short.append(job_bd(es))
        return es

    def job_bd(es):
        a = AC.op(act(bet, bd[:, :, 0:8], ACT.Tanh, scale=0.5), es)
        tk["bet"] = DV.op(ts(bet, bet, 1.0, ADD, 0.5, MUL), [a])
        z = DV.op(tt(tA, bd[:, :, 8:16], mid(dtb, 2), ADD), [*es, setup["row"]])
        n_ = DV.op(ts(tB, tA, -1.0, MUL), [z])
        n_ = DV.op(tt(tB, tB, tA, MAX), [n_])
        n_ = AC.op(act(tB, tB, ACT.Exp, scale=-1.0), [n_])
        n_ = AC.op(act(tB, tB, ACT.Ln, bias=ones[:, 0:1]), [n_, t_cst])
        z = DV.op(ts(tA, tA, 0.0, MAX), [z, n_])
        z = DV.op(tt(tA, tA, tB, ADD), [z])
        ea = AC.op(act(alog, alog, ACT.Exp), [setup["row"]])
        g = DV.op(stt(gd, tA, -1.0, mid(alog, 2), MUL, MUL), [z, ea])
        tk["g"] = g
        yield 3
        b, w = take()
        p = PE.op(mm(b[:, 0:16], tri, gd.rearrange("p n c -> p (n c)")), [g, *w])
        v = DV.op(ts(gcn, b[:, 0:16].rearrange("p (n c) -> p n c", n=2), -1.0, MUL), [p])
        give(b, v)
        x_ = AC.op(act(eg, gcn, ACT.Exp, scale=-1.0), [v])
        tk["gcn"] = v
        tk["eg"] = x_
        tk["beg"] = DV.op(tt(beg, bet[:, 1, :], eg[:, 1, :], MUL), [x_, tk["bet"]])
        yield

    def gdn(bt):
        lane = bt % 2
        base = LANE[lane]
        h0 = 2 * bt
        GM, AT, XT, XX, PP, AL, QK, VB = (carve(base + 512 * i, 4, 128) for i in range(8))
        KX = GM
        sml = lane_sm[lane]
        gl, ekd, oss, orr = sml[:, 0:2], sml[:, 2:4], sml[:, 4:8], sml[:, 8:12]
        bk, egq = sml[:, 12:16], sml[:, 16:18]
        rk4, rq4 = rk[:, 4 * bt:4 * bt + 4], rq[:, 4 * bt:4 * bt + 4]
        U = [(u, h0 + u // 2, u % 2, slice(128 * (u % 2), 128 * (u % 2) + 128)) for u in range(4)]
        fl = lambda a: a.rearrange("p a b -> p (a b)")
        lw = lane_free[lane]
        B = lambda b, u: b[:, 128 * u:128 * u + 128]
        bkt = DV.op(tt(bk.rearrange("p (h n) -> p h n", n=2), bet[:, :, h0:h0 + 2].rearrange("p n h -> p h n"),
                       rk4.rearrange("p (h n) -> p h n", n=2), MUL), [tk["bet"], tk[("gk", bt)], *lw])
        eq = DV.op(tt(egq, eg[:, 1, h0:h0 + 2], rq4.rearrange("p (h n) -> p h n", n=2)[:, :, 1], MUL),
                   [tk["eg"], tk[("gq", bt)], *lw])
        yield 2
        b1, w1 = take()
        b2, w2 = take()
        p1 = PE.op(mms(*[mm(B(b1, u), gd[:, n, h:h + 1].to_broadcast([128, 128]), tri) for u, h, n, c in U]),
                   [tk["g"], *w1])
        p2 = PE.op(mms(*[mm(B(b2, u), bk[:, u:u + 1].to_broadcast([128, 128]), ident) for u, h, n, c in U]),
                   [bkt, *w2])
        for u, h, n, c in U:
            m = DV.op(stt(GM[:, u, :], B(b1, u), gcn[:, n, h:h + 1], gmask, ADD, ADD), [p1, tk["gcn"], *lw])
        gl_t = DV.op(cp(gl, b1[:, :].rearrange("p (a b) -> p a b", a=4)[:, 0:4:2, 127]), [p1])
        br = copy_out(fl(PP), b2[:, :], [p2, *lw])
        give(b1, gl_t)
        give(b2, br)
        yield
        ex = AC.op(act(fl(GM), fl(GM), ACT.Exp), [m])
        for q_ in range(2):
            ek = AC.op(act(ekd[:, q_:q_ + 1], gcn[:, 0, h0 + q_:h0 + q_ + 1], ACT.Exp, bias=gl[:, q_:q_ + 1]), [gl_t])
        yield
        b1, w1 = take()
        b2, w2 = take()
        p1 = PE.op(mms(*[mm(B(b1, u), GK[:, h, c], GK[:, h, c]) for u, h, n, c in U]), [tk[("gk", bt)], *w1])
        p2 = PE.op(mms(*[mm(B(b2, u), GK[:, h, c], GQ[:, h, c]) for u, h, n, c in U]), [tk[("gq", bt)], *w2])
        for u in range(4):
            a = DV.op(stt(AT[:, u, :], B(b1, u), rk4[:, u:u + 1], GM[:, u, :], MUL, MUL), [p1, ex, *lw])
        for u in range(4):
            qk = DV.op(stt(QK[:, u, :], B(b2, u), rk4[:, u:u + 1], GM[:, u, :], MUL, MUL), [p2, ex, *lw])
        at = GP.op(tt(fl(AT), fl(AT), fl(PP), MUL), [a, br])
        al = GP.op(tt(AL, AT, mid(lev[:, 0, :], 4), MUL), [at, *early, *lw])
        give(b1, a)
        give(b2, qk)
        yield
        b1, w1 = take()
        b2, w2 = take()
        p1 = PE.op(mms(*[tp(B(b1, u), GV[:, h, c], ident) for u, h, n, c in U]), [tk[("gv", bt)], *w1])
        p2 = PE.op(mms(*[tp(B(b2, u), GK[:, h, c], ident) for u, h, n, c in U]), w2)
        for u, h, n, c in U:
            vb = DV.op(ts(VB[:, u, :], B(b1, u), bet[:, n, h:h + 1], MUL, 0.5, MUL), [p1, tk["bet"], *lw])
            sc = ekd[:, u // 2:u // 2 + 1] if n == 0 else beg[:, h:h + 1]
            kx = DV.op(ts(KX[:, u, :], B(b2, u), sc, MUL, rk4[:, u:u + 1], MUL), [p2, ek, qk, a, tk["beg"]])
        give(b1, vb)
        give(b2, kx)
        xt = DV.op(tt(XT, mid(ident, 4), AL, SUB), [al, *lw])
        al_free = xt
        yield 2
        al = GP.op(tt(AL, AT, mid(lev[:, 1, :], 4), MUL), [al_free])
        b1, w1 = take()
        p1 = PE.op(mms(*[tp(B(b1, u), XT[:, u, :], ident) for u in range(4)]), [xt, *w1])
        xx = copy_out(fl(XX), b1[:, :], [p1, *lw])
        give(b1, xx)
        half = lambda v, c, b: v.rearrange("p (m c b) -> p m c b", c=2, b=b)[:, :, c, :]
        pz = at
        for l in range(1, 7):
            b = 1 << l
            flat = lambda v: v.rearrange("p (m b) -> p m b", b=b)
            zero = GP.op(lambda e: e.memset(fl(PP), 0.0), [pz])
            yield
            b1, w1 = take()
            p1 = PE.op(mms(*[mm(flat(b1[:, 64 * u:64 * u + 64]), AL[:, u, :], half(XX[:, u, :], 0, b))
                             for u in range(4)]), [al, xx, *w1])
            pp = copy_out(half(fl(PP), 0, b), flat(b1[:, 0:256]), [p1, zero])
            give(b1, pp)
            if l < 6:
                al = GP.op(tt(AL, AT, mid(lev[:, l + 1, :], 4), MUL), [p1])
            else:
                al = p1
            yield
            b1, w1 = take()
            pz = PE.op(mms(*[mm(flat(b1[:, 64 * u:64 * u + 64]), PP[:, u, :], half(XT[:, u, :], 1, b))
                             for u in range(4)]), [pp, xt, *w1])
            if l < 6:
                pz = PE.op(mms(*[mm(flat(b1[:, 256 + 64 * u:320 + 64 * u]), XT[:, u, :], half(PP[:, u, :], 0, b))
                                 for u in range(4)]))
            xt = DV.op(tt(half(fl(XT), 1, b), half(fl(XT), 1, b), flat(b1[:, 0:256]), SUB), [pz])
            last = xt
            if l < 6:
                last = xx = DV.op(tt(half(fl(XX), 0, b), half(fl(XX), 0, b), flat(b1[:, 256:512]), SUB), [pz])
            give(b1, last)
        yield
        VN, WT, SS, QS = AT, XX, AL, PP
        b1, w1 = take()
        b2, w2 = take()
        p1 = PE.op(mms(*[mm(B(b1, u), XT[:, u, :], VB[:, u, :]) for u in range(4)]), [xt, vb, *w1])
        p2 = PE.op(mms(*[mm(B(b2, q_), KX[:, 2 * q_ + 1, :], XT[:, 2 * q_ + 1, :]) for q_ in range(2)]), [kx, *w2])
        vn = copy_out(fl(VN), b1[:, :], [p1, al])
        wt = copy_out(fl(WT)[:, 0:256], b2[:, 0:256], [p2])
        give(b1, vn)
        give(b2, wt)
        yield
        b1, w1 = take()
        p1 = PE.op(mms(*[mm(B(b1, q_), KX[:, 2 * q_, :], VN[:, 2 * q_, :]) for q_ in range(2)]), [vn, *w1])
        ss = copy_out(fl(SS)[:, 0:256], b1[:, 0:256], [p1, al])
        give(b1, ss)
        yield
        b1, w1 = take()
        b2, w2 = take()
        p2 = PE.op(mms(*[mm(B(b2, q_), WT[:, q_, :], SS[:, q_, :]) for q_ in range(2)]), [wt, ss, *w2])
        p1 = PE.op(mms(*[mm(B(b1, q_), GQ[:, h0 + q_, 128:256], SS[:, q_, :]) for q_ in range(2)]), w1)
        for q_ in range(2):
            v1 = DV.op(tt(VN[:, 2 * q_ + 1, :], VN[:, 2 * q_ + 1, :], B(b2, q_), SUB), [p2, vn])
            qs = AC.op(act(QS[:, q_, :], B(b1, q_), ACT.Copy, scale=egq[:, q_:q_ + 1]), [p1, eq])
        give(b1, qs)
        give(b2, v1)
        yield
        b2, w2 = take()
        p2 = PE.op(mms(*[mm(B(b2, u), QK[:, u, :], VN[:, u, :]) for u in range(4)]), [v1, *w2])
        O = XT
        o4 = b2[:, :].rearrange("p (h n d) -> p h n d", h=2, n=2)
        Ov = O.rearrange("p (h n) d -> p h n d", h=2)
        for q_ in range(2):
            o0 = DV.op(ts(Ov[:, q_, 0, :], o4[:, q_, 0, :], rq4[:, 2 * q_:2 * q_ + 1], MUL), [p2])
            o1 = DV.op(stt(Ov[:, q_, 1, :], o4[:, q_, 1, :], rq4[:, 2 * q_ + 1:2 * q_ + 2], QS[:, q_, :], MUL, ADD),
                       [p2, qs])
        give(b2, o1)
        sq = GP.op(tt(fl(VB), fl(O), fl(O), MUL), [o0, o1])
        yield
        r = DV.op(red(oss, VB, ADD), [sq])
        yield
        r = AC.op(act(orr, oss, ACT.Sqrt, bias=eps_c, scale=1.0 / 128), [r, t_eps])
        yield
        r = DV.op(recip(orr, orr), [r])
        for u, h, n, c in U:
            og = DV.op(stt(O[:, u, :], O[:, u, :], orr[:, u:u + 1], ZS[:, n, 128 * h:128 * h + 128], MUL, MUL),
                       [r, sq, *tk[("zs", h // 4)]])
        yield 4
        b1, w1 = take()
        p1 = PE.op(mms(*[tp(B(b1, u), O[:, u, :], ident) for u in range(4)]), [og, *w1])
        si, s_, w = stage()
        e = DV.op(ts(s_, b1[:, :], col("gn", 0), MUL, 0.5, MUL), [p1, *w])
        give(b1, e)
        yield
        o = yield from split_out(YA, h0, s_, [e])
        unstage(si, o)
        lane_free[lane] = [p1, o]
        tk[("ya", bt)] = o

    def z_evac(blk):
        def evac(ps, tok):
            f = []
            for i in range(2):
                si, s_, w = stage()
                e = copy_out(s_, ps[i][:, :], [tok, *w])
                f.append(e)
                short.append(job(si, s_, e, i))
            return f

        def job(si, s_, e, i):
            z_ = ZS[:, i, 512 * blk:512 * blk + 512]
            a = AC.op(act(z_, s_, ACT.Tanh, scale=0.5), [e, *early])
            r = DV.op(stt(z_, z_, 1.0, s_, ADD, MUL), [a])
            unstage(si, r)
            tk.setdefault(("zs", blk), []).append(r)
            yield
        return evac

    def launch(*gens):
        return lambda: long.extend(gens)

    def qkv(blk, need):
        for kind, c0 in (("q", 0), ("k", 1024), ("v", 2048)):
            add(t["w_in"][0], c0 + 512 * blk, 512, KT, "CM", h_ops, conv_block(kind, blk), need)
            need = None

    add(t["w_in"][0], 3072, 16, KT, "TM", h_ops, evac_bd, launch(moba(0), moba(1), moba(2), moba(3)))
    qkv(0, None)
    for blk in range(2):
        b_z1 = add(t["w_in"][0], 3088 + 512 * blk, 512, KT, "TM", h_ops, z_evac(blk),
                   None if blk else launch(gdn(0), gdn(1)))
    qkv(1, None)

    def gb_evac(blk):
        def evac(ps, tok):
            f = []
            for hf in range(2):
                f.append(AC.op(act(GBT[:, 4 * blk + 2 * hf:4 * blk + 2 * hf + 2, :].rearrange("p a s -> p (a s)"),
                                   ps[hf][:, :], ACT.Tanh, scale=0.5), [tok, *[x for hp in range(4)
                                                                            for x in tk[("moba_read", hp)]]]))
            tk[("gb", blk)] = f
            return f
        return evac

    b_gb = [add(t["w_in"][0], 9232 + 512 * blk, 512, KT, "CM", h_ops, gb_evac(blk),
                launch(gdn(2), gdn(3)) if blk == 1 else None) for blk in range(4)]

    merge = {}

    def ga_evac(blk):
        def evac(ps, tok):
            f = []
            for hf in range(2):
                si, s_, w = stage()
                e = AC.op(act(s_, ps[hf][:, :], ACT.Tanh, scale=0.5), [tok, *w])
                f.append(e)
                merge[(blk, hf)] = (si, s_, e)
            return f
        return evac

    def yb_evac(blk):
        def evac(ps, tok):
            f = []
            for hf in range(2):
                k = 4 * blk + 2 * hf
                g = GBT[:, k:k + 2, :].rearrange("p a s -> p (a s)")
                f.append(DV.op(stt(g, g, 1.0, ps[hf][:, :], ADD, MUL), [tok, *tk[("gb", blk)]]))
                tk[("gyb", k)] = f[-1]
            return f
        return evac

    def ya_evac(blk):
        def evac(ps, tok):
            f = []
            for hf in range(2):
                k = 4 * blk + 2 * hf
                si, s_, e = merge[(blk, hf)]
                m = DV.op(stt(s_, s_, 1.0, ps[hf][:, :], ADD, MUL), [tok, e])
                f.append(m)
                g = GBT[:, k:k + 2, :].rearrange("p a s -> p (a s)")
                short.append(job(si, s_, GP.op(tt(s_, s_, g, ADD), [m, tk[("gyb", k)]]), k))
            return f

        def job(si, s_, y, k):
            hv, lv = (v[:, k:k + 2, :].rearrange("p a s -> p (a s)") for v in (MHI, MLO))
            yield
            a = AC.op(act(hv, s_, ACT.Copy), [y])
            yield
            l = DV.op(tt(lv, s_, hv, SUB), [a])
            unstage(si, l)
            tk[("merged", k // 2)] = l
        return evac

    def y_ops(Y, name):
        return (lambda k: Y[:, k, 0, :]), (lambda k: Y[:, k, 1, :]), (lambda k: [tk[(name, k // 2)]])

    for blk in range(4):
        add(t["w_branch_b"][0], 512 * blk, 512, 8, "CM", y_ops(YB, "yb"), yb_evac(blk))
    for blk in range(4):
        add(t["w_in"][0], 7184 + 512 * blk, 512, KT, "CM", h_ops, ga_evac(blk))
        add(t["w_branch_a"][0], 512 * blk, 512, 8, "CM", y_ops(YA, "ya"), ya_evac(blk),
            finish_all if blk == 0 else None)

    def resid(blk, half):
        def evac(ps, tok):
            f = []
            for i in range(2):
                xs = X[:, i, 512 * blk:512 * blk + 512]
                e = DV.op(stt(xs, ps[i][:, :], half, xs, MUL, ADD), [tok])
                f.append(e)
                state["x"][i][blk] = e
                state["sq"].append(sumsq(i, blk, [e]))
            xpose_later(blk)
            return f
        return evac

    m_ops = ((lambda k: MHI[:, k, :]), (lambda k: MLO[:, k, :]), (lambda k: [tk[("merged", k // 2)]]))

    def clear_sq():
        state["sq"] = []

    for blk in range(4):
        add(t["w_out"][0], 512 * blk, 512, KT, "TM", m_ops, resid(blk, 0.5),
            clear_sq if blk == 0 else sqrt_ahead if blk == 3 else None)

    AHI, ALO = carve(0, FT, S, dt=BF16), carve(5632, FT, S, dt=BF16)
    SG = carve(11264, 4, S)
    B0, B1 = carve(12288, 8, 128), carve(13312, 8, 256)

    def ffn_need():
        norm_to_h(lambda k: col("ln2", k), None, rstd_of(state["sq"]), early)

    def start_bias():
        long.append(bias_job([state["h"][-1]]))
        long.append(rope2_job([state["h"][-1]]))

    fst = {"sg": [], "sgr": [], "uv": []}

    def up_evac(val, j):
        def evac(ps, tok):
            f = []
            for hf in range(2):
                si, s_, w = stage()
                e = copy_out(s_, ps[hf][:, :], [tok, *w])
                f.append(e)
                short.append(job(si, s_, e, hf))
            return f

        def job(si, s_, e, hf):
            s2, s2_, w2 = stage()
            dst = s2_
            for q_ in range(2):
                ch = (FT if val else 0) + 4 * j + 2 * hf + q_
                x_ = s_[:, 256 * q_:256 * q_ + 256]
                y_ = dst[:, 256 * q_:256 * q_ + 256]
                wt = lambda i: col("fconv", 88 * i + ch)
                c_ = DV.op(ts(y_, x_, wt(2), MUL, col("fbias", ch), ADD), [e, *w2])
                for i in range(2):
                    sh = 2 - i
                    c_ = DV.op(stt(y_[:, sh:S], x_[:, 0:S - sh], wt(i), y_[:, sh:S], MUL, ADD), [c_])
            g = SG[:, 2 * hf:2 * hf + 2, :].rearrange("p a s -> p (a s)")
            if not val:
                yield
                a = AC.op(act(s_, dst, ACT.Tanh, scale=0.5), [c_])
                yield
                r = DV.op(stt(g, s_, 1.0, dst, ADD, MUL), [a, fst.get(("free", hf))])
                fst[("sg", hf)] = r
                unstage(si, r)
                unstage(s2, r)
            else:
                unstage(si, c_)
                r = GP.op(tt(s2_, s2_, g, MUL), [c_, fst[("sg", hf)]])
                fst[("free", hf)] = r
                k = 4 * j + 2 * hf
                hv, lv = (v[:, k:k + 2, :].rearrange("p a s -> p (a s)") for v in (AHI, ALO))
                yield
                a = AC.op(act(hv, s2_, ACT.Copy), [r])
                yield
                l = DV.op(tt(lv, s2_, hv, SUB), [a])
                unstage(s2, l)
                tk[("act", k // 2)] = l
        return evac

    b_up = []
    for j in range(11):
        b_up.append(add(t["w_up"][0], 512 * j, 512, KT, "CM", h_ops, up_evac(False, j),
                        ffn_need if j == 0 else start_bias if j == 2 else None))
        b_up.append(add(t["w_up"][0], DFF + 512 * j, 512, KT, "CM", h_ops, up_evac(True, j)))

    a_ops = ((lambda k: AHI[:, k, :]), (lambda k: ALO[:, k, :]), (lambda k: [tk[("act", k // 2)]]))

    def down_evac(blk):
        def evac(ps, tok):
            f = []
            for i in range(2):
                xs = X[:, i, 512 * blk:512 * blk + 512]
                e = DV.op(stt(xs, ps[i][:, :], 0.5, xs, MUL, ADD), [tok])
                f.append(e)
                q = sumsq(i, blk, [e])
                state["sq"].append(q)
                x_ = DV.op(tt(xs, xs, GB[:, 512 * blk:512 * blk + 512], MUL), [q, fn_tok[0]])
                state["x"][i][blk] = x_
                state["sqf"].append(sumsq(i, blk, [x_], ssf))
            xpose_later(blk)
            return f
        return evac

    fn_tok = [None]

    def down_need():
        state["sq"] = []
        fn_tok[0] = SP.dma(GB, t["final_norm"].partition_broadcast(128), s_fn, [state["h"][-1]])

    for blk in range(4):
        add(t["w_down"][0], 512 * blk, 512, FT, "TM", a_ops, down_evac(blk),
            down_need if blk == 0 else sqrt_ahead if blk == 3 else None)

    REL = carve(17408, 16, 128, dt=I32)
    STEP = carve(19456, 16, 128)
    PQR = carve(21504, S, dt=I32)
    PKC = carve(21760, 64, dt=I32)
    RBP, RBM = carve(21824, 8), carve(21832, 8)
    RBW = carve(21840, 4, 8)
    s_rb = Slot(sem("in_bias"))

    def bias_job(after):
        z = GP.op(lambda e: e.memset(RBM, 0.0), after)
        z = GP.op(lambda e: e.memset(RBW, 0.0), after)
        pos2 = t["positions_2"].rearrange("a s -> (a s)")
        SP.dma(PQR, pos2.partition_broadcast(128), s_rb, [z])
        for g in range(4):
            pp = slice(32 * g, 32 * g + 32)
            SP.dma(RBP[pp, :], t["rel_bias_2"], s_rb)
            SP.dma(RBM[32 * g + 1:32 * g + 32, :], t["rel_bias_2"][0:31, :], s_rb)
            for kb in range(2):
                r = SP.dma(PKC[pp, 32 * kb:32 * kb + 32],
                           pos2[128 * kb + 32 * g:128 * kb + 32 * g + 32].partition_broadcast(32), s_rb)
        yield 6
        d = DV.op(tt(RBP, RBP, RBM, SUB), [r])
        q = DV.op(lambda e: e.tensor_single_scalar(PKC, PKC, -1, ALU.bitwise_xor), [r])
        for g in range(4):
            pp = slice(32 * g, 32 * g + 32)
            w_ = DV.op(cp(RBW[pp, g, :], RBP[pp, :]), [d, z])
        rbw = RBW.rearrange("p g h -> p (g h)")
        pm = m = None
        ends = []
        for qt, kb in ((0, 0), (1, 0), (1, 1)):
            for jh in range(2):
                a = GP.op(tt(REL, mid(PQR[:, 128 * qt:128 * qt + 128], 16),
                             rep(PKC[:, 32 * kb + 16 * jh:32 * kb + 16 * jh + 16], 128), ADD), [q, r, m])
                yield 4
                m = DV.op(ts(STEP, REL, cst[:, C_THR:C_THR + 1], ALU.is_ge), [a, pm])
                yield 6
                b, w = take()
                pm = PE.op(mms(*[mm(b[:, 32 * j:32 * j + 32], STEP[:, j, :], rbw) for j in range(16)]), [m, w_, *w])
                dst = B0 if qt == 0 else B1
                c0 = 128 * kb + 16 * jh
                for g in range(4):
                    e = AC.op(act(dst[:, :, c0 + 32 * g:c0 + 32 * g + 16],
                                  b[:, :].rearrange("p (j g h) -> p g h j", g=4, h=8)[:, g, :, :], ACT.Copy), [pm])
                give(b, e)
                ends.append(e)
                yield
        tk["bias"] = ends

    def rope2_job(after):
        yield 12
        tk["rope2"] = rope_table(PQR, cst[:, C_INV2:C_INV2 + 1], cst[:, C_SG2:C_SG2 + 1],
                                 [(s_rb.sem, s_rb.n), *after], ROPEW)
        yield

    QA, KA, VA = carve(0, 8, S), carve(2048, S), carve(2304, 2, 128)
    KI, QI = carve(2560, S), carve(2816, 8, S)
    QB, KB, VBB = carve(4864, 8, S), carve(6912, 8, S), carve(8960, 2, GW)
    YA2 = carve(0, 8, 2, S, dt=BF16)
    YB2 = carve(2816, 8, 2, S, dt=BF16)
    YAF, YBF = QA, QI
    MN0, MN1 = carve(11008, 128), carve(11136, S)
    IW = carve(11392, 2, S)
    IT = carve(11904, 384)
    DM = carve(17408, 8, 256)
    W2 = 17408 + 2048

    def layer2(L):
        dm = {}
        WIN = t["w_in_2"][L]

        def start():
            r = rstd_of(state["sq"])
            if L == 0:
                q = DV.op(red(rs2[:, 0:2], ssf.rearrange("p (i j) -> p i j", i=2), ADD), state["sqf"])
                q = DV.op(tt(rs2[:, 0:2], rs2[:, 0:2], rst[:, 2:4], MUL), [q, r])
                q = DV.op(tt(rs2[:, 0:2], rs2[:, 0:2], rst[:, 2:4], MUL), [q])
                q = AC.op(act(rs2[:, 0:2], rs2[:, 0:2], ACT.Sqrt, bias=eps_c, scale=1.0 / D), [q])
                q = DV.op(recip(rs2[:, 2:4], rs2[:, 0:2]), [q])
                r1 = DV.op(cp(rs2[:, 0:2], rst[:, 2:4]), [q])
                r = DV.op(tt(rst[:, 2:4], rst[:, 2:4], rs2[:, 2:4], MUL), [q, r1])
                tk["dm"] = SP.dma(DM, t["dm"].rearrange("p (h s) -> p h s", h=8), s_dm, tk["bias"] + tk["rope2"])
                more_stages([carve(21504 + 512 * i, 512) for i in range(2)], tk["bias"] + tk["rope2"])
            g = DV.op(stt(gsc, modcm[:, L, 16:32], 1.0, cols("ng", 16 * L, 16), ADD, MUL),
                      [mod_done[(L, b)] for b in range(8)] + state["gsc_free"])
            norm_to_h(lambda k: gsc[:, k:k + 1], lambda k: modcm[:, L, k:k + 1], r, [g])
            state["gsc_free"] = [state["h"][-1]]
            gate_loaded[L] = SP.dma(GB, t["b_mod_2"][L, 4096:6144].partition_broadcast(128), s_gb[L],
                                    state["gb_free"] + [state["h"][-1]])
            ready[0] = [state["h"][-1]]
            if L == 0:
                short.append(scale_x(state["xlast"], r1))

        def scale_x(pe, r1):
            for i in range(2):
                for j in range(4):
                    xs = X[:, i, 512 * j:512 * j + 512]
                    state["x"][i][j] = DV.op(ts(xs, xs, rs2[:, i:i + 1], MUL), [pe, r1])
                    yield

        ready = [[]]

        def ki_evac(ps, tok):
            e = copy_out(KI, ps[0][:, 0:256], [tok, *ready[0]])
            tk["ki"] = e
            return [e]

        def wi_evac(ps, tok):
            e = [copy_out(wi[:, i, :], ps[i][:, 0:16], [tok]) for i in range(2)]
            tk["wi"] = e
            return e

        def qi_evac(blk):
            def evac(ps, tok):
                f = [copy_out(QI[:, 4 * blk + 2 * hf:4 * blk + 2 * hf + 2, :].rearrange("p a s -> p (a s)"),
                              ps[hf][:, :], [tok, *ready[0]]) for hf in range(2)]
                tk[("qi", blk)] = f
                return f
            return evac

        def indexer():
            a0 = carve(W2, 2, 128)
            a1 = carve(W2 + 256, 2, 256)
            g0 = g1 = None
            for ti in range(8):
                b0, w0 = take()
                b1, w1 = take()
                fs = []
                for hh, bk in ((0, b0), (1, b1)):
                    pp = slice(64 * hh, 64 * hh + 64)
                    fs.append(mm(bk[:, 0:128], QI[pp, ti, 0:128], KI[pp, 0:128]))
                    fs.append(mm(bk[:, 128:384], QI[pp, ti, 128:256], KI[pp, :]))
                p = PE.op(mms(*fs), [*tk[("qi", ti // 4)], tk["ki"], *w0, *w1])
                if ti == 0:
                    x0, x1, w = a0, a1, [*lane_free[0], *lane_free[1]]
                else:
                    si, s_, w = stage()
                    sj, t_, w3 = stage()
                    x0 = s_[:, 0:256].rearrange("p (h s) -> p h s", h=2)
                    x1 = t_.rearrange("p (h s) -> p h s", h=2)
                    w = [*w, *w3]
                ev = []
                for hh, bk in ((0, b0), (1, b1)):
                    DV.op(ts(x0[:, hh, :], bk[:, 0:128], 0.0, MAX, wi[:, 0, 2 * ti + hh:2 * ti + hh + 1], MUL),
                          [p, *tk["wi"], *w])
                    ev.append(DV.op(ts(x1[:, hh, :], bk[:, 128:384], 0.0, MAX,
                                       wi[:, 1, 2 * ti + hh:2 * ti + hh + 1], MUL), [p]))
                e0, e1 = ev
                if ti == 0:
                    g0 = g1 = e1
                else:
                    g0 = GP.op(tt(a0, a0, x0, ADD), [e1, g0])
                    g1 = GP.op(tt(a1, a1, x1, ADD), [e1, g1])
                    unstage(si, g0)
                    unstage(sj, g1)
                give(b0, e0)
                give(b1, e1)
                yield
            tk["qi_read"] = p
            r0, r1 = IW[:, 0, 0:128], IW[:, 1, :]
            q0 = DV.op(tt(r0, a0[:, 0, :], a0[:, 1, :], ADD), [g0, *ready[0]])
            q1 = DV.op(tt(r1, a1[:, 0, :], a1[:, 1, :], ADD), [g1])
            q0 = DV.op(tt(r0, r0, causal[:, 128:256], ADD), [q0])
            q1 = DV.op(tt(r1, r1, causal, ADD), [q1])
            mxa, mxb = mx8, sm[:, 344:352]
            for it in range(8):
                x0 = DV.op(lambda e: e.max(mxa, r0), [q0])
                x1 = DV.op(lambda e: e.max(mxb, r1), [q1])
                q0 = DV.op(lambda e: e.match_replace(r0, mxa, r0, -3e38), [x0])
                q1 = DV.op(lambda e: e.match_replace(r1, mxb, r1, -3e38), [x1])
                if it % 2:
                    yield
            q0 = DV.op(ts(MN0, r0, -2e38, ALU.is_gt, NEG, MUL), [q0])
            q1 = DV.op(ts(MN1, r1, -2e38, ALU.is_gt, NEG, MUL), [q1])
            q0 = DV.op(tt(MN0, MN0, causal[:, 128:256], ADD), [q0])
            q1 = DV.op(tt(MN1, MN1, causal, ADD), [q1])
            tk["sel"] = [q0, q1]
            lane_free[0] = lane_free[1] = [q0, q1]
            yield

        def k_evac(ps, tok):
            si, s_, w = stage()
            e = copy_out(s_[:, 0:256], ps[0][:, 0:256], [tok, *w])
            short.append(k_job(si, s_, e))
            return [e]

        def k_job(si, s_, e):
            s2, s2_, w2 = stage()
            g = GP.op(tt(s2_[:, 0:256], s_[:, 0:256], s_[:, 0:256], MUL), [e, *w2])
            yield 3
            b, w = take()
            p = PE.op(mm(b[:, 0:256], on128, s2_[:, 0:256]), [g, *w])
            yield 2
            a = AC.op(act(s2_[:, 0:256], b[:, 0:256], ACT.Sqrt, bias=eps_c), [p, t_eps])
            give(b, a)
            yield
            r = DV.op(recip(s2_[:, 0:256], s2_[:, 0:256]), [a])
            r = DV.op(stt(KA, s_[:, 0:256], col("kn", L), s2_[:, 0:256], MUL, MUL), [r, *ready[0]])
            unstage(si, r)
            unstage(s2, r)
            tk[("ka", 0)] = r

        def q_evac(blk):
            def evac(ps, tok):
                f = []
                for hf in range(2):
                    h = 4 * blk + 2 * hf
                    si, s_, w = stage()
                    e = AC.op(act(s_, ps[hf][:, :], ACT.Square), [tok, *w])
                    e2 = copy_out(QA[:, h:h + 2, :].rearrange("p a s -> p (a s)"), ps[hf][:, :], [tok, *ready[0]],
                                  scale=col("qn", L))
                    f.append(e2)
                    short.append(job(si, s_, e, e2, h))
                return f

            def job(si, s_, e, e2, h):
                yield
                b, w = take()
                p = PE.op(mms(*[mm(b[:, u:u + 1], s_[:, 128 * u:128 * u + 128], on128[:, 0:1]) for u in range(4)]),
                          [e, *w])
                yield 2
                a = AC.op(act(s_[:, 0:4], b[:, 0:4], ACT.Sqrt, bias=eps128_c, scale=128.0), [p, t_eps])
                give(b, a)
                yield
                r = DV.op(recip(qr[:, h:h + 2, :].rearrange("p h n -> p (h n)"), s_[:, 0:4]), [a])
                unstage(si, r)
                tk[("qa", h // 2)] = [r, e2]
            return evac

        def va_evac(ps, tok):
            e = [copy_out(VA[:, i, :], ps[i][:, 0:128], [tok, *ready[0]]) for i in range(2)]
            tk["va"] = e
            return e

        def sparse(hp):
            h0 = 2 * hp
            base = W2
            L0, L1 = carve(base, 2, 128), carve(base + 256, 2, 256)
            mcol, rcol = lane_sm[0][:, 0:4], lane_sm[0][:, 4:8]
            lw = lane_free[0]
            g0 = GP.op(tt(L0, B0[:, h0:h0 + 2, :], mid(MN0, 2), ADD), [*tk["sel"], *tk["bias"], *lw])
            g1 = GP.op(tt(L1, B1[:, h0:h0 + 2, :], mid(MN1, 2), ADD), [*tk["sel"], *tk["bias"], *lw])
            b0, w0 = take()
            b1, w1 = take()
            fs = []
            for h in range(2):
                fs.append(mm(b0[:, 128 * h:128 * h + 128], QA[:, h0 + h, 0:128], KA[:, 0:128]))
                fs.append(mm(b1[:, 256 * h:256 * h + 256], QA[:, h0 + h, 128:256], KA))
            p = PE.op(mms(*fs), [*tk[("qa", hp)], tk[("ka", 0)], *w0, *w1])
            for h in range(2):
                e0 = DV.op(stt(L0[:, h, :], b0[:, 128 * h:128 * h + 128], qr[:, h0 + h, 0:1], L0[:, h, :], MUL, ADD),
                           [p, g0])
                e1 = DV.op(stt(L1[:, h, :], b1[:, 256 * h:256 * h + 256], qr[:, h0 + h, 1:2], L1[:, h, :], MUL, ADD),
                           [p, g1])
            give(b0, e0)
            give(b1, e1)
            yield
            n0, n1 = yield from softmax_rows(L0, L1, e0, e1, 2, mcol, rcol, 1.0)
            yield 4
            PT0, PT1, pt, cc = attend_pv(L0, L1, n0, n1, None, None, 0, base)
            yield 2
            b, w = take()
            fs = []
            for h in range(2):
                fs.append(mm(b[:, 256 * h:256 * h + 256], VA[:, 0, :], PT0[:, h, :], start=(h == 0), stop=False))
                fs.append(mm(b[:, 256 * h + 128:256 * h + 256], VA[:, 1, :], PT1[:, h, :], start=False, stop=True))
            p = PE.op(mms(*fs), [*cc, *w, *tk["va"]])
            e = copy_out(YAF[:, h0:h0 + 2, :].rearrange("p a s -> p (a s)"), b[:, :], [p])
            give(b, e)
            lane_free[0] = [p]
            tk[("yaf", hp)] = e
            yield

        def rot(dst, name, blk):
            def evac(ps, tok):
                f = []
                for hf in range(2):
                    si, s_, w = stage()
                    e = copy_out(s_, ps[hf][:, :], [tok, *w])
                    f.append(e)
                    short.append(job(si, s_, e, 2 * blk + hf))
                return f

            def job(si, s_, e, hp):
                d = dst[:, 2 * hp:2 * hp + 2, :]
                sv = s_.rearrange("p (h s) -> p h s", h=2)
                s2, s2_, w2 = stage()
                s2v = s2_.rearrange("p (h s) -> p h s", h=2)
                m = DV.op(tt(d, sv, mid(cs[:, 0, :], 2), MUL), [e, *ready[0], *tk["rope2"]])
                x_ = DV.op(tt(s2v[0:64], sv[64:128], mid(cs[64:128, 1, :], 2), MUL), [e, *w2])
                x_ = DV.op(tt(s2v[64:128], sv[0:64], mid(cs[0:64, 1, :], 2), MUL), [e, *w2])
                g = GP.op(tt(d, d, s2v, ADD), [m, x_])
                unstage(si, x_)
                unstage(s2, g)
                tk[(name, hp)] = g
                yield
            return evac

        def vb_evac(blk):
            def evac(ps, tok):
                f = [copy_out(VBB[:, i, 512 * blk:512 * blk + 512], ps[i][:, :], [tok, *ready[0]]) for i in range(2)]
                tk[("vb", blk)] = f
                return f
            return evac

        def retain(hp):
            h0 = 2 * hp
            si, s_, w = stage()
            sj, t_, w3 = stage()
            S0, S1 = s_.rearrange("p (h s) -> p h s", h=2), t_[:, 0:256].rearrange("p (h s) -> p h s", h=2)
            b0, w0 = take()
            b1, w1 = take()
            fs = []
            for h in range(2):
                fs.append(mm(b0[:, 256 * h:256 * h + 256], KB[:, h0 + h, 0:128], QB[:, h0 + h, :]))
                fs.append(mm(b1[:, 128 * h:128 * h + 128], KB[:, h0 + h, 128:256], QB[:, h0 + h, 128:256]))
            p = PE.op(mms(*fs), [tk[("qb", hp)], tk[("kb", hp)], *w0, *w1])
            e0 = DV.op(tt(S0, b0[:, :].rearrange("p (h s) -> p h s", h=2), DM[:, h0:h0 + 2, 0:256], MUL),
                       [p, tk["dm"], *w])
            e1 = DV.op(tt(S1, b1[:, 0:256].rearrange("p (h s) -> p h s", h=2), DM[:, h0:h0 + 2, 0:128], MUL),
                       [p, tk["dm"], *w3])
            give(b0, e0)
            give(b1, e1)
            yield 2
            b, w = take()
            fs = []
            for h in range(2):
                sl = slice(128 * (h0 + h), 128 * (h0 + h) + 128)
                o0, o1 = (b[:, 128 * (2 * h + i):128 * (2 * h + i) + 128] for i in range(2))
                fs.append(mm(o0, S0[:, h, 0:128], VBB[:, 0, sl]))
                fs.append(mm(o1, S0[:, h, 128:256], VBB[:, 0, sl], start=False, stop=False))
                fs.append(mm(o1, S1[:, h, :], VBB[:, 1, sl], start=False, stop=True))
            p = PE.op(mms(*fs), [e0, e1, *w, *tk[("vb", hp // 2)]])
            c_ = copy_out(s_, b[:, :], [p])
            give(b, c_)
            yield 2
            mean, var, rs = (ret_sm[hp][:, 4 * i:4 * i + 4] for i in range(3))
            sv, tv = (v.rearrange("p (u d) -> p u d", u=4) for v in (s_, t_))
            r = DV.op(red(mean, sv, ADD), [c_])
            r = DV.op(ts(mean, mean, -1.0 / 128, MUL), [r])
            x_ = DV.op(tt(sv, sv, rep(mean, 128), ADD), [r])
            g = GP.op(tt(t_, s_, s_, MUL), [x_])
            yield 2
            r = DV.op(red(var, tv, ADD), [g])
            a = AC.op(act(rs, var, ACT.Sqrt, bias=eps_c, scale=1.0 / 128), [r, t_eps])
            yield
            r = DV.op(recip(var, rs), [a])
            y = DV.op(tt(sv, sv, rep(var, 128), MUL), [r, g])
            yield 3
            b, w = take()
            p = PE.op(mms(*[tp(b[:, 128 * u:128 * u + 128], sv[:, u, :], ident) for u in range(4)]), [y, *w])
            yield
            for h in range(2):
                e = copy_out(YBF[:, h0 + h, :], b[:, 256 * h:256 * h + 256], [p, tk["qi_read"]],
                             scale=col("rn", 8 * L + h0 + h))
            give(b, e)
            unstage(si, p)
            unstage(sj, y)
            tk[("ybf", hp)] = e
            yield

        def g_evac(src, dst, name, sname, blk):
            def evac(ps, tok):
                f = []
                for hf in range(2):
                    hp = 2 * blk + hf
                    si, s_, w = stage()
                    sj, t_, w3 = stage()
                    a = AC.op(act(t_, ps[hf][:, :], ACT.Tanh, scale=0.5), [tok, *w3])
                    r = DV.op(stt(t_, t_, 1.0, ps[hf][:, :], ADD, MUL), [a])
                    f.append(r)
                    short.append(job(hp, si, s_, sj, t_, r, w))
                return f

            def job(hp, si, s_, sj, t_, r, w):
                y = GP.op(tt(s_, src[:, 2 * hp:2 * hp + 2, :].rearrange("p a s -> p (a s)"), t_, MUL),
                          [r, tk[(sname, hp)], *w])
                unstage(sj, y)
                yield
                o = yield from split_out(dst, 2 * hp, s_, [y])
                unstage(si, o)
                tk[(name, hp)] = o
            return evac

        add(WIN, 2304, 512, KT, "CM", h_ops, qi_evac(0), start)
        add(WIN, 3328, 128, KT, "CM", h_ops, ki_evac, dup=True)
        add(WIN, 3392, 16, KT, "TM", h_ops, wi_evac)
        add(WIN, 2816, 512, KT, "CM", h_ops, qi_evac(1))
        add(WIN, 1024, 128, KT, "CM", h_ops, k_evac,
            launch(indexer()))
        add(WIN, 0, 512, KT, "CM", h_ops, q_evac(0))
        add(WIN, 512, 512, KT, "CM", h_ops, q_evac(1))
        add(WIN, 1152, 128, KT, "TM", h_ops, va_evac)

        def chain(f):
            for hp in range(4):
                yield from f(hp)

        for blk in range(2):
            add(WIN, 3408 + 512 * blk, 512, KT, "CM", h_ops, rot(QB, "qb", blk),
                launch(retain(0), retain(1)) if blk else launch(chain(sparse)))
            add(WIN, 4432 + 512 * blk, 512, KT, "CM", h_ops, rot(KB, "kb", blk))
            add(WIN, 5456 + 512 * blk, 512, KT, "TM", h_ops, vb_evac(blk))
        for blk in range(2):
            b = add(WIN, 1280 + 512 * blk, 512, KT, "CM", h_ops, g_evac(YAF, YA2, "y2a", "yaf", blk),
                    None if blk else launch(retain(2), retain(3)))
            b_g.setdefault(L, b)
        for blk in range(2):
            add(WIN, 6480 + 512 * blk, 512, KT, "CM", h_ops, g_evac(YBF, YB2, "y2b", "ybf", blk))

        def begin():
            state["sq"] = []
            state["gb_free"] = []

        o_ops = ((lambda k: YA2[:, k, 0, :] if k < 8 else YB2[:, k - 8, 0, :]),
                 (lambda k: YA2[:, k, 1, :] if k < 8 else YB2[:, k - 8, 1, :]),
                 (lambda k: [tk[("y2a", k // 2)]] if k < 8 else [tk[("y2b", k // 2 - 4)]]))

        def o_evac(blk):
            def evac(ps, tok):
                f = []
                for i in range(2):
                    xs = X[:, i, 512 * blk:512 * blk + 512]
                    si, s_, w = stage()
                    e = DV.op(stt(s_, ps[i][:, :], 0.5, GB[:, 512 * blk:512 * blk + 512], MUL, MUL),
                              [tok, mod_done[(L, 8 + blk)], *w])
                    f.append(e)
                    x_ = DV.op(tt(xs, xs, s_, ADD), [e, state["x"][i][blk]])
                    unstage(si, x_)
                    state["x"][i][blk] = x_
                    state["gb_free"] = state["gb_free"] + [e]
                    if L == 0:
                        state["sq"].append(sumsq(i, blk, [x_]))
                    else:
                        SP.dma(out[0, 128 * i:128 * i + 128, 512 * blk:512 * blk + 512], xs, s_out, [x_])
                if L == 0:
                    xpose_later(blk)
                return f
            return evac

        for blk in range(4):
            add(t["w_out_2"][L], 512 * blk, 512, KT, "TM", o_ops, o_evac(blk),
                begin if blk == 0 else sqrt_ahead if blk == 3 and L == 0 else None)

    state["gsc_free"] = []
    state["gb_free"] = []
    marks, b_g = {}, {}
    for L in range(2):
        marks[L] = len(chunks)
        layer2(L)

    def first_chunk(b):
        return next(i for i, c in enumerate(chunks) if c[1] is b)

    def spread(items, *ranges):
        room = [i for lo, hi in ranges for i in range(lo, hi)]
        return [(room[len(room) * i // len(items)], it) for i, it in enumerate(items)]

    z1, gb0, up0, up5 = (first_chunk(b) for b in (b_z1, b_gb[0], b_up[0], b_up[10]))
    puts = spread([c for L in range(2) for b in range(8) for c in add_mod(L, b)],
                  (12, 24), (z1, z1 + 8), (gb0 + 4, up0 - 2), (up5, marks[0] - 8))
    for L in range(2):
        g0 = first_chunk(b_g[L])
        puts += spread([c for b in range(8, 12) for c in add_mod(L, b)], (marks[L] + 4, marks[L] + 9), (g0 - 20, g0 + 14))
    by = {}
    for at, c in puts:
        by.setdefault(at, []).append(c)
    merged = []
    for i, c in enumerate(chunks):
        merged += by.get(i, [])
        merged.append(c)
    chunks[:] = merged

    for j in range(R1):
        send(j)
    at = 0
    for b in blocks:
        at = run_block(b, at)
    finish_all()
    SP.wait([(s_out.sem, s_out.n)])

    block = ctx.enter_context(nc.Block())

    @block.sync
    def _(e):
        SP.emit(e)

    @block.tensor
    def _(e):
        PE.emit(e)

    @block.scalar
    def _(e):
        AC.emit(e)

    @block.vector
    def _(e):
        DV.emit(e)

    @block.gpsimd
    def _(e):
        GP.emit(e)


_INS = ["x", "positions", "ln1", "w_in", "gdn_conv", "gdn_a_log", "gdn_dt_bias", "gdn_norm", "w_branch_a",
        "w_branch_b", "w_out", "ln2", "w_up", "ffn_conv", "ffn_conv_bias", "w_down", "final_norm", "c_2",
        "positions_2", "rel_bias_2", "norm_gain_2", "w_mod_2", "b_mod_2", "w_in_2", "q_norm_gain_2",
        "k_norm_gain_2", "ret_norm_gain_2", "w_out_2"]


def kernel(**inputs):
    import numpy as _np
    import concourse.bacc as _bacc
    from concourse import mybir as _mybir
    from concourse.bass_utils import run_bass_kernel_spmd as _run

    nc = _bacc.Bacc("TRN2", target_bir_lowering=False, num_devices=1)
    arrays, aps = {}, {}
    for name in _INS:
        a = _np.ascontiguousarray(inputs[name])
        arrays[f"in_{name}"] = a
        aps[name] = nc.dram_tensor(f"in_{name}", a.shape, _mybir.dt.from_np(a.dtype), kind="ExternalInput").ap()
    for name, a in (("cst", constants()), ("dm", decay())):
        arrays[f"in_{name}"] = a
        aps[name] = nc.dram_tensor(f"in_{name}", a.shape, _mybir.dt.from_np(a.dtype), kind="ExternalInput").ap()
    out = nc.dram_tensor("out_0", (1, 256, 2048), _mybir.dt.float32, kind="ExternalOutput").ap()
    build(nc, aps, out)
    r = _run(nc, [arrays], core_ids=[0])
    return r.results[0]["out_0"]
```
